# Optimizing a Trainium2 kernel written in Bass

```python
import jax, jax.numpy as jnp
from jax import lax
import numpy as np

D_MODEL = 1024
BATCH = 1
SEQ = 1024
DEPTH = 2
DEC_BATCH = 1
DEC_SEQ = 32
PAST_LEN = 256

CHUNK = 64
Q_BLOCK = 128
N_A = (DEPTH + 1) // 2
N_B = DEPTH - N_A
PLE_DIM = 256
EPS = 1e-6
NEG = -1e30
H_A = 16
Q_RANK = 512
KV_RANK = 256
QK_NOPE = 64
QK_ROPE = 32
V_DIM = 64
ROPE_THETA = 10000.0
MLA_SCALE = (QK_NOPE + QK_ROPE) ** -0.5
H_B = 16
KV_H_B = 4
HD_B = 64
G_B = H_B // KV_H_B
FOX_SCALE = HD_B ** -0.5
FORGET_BIAS = 3.0
D_FF = ((8 * D_MODEL + 3 * 256 - 1) // (3 * 256)) * 256

kernel_name = "yoco_mla_fox_streaming_step"

def rms_norm(x, g):
    xf = x.astype(jnp.float32)
    y = xf * lax.rsqrt(jnp.mean(xf * xf, axis=-1, keepdims=True) + EPS)
    return (y * g.astype(jnp.float32)).astype(x.dtype)

def rope(x, pos):
    half = x.shape[-1] // 2
    inv = jnp.power(ROPE_THETA, -jnp.arange(half, dtype=jnp.float32) / half)
    ang = pos.astype(jnp.float32)[:, None] * inv[None, :]
    cos = jnp.cos(ang)[None, :, None, :]
    sin = jnp.sin(ang)[None, :, None, :]
    x1 = x[..., :half].astype(jnp.float32)
    x2 = x[..., half:].astype(jnp.float32)
    return jnp.concatenate([x1 * cos - x2 * sin, x1 * sin + x2 * cos], axis=-1).astype(x.dtype)

def mla_project(h, pos, w_dq, g_q, w_uq, w_dkv, g_kv):
    b, t, _ = h.shape
    cq = rms_norm(h @ w_dq, g_q)
    q = (cq @ w_uq).reshape(b, t, H_A, QK_NOPE + QK_ROPE)
    q_nope = q[..., :QK_NOPE]
    q_rope = rope(q[..., QK_NOPE:], pos)
    kv = h @ w_dkv
    ckv = rms_norm(kv[..., :KV_RANK], g_kv)
    kr = rope(kv[..., KV_RANK:][:, :, None, :], pos)[:, :, 0, :]
    return q_nope, q_rope, ckv, kr

def mla_prompt(q_nope, q_rope, ckv, kr, w_uk, w_uv):
    b, s = ckv.shape[:2]
    k_nope = jnp.einsum('bsr,rhd->bshd', ckv, w_uk)
    v = jnp.einsum('bsr,rhd->bshd', ckv, w_uv)
    kchunk = jnp.arange(s) // CHUNK

    def block(qb):
        start = qb * Q_BLOCK
        qn = lax.dynamic_slice_in_dim(q_nope, start, Q_BLOCK, axis=1)
        qr = lax.dynamic_slice_in_dim(q_rope, start, Q_BLOCK, axis=1)
        sc = (jnp.einsum('bqhd,bshd->bhqs', qn, k_nope)
              + jnp.einsum('bqhe,bse->bhqs', qr, kr)).astype(jnp.float32) * MLA_SCALE
        qchunk = (start + jnp.arange(Q_BLOCK)) // CHUNK
        sc = jnp.where(kchunk[None, :] <= qchunk[:, None], sc, NEG)
        pr = jax.nn.softmax(sc, axis=-1).astype(v.dtype)
        return jnp.einsum('bhqs,bshd->bqhd', pr, v)

    o = lax.map(block, jnp.arange(s // Q_BLOCK))
    return o.transpose(1, 0, 2, 3, 4).reshape(b, s, H_A * V_DIM)

def mla_sample(q_nope, q_rope, ckv_all, kr_all, w_uk, w_uv):
    b, t = q_nope.shape[:2]
    q_lat = jnp.einsum('bthd,rhd->bthr', q_nope, w_uk)
    sc = (jnp.einsum('bthr,bsr->bhts', q_lat, ckv_all)
          + jnp.einsum('bthe,bse->bhts', q_rope, kr_all)).astype(jnp.float32) * MLA_SCALE
    pr = jax.nn.softmax(sc, axis=-1).astype(ckv_all.dtype)
    o_lat = jnp.einsum('bhts,bsr->bthr', pr, ckv_all)
    o = jnp.einsum('bthr,rhd->bthd', o_lat, w_uv)
    return o.reshape(b, t, H_A * V_DIM)

def shared_kv(r, g_shared, w_kb, w_vb, w_f, b_f):
    b, t, _ = r.shape
    z = rms_norm(r, g_shared)
    k = (z @ w_kb).reshape(b, t, KV_H_B, HD_B)
    v = (z @ w_vb).reshape(b, t, KV_H_B, HD_B)
    logf = jax.nn.log_sigmoid((z @ w_f + b_f).astype(jnp.float32))
    return k, v, logf

def fox_prompt(q, k, v, logf):
    b, s = q.shape[:2]
    qg = q.reshape(b, s, KV_H_B, G_B, HD_B)
    cum = jnp.cumsum(logf.astype(jnp.float32), axis=1)
    cum_k = cum.transpose(0, 2, 1).reshape(b, KV_H_B, G_B, 1, s)
    kpos = jnp.arange(s)

    def block(qb):
        start = qb * Q_BLOCK
        qblk = lax.dynamic_slice_in_dim(qg, start, Q_BLOCK, axis=1)
        cq = lax.dynamic_slice_in_dim(cum, start, Q_BLOCK, axis=1)
        cq = cq.transpose(0, 2, 1).reshape(b, KV_H_B, G_B, Q_BLOCK, 1)
        sc = jnp.einsum('bqkgd,bskd->bkgqs', qblk, k).astype(jnp.float32) * FOX_SCALE + (cq - cum_k)
        qpos = start + jnp.arange(Q_BLOCK)
        sc = jnp.where(kpos[None, :] <= qpos[:, None], sc, NEG)
        pr = jax.nn.softmax(sc, axis=-1).astype(v.dtype)
        return jnp.einsum('bkgqs,bskd->bqkgd', pr, v)

    o = lax.map(block, jnp.arange(s // Q_BLOCK))
    return o.transpose(1, 0, 2, 3, 4, 5).reshape(b, s, H_B * HD_B)

def fox_sample(q, k_all, v_all, logf_all):
    b, t = q.shape[:2]
    total = k_all.shape[1]
    past = total - t
    qg = q.reshape(b, t, KV_H_B, G_B, HD_B)
    lf = logf_all.astype(jnp.float32)
    suf = lax.cumsum(lf, axis=1, reverse=True) - lf
    suf_k = suf.transpose(0, 2, 1).reshape(b, KV_H_B, G_B, 1, total)
    suf_q = suf[:, past:].transpose(0, 2, 1).reshape(b, KV_H_B, G_B, t, 1)
    sc = jnp.einsum('btkgd,bskd->bkgts', qg, k_all).astype(jnp.float32) * FOX_SCALE + (suf_k - suf_q)
    qpos = past + jnp.arange(t)
    sc = jnp.where(jnp.arange(total)[None, :] <= qpos[:, None], sc, NEG)
    pr = jax.nn.softmax(sc, axis=-1).astype(v_all.dtype)
    o = jnp.einsum('bkgts,bskd->btkgd', pr, v_all)
    return o.reshape(b, t, H_B * HD_B)

def setup_inputs(seed: int = 0) -> dict:
    key = jax.random.key(seed)
    ks = iter(jax.random.split(key, 48))

    def nrm(shape, scale=1.0):
        return scale * jax.random.normal(next(ks), shape, jnp.float32)

    def gain(shape):
        return 1.0 + 0.05 * nrm(shape)

    d = D_MODEL
    return {
        "x_prompt": nrm((BATCH, SEQ, d)),
        "x_sample": nrm((DEC_BATCH, DEC_SEQ, d)),
        "p_prompt": nrm((DEPTH, BATCH, SEQ, PLE_DIM)),
        "p_sample": nrm((DEPTH, DEC_BATCH, DEC_SEQ, PLE_DIM)),
        "cache_ckv": nrm((N_A, DEC_BATCH, PAST_LEN, KV_RANK)),
        "cache_kr": nrm((N_A, DEC_BATCH, PAST_LEN, QK_ROPE)),
        "cache_k": nrm((DEC_BATCH, PAST_LEN, KV_H_B, HD_B)),
        "cache_v": nrm((DEC_BATCH, PAST_LEN, KV_H_B, HD_B)),
        "cache_logf": jax.nn.log_sigmoid(FORGET_BIAS + nrm((DEC_BATCH, PAST_LEN, H_B))),
        "w_dq": nrm((N_A, d, Q_RANK), d ** -0.5),
        "g_q": gain((N_A, Q_RANK)),
        "w_uq": nrm((N_A, Q_RANK, H_A * (QK_NOPE + QK_ROPE)), Q_RANK ** -0.5),
        "w_dkv": nrm((N_A, d, KV_RANK + QK_ROPE), d ** -0.5),
        "g_kv": gain((N_A, KV_RANK)),
        "w_uk": nrm((N_A, KV_RANK, H_A, QK_NOPE), KV_RANK ** -0.5),
        "w_uv": nrm((N_A, KV_RANK, H_A, V_DIM), KV_RANK ** -0.5),
        "w_oa": nrm((N_A, H_A * V_DIM, d), (H_A * V_DIM) ** -0.5),
        "g_shared": gain((d,)),
        "w_kb": nrm((d, KV_H_B * HD_B), d ** -0.5),
        "w_vb": nrm((d, KV_H_B * HD_B), d ** -0.5),
        "w_f": nrm((d, H_B), d ** -0.5),
        "b_f": FORGET_BIAS + 0.5 * nrm((H_B,)),
        "w_qb": nrm((N_B, d, H_B * HD_B), d ** -0.5),
        "w_ob": nrm((N_B, H_B * HD_B, d), (H_B * HD_B) ** -0.5),
        "g_mix_pre": gain((DEPTH, d)),
        "g_mix_post": gain((DEPTH, d)),
        "g_ffn_pre": gain((DEPTH, d)),
        "g_ffn_post": gain((DEPTH, d)),
        "w_gate": nrm((DEPTH, d, D_FF), d ** -0.5),
        "w_up": nrm((DEPTH, d, D_FF), d ** -0.5),
        "w_down": nrm((DEPTH, D_FF, d), D_FF ** -0.5),
        "w_ple": nrm((DEPTH, PLE_DIM, d), PLE_DIM ** -0.5),
        "g_ple_gate": gain((DEPTH, d)),
        "w_ple_gate": nrm((DEPTH, d, d), d ** -0.5),
        "g_ple_post": gain((DEPTH, d)),
    }

def reference(x_prompt, x_sample, p_prompt, p_sample, cache_ckv, cache_kr, cache_k, cache_v, cache_logf,
              w_dq, g_q, w_uq, w_dkv, g_kv, w_uk, w_uv, w_oa,
              g_shared, w_kb, w_vb, w_f, b_f, w_qb, w_ob,
              g_mix_pre, g_mix_post, g_ffn_pre, g_ffn_post, w_gate, w_up, w_down,
              w_ple, g_ple_gate, w_ple_gate, g_ple_post):

    def run(x, p, pos, cached):
        b, t, _ = x.shape
        r = x
        ckv_rows, kr_rows = [], []
        k_new = v_new = lf_new = None
        for i in range(DEPTH):
            if i < N_A:
                h = rms_norm(r, g_mix_pre[i])
                q_nope, q_rope, ckv, kr = mla_project(h, pos, w_dq[i], g_q[i], w_uq[i], w_dkv[i], g_kv[i])
                ckv_rows.append(ckv)
                kr_rows.append(kr)
                if cached:
                    o = mla_sample(q_nope, q_rope,
                                   jnp.concatenate([cache_ckv[i].astype(ckv.dtype), ckv], axis=1),
                                   jnp.concatenate([cache_kr[i].astype(kr.dtype), kr], axis=1),
                                   w_uk[i], w_uv[i])
                else:
                    o = mla_prompt(q_nope, q_rope, ckv, kr, w_uk[i], w_uv[i])
                y = o @ w_oa[i]
            else:
                j = i - N_A
                if k_new is None:
                    k_new, v_new, lf_new = shared_kv(r, g_shared, w_kb, w_vb, w_f, b_f)
                h = rms_norm(r, g_mix_pre[i])
                q = (h @ w_qb[j]).reshape(b, t, H_B, HD_B)
                if cached:
                    o = fox_sample(q,
                                   jnp.concatenate([cache_k.astype(k_new.dtype), k_new], axis=1),
                                   jnp.concatenate([cache_v.astype(v_new.dtype), v_new], axis=1),
                                   jnp.concatenate([cache_logf.astype(jnp.float32), lf_new], axis=1))
                else:
                    o = fox_prompt(q, k_new, v_new, lf_new)
                y = o @ w_ob[j]
            r = r + rms_norm(y, g_mix_post[i])
            h = rms_norm(r, g_ffn_pre[i])
            f = (jax.nn.silu(h @ w_gate[i]) * (h @ w_up[i])) @ w_down[i]
            r = r + rms_norm(f, g_ffn_post[i])
            e = p[i] @ w_ple[i]
            gate = jax.nn.sigmoid(rms_norm(r, g_ple_gate[i]) @ w_ple_gate[i])
            r = r + rms_norm(e * gate, g_ple_post[i])
        return r, jnp.stack(ckv_rows), jnp.stack(kr_rows), k_new, v_new, lf_new

    pos_p = jnp.arange(x_prompt.shape[1])
    pos_s = PAST_LEN + jnp.arange(x_sample.shape[1])
    y_prompt, ckv_p, kr_p, k_p, v_p, logf_p = run(x_prompt, p_prompt, pos_p, False)
    y_sample, ckv_s, kr_s, k_s, v_s, logf_s = run(x_sample, p_sample, pos_s, True)
    return (y_prompt, y_sample, ckv_p, kr_p, k_p, v_p, logf_p, ckv_s, kr_s, k_s, v_s, logf_s)


_drawn_inputs = setup_inputs


def setup_inputs(seed=0):
    import zlib

    import numpy as np

    out = dict(_drawn_inputs(seed))
    spreads = {}
    factors = {'g_ple_gate': 4.271}
    for name, (base, spread) in spreads.items():
        noise = np.random.default_rng([zlib.crc32(name.encode()), seed]).standard_normal(out[name].shape)
        drawn = base * np.exp(spread * noise) if base else spread * noise
        out[name] = __import__('jax').numpy.asarray(drawn.astype(out[name].dtype))
    for name, factor in factors.items():
        out[name] = (out[name] * factor).astype(out[name].dtype)
    return out
```

```python
from contextlib import ExitStack

import concourse.bass as bass
from concourse import mybir

F32 = mybir.dt.float32
F32R = mybir.dt.float32r
ACT = mybir.ActivationFunctionType
ALU = mybir.AluOpType
AX = mybir.AxisListType

P = 128
D = 1024
KD = D // P
SEQ, DEC, PAST = 1024, 32, 256
T = SEQ + DEC
TK = T + PAST
NB = 3
TB = T // NB
KB = 4
TKB = TK // KB
KT = (TK + P - 1) // P
H = 16
Q_RANK, KV_RANK, NOPE, ROPE, VD = 512, 256, 64, 32, 64
KVH, HD = 4, 64
PLE = 256
F = 2816
NF = F // P
EPS = 1e-6
NEG = -1e30
FOX_SCALE = HD ** -0.5
UW = 1024

LIN = [("dq", 4, "mix_pre0"), ("dkv", 2, "mix_pre0"), ("kr", 1, "mix_pre0"), ("uk", 2, None),
       ("uv", 2, None), ("uq", 8, "q"), ("oa", 8, None), ("ffn0", 3 * NF, "ffn_pre0"),
       ("pe0", 2, None), ("pg0", 8, "ple_gate0"),
       ("kb", 2, "shared"), ("wf", 1, "shared"), ("vb", 2, "shared_v"), ("qb", 8, "mix_pre1"),
       ("ob", 8, None), ("ffn1", 3 * NF, "ffn_pre1"), ("pe1", 2, None), ("pg1", 8, "ple_gate1")]
GAINS = ["mix_pre0", "q", "mix_post0", "ffn_pre0", "ffn_post0", "ple_gate0", "ple_post0", "shared",
         "shared_v", "shared_v2", "mix_pre1", "mix_post1", "ffn_pre1", "ffn_post1", "ple_gate1",
         "ple_post1", "kv", "bf"]
GAIN_AT = {name: 8 * i for i, name in enumerate(GAINS)}


def unit_places():
    first, used, gained = {}, {}, {}
    at, use, gain = 0, [0, 0, 0], [0, 0, 0]
    for name, n, g in LIN:
        first[name], used[name], gained[name] = at, list(use), list(gain)
        at += n
        for u in range(n):
            s = u % 3 if name.startswith("ffn") else u % 2
            use[s] += 1
            if g is not None and s < 2:
                gain[s] += 1
    return first, used, gained, at


UNIT0, USED, GAINED, UNITS = unit_places()

GROUPS = [("dq", 12), ("dkv", 6), ("kr", 3), ("uk", 8 * KB), ("uv", 2 * KT), ("uq", 48), ("oa", 24),
          ("pe0", 24), ("pg0", 24), ("kb", 6), ("wf", 3), ("vb", 9), ("qb", 24), ("ob", 24),
          ("pe1", 24), ("pg1", 24)]
GROUP0 = {}
_at = 0
for _n, _c in GROUPS:
    GROUP0[_n] = _at
    _at += _c
LBANKS = 6

CHAIN = [("post", 0), ("post", 1), ("pre", 0), ("post", 2), ("pre", 1), ("pre", 2)]
NORMS = ([("s0", "pre", b) for b in range(NB)] + [("s1", "q", b) for b in range(NB)]
         + [("s1", "kv", b) for b in range(NB)]
         + [(s, k, b) for s in ("s2", "s3", "s4", "s5", "s6") for k, b in CHAIN]
         + [("s7", "post", b) for b in range(NB)])
NORM_AT = {n: i for i, n in enumerate(NORMS)}
POST_GAIN = {"s2": "mix_post0", "s3": "ffn_post0", "s4": "ple_post0", "s5": "mix_post1",
             "s6": "ffn_post1", "s7": "ple_post1"}

ORDER = [7, 0, 6, 1, 5, 2, 8, 3, 4]
STEPS = len(ORDER)
PAIR = 2 * STEPS
T_LAG, PV_LAG = 2, 3
D_AT = [16 + (9 * d) // 2 for d in range(24)]


PER_UNIT = {"dq": 3, "dkv": 3, "kr": 3, "uk": 4 * KB, "uv": KT, "uq": 6, "oa": 3, "pe0": 12, "pg0": 3,
            "kb": 3, "wf": 3, "vb": 9, "qb": 3, "ob": 3, "pe1": 12, "pg1": 3}


def group_after(name, slot, j):
    if name == "vb":
        return GROUP0[name] + 9
    return j * (2 * PER_UNIT[name]) + (GROUP0[name] + PER_UNIT[name] * (slot + 1))


HI_COUNT = [sum(n[1] != "post" for n in NORMS[:k + 1]) for k in range(len(NORMS))]


def build_program(nc, io):
    with ExitStack() as ctx:
        base = (nc.sbuf_base + 31) // 32 * 32
        end = nc.sbuf_usable_end

        def at(name, shape, dt, offset):
            n = 4
            for x in shape[1:]:
                n *= x
            n = (n + 31) // 32 * 32
            assert base + offset + n <= end, (name, base + offset + n - end)
            return nc.alloc_sbuf_tensor_at(name, shape, dt, offset=base + offset), offset + n

        res, o = at("residual", [P, KD, T], F32, 0)
        n_off = o
        nh, o = at("act_hi", [P, KD, T], F32R, o)
        nl, o = at("act_lo", [P, KD, T], F32R, o)
        cvh, _ = at("latent_hi", [P, 2, TK], F32R, n_off + 4 * T * 4)
        cvl, _ = at("latent_lo", [P, 2, TK], F32R, n_off + KD * T * 4 + 4 * T * 4)
        wraw, o = at("weight_raw", [P, 3, UW], F32, o)
        attn_off = o
        wh, o = at("weight_hi", [P, 3, UW], F32R, o)
        wl, o = at("weight_lo", [P, 3, UW], F32R, o)
        y, o = at("sublayer_out", [P, KD, T], F32, o)
        scr = o
        NGC = 8 * len(GAINS)
        const_bytes = 4 * (NGC + P + P + P + 2 * P + 8)
        o = (end - base - const_bytes) // 32 * 32
        top = o
        gains, o = at("gains", [P, NGC], F32, o)
        ones, o = at("ones", [P, P], F32, o)
        ident, o = at("ident", [P, P], F32, o)
        ident_r, o = at("ident_r", [P, P], F32R, o)
        mask_r, o = at("mask_r", [P, 2, P], F32R, o)
        epsc, o = at("eps_col", [P, 8], F32, o)
        sq, o = at("squares", [P, 2, KD, TB], F32, scr)
        rt, o = at("root", [P, 2, TB], F32, o)
        rs, o = at("rstd", [P, 2, TB], F32, o)
        stg, o = at("stage", [P, 2, TK], F32, scr)
        cs, o = at("rope_table", [P, T], F32, o)
        assert o <= top
        cc, o = at("cached_latent", [P, 2, PAST], F32, scr + 4 * (2 * KD * TB + 4 * TB))
        krf, o = at("rope_key", [ROPE, T], F32, o)
        assert o <= top
        krt, _ = at("rope_table_k", [2 * ROPE, T], F32, scr - 4 * T)
        hh, o = at("ffn_hi", [P, 2, T], F32R, scr)
        hl, o = at("ffn_lo", [P, 2, T], F32R, o)
        sg, o = at("ffn_act", [P, NB, TB], F32, o)
        praw, o = at("ple_raw", [P, 2, T], F32, scr)
        ph, o = at("ple_hi", [P, 2, T], F32R, o)
        pl, o = at("ple_lo", [P, 2, T], F32R, o)
        gt, o = at("gate", [P, 2, TB], F32, o)
        assert o <= top
        yo = scr - 4 * KD * T
        fz, o = at("forget_z", [H, T], F32, yo)
        fe, o = at("forget_e", [H, T], F32, o)
        fu, o = at("forget_u", [H, T], F32, o)
        fl, o = at("forget_l", [H, T], F32, o)
        flog, o = at("forget_log", [H, TK], F32, o)
        fcum, o = at("forget_cum", [H, TK], F32, o)
        qh, o = at("q_hi", [P, 2, T], F32R, attn_off)
        ql, o = at("q_lo", [P, 2, T], F32R, o)
        kh, o = at("k_hi", [P, 2, TK], F32R, o)
        kl, o = at("k_lo", [P, 2, TK], F32R, o)
        vh, o = at("v_hi", [P, 2, KT, VD], F32R, o)
        vl, o = at("v_lo", [P, 2, KT, VD], F32R, o)
        pr, o = at("probs", [P, 3, SEQ], F32, o)
        pth, o = at("probs_t_hi", [P, 2, 8, P], F32R, o)
        ptl, o = at("probs_t_lo", [P, 2, 8, P], F32R, o)
        nmx, o = at("neg_max", [P, 2], F32, o)
        rsum, o = at("row_sum", [P, 2], F32, o)
        rinv, o = at("row_inv", [P, 2], F32, o)
        assert o <= top
        rawoff = attn_off - 3 * UW * 4
        qraw, o = at("q_raw", [P, T], F32, rawoff)
        kraw, o = at("k_raw", [P, TK], F32, o)
        vraw, o = at("v_raw", [P, KT, VD], F32, o)
        assert o == attn_off

        ps = ctx.enter_context(nc.psum_tensor("ps", [P, 8, 512], F32))

        def sem(name):
            return ctx.enter_context(nc.semaphore(name))

        const_in = sem("const_in")
        ones_set = sem("ones_set")
        const_r = sem("const_r")
        x_in = [sem(f"x_in{b}") for b in range(NB)]
        w_raw = [sem(f"w_raw{s}") for s in range(3)]
        w_gain = [sem(f"w_gain{s}") for s in range(2)]
        w_hi = [sem(f"w_hi{s}") for s in range(3)]
        w_rdy = [sem(f"w_rdy{s}") for s in range(3)]
        lin_rd = sem("lin_rd")
        lin_ev = sem("lin_ev")
        n_sq, n_mm, n_rt = sem("norm_squares"), sem("norm_sum"), sem("norm_root")
        n_rs, n_ap, n_hi, n_done = sem("norm_rstd"), sem("norm_applied"), sem("norm_hi"), sem("norm_done")
        kv_raw = sem("kv_raw")
        tab_in, cache_in, p_in = sem("tab_in"), sem("cache_in"), sem("p_in")
        cc_hi, cc_lo = sem("cc_hi"), sem("cc_lo")
        q_raw = sem("q_raw")
        kr_a, kr_done = sem("kr_products"), sem("kr_done")
        q_done = sem("q_done")
        st_out = [sem("st_out0"), sem("st_out1")]
        ckv_out, kr_out, lf_out, nck_out, y_out = (sem("ckv_out"), sem("kr_out"), sem("lf_out"),
                                                   sem("nck_out"), sem("y_out"))
        fg_rd, fu_rd, fd_rd = sem("ffn_gate_rd"), sem("ffn_up_rd"), sem("ffn_down_rd")
        f_sg, f_u, f_hi, f_lo, f_acc = (sem("ffn_silu"), sem("ffn_mul"), sem("ffn_hi_done"),
                                        sem("ffn_lo_done"), sem("ffn_acc"))
        p_hi, p_lo, g_mul = sem("ple_hi_done"), sem("ple_lo_done"), sem("gate_mul")
        fx_a, fx_v = sem("forget_act"), sem("forget_dve")
        at_raw, at_khi, at_split = sem("at_raw"), sem("at_split_hi"), sem("at_split")
        at_kr, at_fix = sem("at_kr"), sem("at_fixed_rows")
        at_s, at_t, at_pv = sem("at_scores"), sem("at_turned"), sem("at_pv")
        at_nm, at_r, at_p, at_lo, at_olo = (sem("at_negmax"), sem("at_rinv"), sem("at_probs"),
                                            sem("at_pt_lo"), sem("at_o_lo"))
        at_e, at_hi, at_ohi = sem("at_exp"), sem("at_pt_hi"), sem("at_o_hi")
        fences = {e: sem(f"fence_{e}") for e in ("pe", "act", "dve", "pool", "sp")}

        def fence(eng, me, n):
            eng.drain().then_inc(fences[me], 1)
            for e, s in fences.items():
                if e != me:
                    eng.wait_ge(s, n)

        def bank(g):
            return g % LBANKS

        kA, vA, qA, qB, nck = io["kA"], io["vA"], io["qA"], io["qB"], io["nck"]

        def turned(s, i, buf):
            if i < 8:
                n = i + 1
                return [(P, buf[:, s % 2, 0:n, :],
                         ps[:, 4:6, :].rearrange("p a (t q) -> p (a t) q", q=P)[:, 0:n, :])]
            v = ps[:, 4, :].rearrange("p (t q) -> p t q", q=P)
            return [(P, buf[:, s % 2, 0:2, 0:DEC], v[:, 0:2, 0:DEC]), (DEC, buf[0:DEC, s % 2, 2, 0:DEC], v[0:DEC, 2, 0:DEC])]

        block = ctx.enter_context(nc.Block())

        @block.sync
        def _(sp):
            def load_unit(name, slot, use, unit):
                if not (isinstance(use, int) and use == 0):
                    sp.wait_ge(w_rdy[slot], use)
                sp.dma_start(wraw[:, slot, :], io["units"][unit]).then_inc(w_raw[slot], 16)

            def lin_load(name, j):
                load_unit(name, j % 2, USED[name][j % 2] + j // 2, UNIT0[name] + j)

            def lin_load_pair(name, i):
                for s in range(2):
                    load_unit(name, s, i + USED[name][s], i * 2 + (UNIT0[name] + s))

            sp.dma_start(gains[:], io["gains"]).then_inc(const_in, 16)
            sp.dma_start(ident[:], io["ident"]).then_inc(const_in, 16)
            for b in range(NB):
                sp.dma_start(res[:, :, b * TB:(b + 1) * TB], io["xT"][:, :, b * TB:(b + 1) * TB]).then_inc(x_in[b], 16)
                if b == 0:
                    lin_load("dq", 0)
                    lin_load("dq", 1)
            sp.dma_start(y[:, 0, 0:2 * P], io["masks"]).then_inc(const_in, 16)
            sp.dma_start(krt[:], io["krt"]).then_inc(tab_in, 16)
            sp.dma_start(cc[:], io["cckvT"]).then_inc(cache_in, 16)
            lin_load("dq", 2)
            lin_load("dq", 3)
            for name in ("dkv", "kr"):
                for j in range(dict((n, c) for n, c, _ in LIN)[name]):
                    lin_load(name, j)
            lin_load("uk", 0)
            lin_load("uk", 1)
            sp.wait_ge(kr_done, NB)
            sp.dma_start(io["kr_out"], krf[:]).then_inc(kr_out, 16)
            sp.wait_ge(n_ap, NORM_AT["s1", "kv", 2] + 1)
            sp.dma_start(io["ckv_out"], y[:, 6:8, :]).then_inc(ckv_out, 16)
            fence(sp, "sp", 1)
            sp.dma_start(cs[:], io["cs"]).then_inc(tab_in, 16)

            def store(slot, dst, src, waits, count=1):
                for s, v in waits:
                    sp.wait_ge(s, v)
                sp.dma_start(dst, src).then_inc(st_out[slot], 16)

            for m in range(8):
                if m < 2:
                    lin_load("uv", m)
                store(m % 2, kA[m * P:(m + 1) * P, :], stg[:, m % 2, :], [(lin_ev, GROUP0["uk"] + KB * (m + 1))])
            lin_load("uq", 0)
            lin_load("uq", 1)
            for g in range(2 * KT):
                half, kt = g // KT, g % KT
                rows = min(P, TK - kt * P)
                store(g % 2, vA[kt * P:kt * P + rows, half * 512:(half + 1) * 512], stg[0:rows, g % 2, 0:512],
                      [(lin_ev, GROUP0["uv"] + g + 1)])
            with sp.Fori(0, 3) as i:
                for s in range(2):
                    load_unit("uq", s, i + (USED["uq"][s] + 1), i * 2 + (UNIT0["uq"] + 2 + s))
                for h in range(4):
                    sp.wait_ge(q_done, i * 12 + NB * (h + 1))
                    sp.dma_start(qA[i * 4 + h], stg[:, h % 2, 0:T]).then_inc(st_out[h % 2], 16)
            for h in range(4):
                sp.wait_ge(q_done, 36 + NB * (h + 1))
                sp.dma_start(qA[12 + h], stg[:, h % 2, 0:T]).then_inc(st_out[h % 2], 16)
            for s in range(2):
                sp.wait_ge(st_out[s], 16 * (4 + KT + 8))
            sp.wait_ge(ckv_out, 16)
            sp.wait_ge(kr_out, 16)
            fence(sp, "sp", 2)

            def attn_loads(layer, h, first):
                if not first:
                    sp.wait_ge(at_split, h + layer * H)
                n = 0
                if layer == 0:
                    sp.dma_start(qraw[:], qA[h]).then_inc(at_raw, 16)
                    sp.dma_start(kraw[0:NOPE, :], io["kA_h"][h]).then_inc(at_raw, 16)
                    sp.dma_start(vraw[:, 0:KT - 1, :], io["vA_full"][h]).then_inc(at_raw, 16)
                    sp.dma_start(vraw[0:TK % P, KT - 1, :], io["vA_last"][h]).then_inc(at_raw, 16)
                else:
                    sp.dma_start(qraw[0:HD, :], qB[h]).then_inc(at_raw, 16)
                    sp.dma_start(kraw[HD:HD + 1, :], nck[h]).then_inc(at_raw, 16)

            def attn_loads_kv(kv):
                sp.dma_start(kraw[0:HD, 0:T], io["kT_h"][kv]).then_inc(at_raw, 16)
                sp.dma_start(kraw[0:HD, T:TK], io["ckT"][kv]).then_inc(at_raw, 16)
                sp.dma_start(vraw[:, 0:8, :], io["v_full"][kv]).then_inc(at_raw, 16)
                sp.dma_start(vraw[0:DEC, 8, :], io["v_new"][kv]).then_inc(at_raw, 16)
                sp.dma_start(vraw[DEC:P, 8, :], io["cv0"][kv]).then_inc(at_raw, 16)
                sp.dma_start(vraw[:, 9, :], io["cv1"][kv]).then_inc(at_raw, 16)
                sp.dma_start(vraw[0:DEC, 10, :], io["cv2"][kv]).then_inc(at_raw, 16)

            for r in range(2):
                rows = slice(NOPE + r * ROPE, NOPE + (r + 1) * ROPE)
                sp.dma_start(kraw[rows, 0:T], io["kr_out"]).then_inc(at_kr, 16)
                sp.dma_start(kraw[rows, T:TK], io["ckrT"]).then_inc(at_kr, 16)
            attn_loads(0, 0, True)
            with sp.Fori(1, H) as h:
                attn_loads(0, h, False)
            fence(sp, "sp", 3)

            def tail_loads(layer):
                name = ("oa", "ob")[layer]
                with sp.Fori(0, 4) as i:
                    lin_load_pair(name, i)
                name = f"ffn{layer}"
                u0 = UNIT0[name]
                for s in range(2):
                    load_unit(name, s, USED[name][s], u0 + s)
                with sp.Fori(0, NF - 1) as f:
                    for k, (s, df) in enumerate(((0, 1), (2, 0), (1, 1))):
                        load_unit(name, s, f + (USED[name][s] + df), f * 3 + (u0 + 2 + k))
                load_unit(name, 2, USED[name][2] + NF - 1, u0 + 3 * NF - 1)
                for j in range(2):
                    lin_load(f"pe{layer}", j)
                sp.wait_ge(n_done, NORM_AT[f"s{3 + 3 * layer}", "pre", 2] + 1)
                sp.dma_start(praw[:], io["pT"][layer]).then_inc(p_in, 16)
                with sp.Fori(0, 4) as i:
                    lin_load_pair(f"pg{layer}", i)

            tail_loads(0)

            for j in range(2):
                lin_load("kb", j)
            fence(sp, "sp", 4)
            for name, j in (("wf", 0), ("vb", 0), ("vb", 1)):
                lin_load(name, j)
            sp.dma_start(flog[:, T:TK], io["clfT"]).then_inc(cache_in, 16)
            for m in range(2):
                store(m, io["kT_out"][m * P:(m + 1) * P, :], stg[:, m, 0:T], [(lin_ev, GROUP0["kb"] + NB * (m + 1))])
            for tt in range(9):
                rows = min(P, T - tt * P)
                store(tt % 2, io["v_out"][tt * P:tt * P + rows, :], stg[0:rows, tt % 2, 0:KVH * HD],
                      [(lin_ev, GROUP0["vb"] + tt + 1)])
            sp.wait_ge(fx_v, 6)
            sp.dma_start(io["lf_out"], flog[:, 0:T]).then_inc(lf_out, 16)
            sp.wait_ge(fx_v, 10)
            sp.dma_start(io["nck_all"], fcum[:]).then_inc(nck_out, 16)
            with sp.Fori(0, 4) as i:
                lin_load_pair("qb", i)
                for m in range(2):
                    sp.wait_ge(lin_ev, i * 6 + (GROUP0["qb"] + NB * (m + 1)))
                    sp.dma_start(io["qB_pair"][i * 2 + m], stg[:, m, 0:T]).then_inc(st_out[m], 16)
            for s in range(2):
                sp.wait_ge(st_out[s], 16 * (4 + KT + 8 + 1 + (5 - s) + 4))
            sp.wait_ge(lf_out, 16)
            sp.wait_ge(nck_out, 16)
            fence(sp, "sp", 5)
            for h in range(4):
                if h:
                    sp.wait_ge(at_split, H + h)
                attn_loads_kv(0)
                attn_loads(1, h, True)
            with sp.Fori(1, KVH) as kv:
                for g in range(4):
                    sp.wait_ge(at_split, kv * 4 + (H + g))
                    attn_loads_kv(kv)
                    attn_loads(1, kv * 4 + g, True)
            fence(sp, "sp", 6)
            tail_loads(1)
            for b in range(NB):
                sp.wait_ge(n_done, NORM_AT["s7", "post", b] + 1)
                sp.dma_start(io["yT"][:, :, b * TB:(b + 1) * TB], res[:, :, b * TB:(b + 1) * TB]).then_inc(y_out, 16)
            sp.wait_ge(y_out, 16 * NB)

        @block.gpsimd
        def _(pool):
            LAST = {}

            def split(slot, use, gain, gained=None, free=None):
                raw = wraw[:, slot, :]
                pool.wait_ge(w_raw[slot], use * 16 + 16)
                if gain is not None:
                    g = gains[:, GAIN_AT[gain]:GAIN_AT[gain] + 8].unsqueeze(2).to_broadcast((P, 8, P))
                    raw8 = raw.rearrange("p (k m) -> p k m", k=8)
                    pool.tensor_tensor(raw8, raw8, g, ALU.mult).then_inc(w_gain[slot], 1)
                    pool.wait_ge(w_gain[slot], gained + 1)
                if free is not None:
                    pool.wait_ge(*free)
                pool.tensor_tensor(wh[:, slot, :], raw, ones[:, 0:1].to_broadcast((P, UW)), ALU.mult).then_inc(w_hi[slot], 1)
                pool.wait_ge(w_hi[slot], use + 1)
                pool.tensor_tensor(wl[:, slot, :], raw, wh[:, slot, :].bitcast(F32), ALU.subtract).then_inc(w_rdy[slot], 1)

            def lin_split(name, j, gain):
                s = j % 2
                split(s, USED[name][s] + j // 2, gain, GAINED[name][s] + j // 2, LAST.get(s))
                LAST[s] = (lin_rd, group_after(name, s, j // 2))

            def lin_split_loop(name, gain, n=4):
                for s in range(2):
                    split(s, USED[name][s], gain, GAINED[name][s], LAST.get(s))
                with pool.Fori(1, n) as i:
                    for s in range(2):
                        split(s, i + USED[name][s], gain, i + GAINED[name][s],
                              (lin_rd, (i - 1) * (2 * PER_UNIT[name]) + group_after(name, s, 0)))
                for s in range(2):
                    LAST[s] = (lin_rd, group_after(name, s, n - 1))

            def attn_split(layer, parity, h, first):
                pool.wait_ge(at_raw, h * 64 + 64 if layer == 0 else h * 144 + (16 * 4 * H - 144 * H + 144))
                if not first:
                    pool.wait_ge(at_pv, h * STEPS - STEPS)
                krows = NOPE if layer == 0 else HD + 1
                qrows = P if layer == 0 else HD
                parts = [(qh[0:qrows, parity, :], ql[0:qrows, parity, :], qraw[0:qrows, :], qrows, T),
                         (kh[0:krows, parity, :], kl[0:krows, parity, :], kraw[0:krows, :], krows, TK),
                         (vh[:, parity, 0:KT - 1, :], vl[:, parity, 0:KT - 1, :], vraw[:, 0:KT - 1, :], P, 0),
                         (vh[0:TK % P, parity, KT - 1, :], vl[0:TK % P, parity, KT - 1, :],
                          vraw[0:TK % P, KT - 1, :], TK % P, VD)]
                for hi, lo, raw, rows, n in parts:
                    one = (ones[0:rows, 0:1].to_broadcast((rows, n)) if n else
                           ones[:, 0:1].unsqueeze(2).to_broadcast((P, KT - 1, VD)))
                    last = pool.tensor_tensor(hi, raw, one, ALU.mult)
                last.then_inc(at_khi, 1)
                pool.wait_ge(at_khi, h + 1)
                for hi, lo, raw, rows, n in parts:
                    last = pool.tensor_tensor(lo, raw, hi.bitcast(F32), ALU.subtract)
                last.then_inc(at_split, 1)

            pool.wait_ge(const_in, 48)
            pool.wait_ge(ones_set, 1)
            for j in range(4):
                lin_split("dq", j, "mix_pre0")
            for j in range(2):
                lin_split("dkv", j, "mix_pre0")
            lin_split("kr", 0, "mix_pre0")
            for j in range(2):
                lin_split("uk", j, None)
            fence(pool, "pool", 1)
            for j in range(2):
                lin_split("uv", j, None)
            lin_split_loop("uq", "q")
            fence(pool, "pool", 2)

            pool.wait_ge(at_kr, 64)
            rows = slice(NOPE, P)
            for r in (slice(64, 96), slice(96, 128)):
                for b in range(2):
                    last = pool.tensor_tensor(kh[r, b, :], kraw[r, :], ones[r, 0:1].to_broadcast((ROPE, TK)), ALU.mult)
            last.then_inc(at_fix, 1)
            pool.wait_ge(at_fix, 1)
            for r in (slice(64, 96), slice(96, 128)):
                for b in range(2):
                    last = pool.tensor_tensor(kl[r, b, :], kraw[r, :], kh[r, b, :].bitcast(F32), ALU.subtract)
            last.then_inc(at_fix, 1)
            pool.wait_ge(at_fix, 2)
            for b in range(2):
                attn_split(0, b, b, True)
            with pool.Fori(1, H // 2) as i:
                for b in range(2):
                    attn_split(0, b, i * 2 + b, False)
            fence(pool, "pool", 3)

            def tail_splits(layer):
                lin_split_loop(("oa", "ob")[layer], None)
                name, gain = f"ffn{layer}", f"ffn_pre{layer}"
                u, g = USED[name], GAINED[name]
                f0 = layer * NF
                for s in range(2):
                    split(s, u[s], gain, g[s], LAST[s])

                def tile(f, down_free):
                    split(0, f + (u[0] + 1), gain, f + (g[0] + 1), (fg_rd, f * 3 + (3 * f0 + 3)))
                    split(2, f + u[2], None, None, down_free)
                    split(1, f + (u[1] + 1), gain, f + (g[1] + 1), (fu_rd, f * 3 + (3 * f0 + 3)))

                tile(0, LAST.get(2))
                with pool.Fori(1, NF - 1) as f:
                    tile(f, (fd_rd, f * 24 + 24 * f0))
                split(2, u[2] + NF - 1, None, None, (fd_rd, 24 * (f0 + NF - 1)))
                LAST[0], LAST[1] = (fg_rd, 3 * (f0 + NF)), (fu_rd, 3 * (f0 + NF))
                LAST[2] = (fd_rd, 24 * (f0 + NF))
                for j in range(2):
                    lin_split(f"pe{layer}", j, None)
                lin_split_loop(f"pg{layer}", f"ple_gate{layer}")

            tail_splits(0)
            for j in range(2):
                lin_split("kb", j, "shared")
            fence(pool, "pool", 4)
            lin_split("wf", 0, "shared")
            for j in range(2):
                lin_split("vb", j, ("shared_v", "shared_v2")[j])
            lin_split_loop("qb", "mix_pre1")
            fence(pool, "pool", 5)
            for b in range(2):
                pool.memset(qh[HD:HD + 1, b, :].bitcast(F32), 1.0)
                last = pool.memset(ql[HD:HD + 1, b, :].bitcast(F32), 0.0)
            last.then_inc(at_fix, 1)
            pool.wait_ge(at_fix, 3)
            for b in range(2):
                attn_split(1, b, H + b, True)
            with pool.Fori(1, H // 2) as i:
                for b in range(2):
                    attn_split(1, b, i * 2 + (H + b), False)
            fence(pool, "pool", 6)
            tail_splits(1)

        @block.tensor
        def _(pe):
            def three(out, ah, al, bh, bl, first, last):
                nc.tensor.matmul(out, ah, bh, start=first, stop=False)
                nc.tensor.matmul(out, ah, bl, start=False, stop=False)
                return nc.tensor.matmul(out, al, bh, start=False, stop=last)

            def wcols(slot, c0, n):
                return wh[:, slot, c0:c0 + n], wl[:, slot, c0:c0 + n]

            def bank_free(g):
                if not isinstance(g, int) or g >= LBANKS:
                    pe.wait_ge(lin_ev, g - (LBANKS - 1))

            def lin_unit(g0, b0, slot, use, xh, xl, K, heads, M, blocks, first_waits=()):
                pe.wait_ge(w_rdy[slot], use + 1)
                n = 0
                for m in range(heads):
                    for b, (c, w) in enumerate(blocks):
                        if m == 0 and first_waits:
                            for s, v in first_waits[b]:
                                pe.wait_ge(s, v)
                        bank_free(g0 + n)
                        out = ps[0:M, (b0 + n) % LBANKS, 0:w]
                        for k in range(K):
                            ah, al = wcols(slot, (m * K + k) * P, M)
                            mm = three(out, ah, al, xh[:, k, c:c + w], xl[:, k, c:c + w], k == 0, k == K - 1)
                        n += 1
                        mm.then_inc(lin_rd, 1)

            TBL = [(b * TB, TB) for b in range(NB)]

            def lin_static(name, xh, xl, K=8, heads=1, M=P, blocks=TBL, waits=()):
                n = {nm: c for nm, c, _ in LIN}[name]
                per = heads * len(blocks)
                for j in range(n):
                    g = GROUP0[name] + j * per
                    lin_unit(g, g, j % 2, USED[name][j % 2] + j // 2, xh, xl, K, heads, M, blocks,
                             waits if j == 0 else ())

            def lin_loop(name, xh, xl, K=8, heads=1, waits=()):
                per = heads * NB
                for b in waits:
                    for s, v in b:
                        pe.wait_ge(s, v)
                with pe.Fori(0, 4) as i:
                    for s in range(2):
                        g = GROUP0[name] + s * per
                        lin_unit(i * (2 * per) + g, g, s, i + USED[name][s], xh, xl, K, heads, P, TBL)

            def norm(key, K):
                k = NORM_AT[key]
                pe.wait_ge(n_sq, k + 1)
                if k:
                    pe.wait_ge(n_rt, k)
                for j in range(K):
                    mm = nc.tensor.matmul(ps[:, 7, 0:TB], ones[:], sq[:, k % 2, j, :], start=(j == 0), stop=(j == K - 1))
                mm.then_inc(n_mm, 1)

            def norm_chain(s):
                for kind, b in CHAIN:
                    norm((s, kind, b), KD)

            def n_ready(s, kind="pre"):
                return [[(n_done, NORM_AT[s, kind, b] + 1)] for b in range(NB)]

            pe.wait_ge(ones_set, 1)
            for b in range(NB):
                norm(("s0", "pre", b), KD)
            lin_static("dq", nh, nl, waits=n_ready("s0"))
            lin_static("dkv", nh, nl)
            lin_static("kr", nh, nl, M=2 * ROPE)
            for kind, K in (("q", 4), ("kv", 2)):
                for b in range(NB):
                    norm(("s1", kind, b), K)
            fence(pe, "pe", 1)
            KBL = [(b * TKB, TKB) for b in range(KB)]
            lin_static("uk", cvh, cvl, K=2, heads=4, blocks=KBL)
            for half in range(2):
                pe.wait_ge(w_rdy[half], USED["uv"][half] + 1)
                for kt in range(KT):
                    g = GROUP0["uv"] + half * KT + kt
                    rows = min(P, TK - kt * P)
                    bank_free(g)
                    for k in range(2):
                        c = slice(kt * P, kt * P + rows)
                        bh, bl = wcols(half, k * 512, 512)
                        mm = three(ps[0:rows, bank(g), :], cvh[:, k, c], cvl[:, k, c], bh, bl, k == 0, k == 1)
                    mm.then_inc(lin_rd, 1)
            lin_loop("uq", nh, nl, K=4, heads=2)
            fence(pe, "pe", 2)

            def attn_pe(layer):
                rows = P if layer == 0 else HD + 1

                def scores(n0, s, first):
                    hp, i = s // STEPS, ORDER[s % STEPS]
                    if s % STEPS == 0:
                        pe.wait_ge(at_split, first[1] * 2 + (layer * H + hp + 1))
                    if not (first[0] and s < 2):
                        pe.wait_ge(at_e, n0 + (s - 1))
                    qc = slice(i * P, i * P + (P if i < 8 else DEC))
                    M = P if i < 8 else DEC
                    k0, k1 = (0, (i + 1) * P) if i < 8 else (SEQ, TK)
                    buf = 2 * (s % 2)
                    masked = i < 8 or layer == 1
                    nb = 0
                    c = k0
                    while c < k1:
                        w = min(512, k1 - c)
                        out = ps[0:M, buf + nb, 0:w]
                        dg = masked and (c + w == k1 if i < 8 else c == k0)
                        mm = three(out, qh[0:rows, hp, qc], ql[0:rows, hp, qc], kh[0:rows, hp, c:c + w],
                                   kl[0:rows, hp, c:c + w], True, not dg)
                        if dg:
                            dc = w - P if i < 8 else 0
                            mm = nc.tensor.matmul(ps[0:M, buf + nb, dc:dc + M], ident_r[0:M, 0:M],
                                                  mask_r[0:M, layer, 0:M], start=False, stop=True)
                        c += w
                        nb += 1
                    mm.then_inc(at_s, 1)

                def turn(n0, s, first):
                    hp, i = (s % PAIR) // STEPS, ORDER[s % STEPS]
                    if i == 8:
                        pe.wait_ge(const_in, 48)
                    pe.wait_ge(at_p, n0 + (s + 1))
                    if not (first[0] and s == 0):
                        pe.wait_ge(at_lo, n0 + s)
                    M = P if i < 8 else DEC
                    n = i + 1 if i < 8 else 3
                    if i >= 4 and i != 8 and ORDER[s % STEPS - 2] == 8:
                        pe.wait_ge(at_olo, (olo0(n0, s, first)) + 1)
                    for kt in range(n):
                        kr = P if (i < 8 or kt < 2) else DEC
                        mm = nc.tensor.transpose(ps[0:kr, 4 + kt // 4, (kt % 4) * P:(kt % 4) * P + M],
                                                 pr[0:M, s % 3, kt * P:kt * P + kr], ident[0:M, 0:M])
                    mm.then_inc(at_t, 1)

                def olo0(n0, s, first):
                    hp = (s % PAIR) // STEPS
                    return first[1] * 4 + (layer * 2 * H + 2 * hp)

                def pv(n0, s, first):
                    hp, i = (s % PAIR) // STEPS, ORDER[s % STEPS]
                    pe.wait_ge(at_lo, n0 + (s + 1))
                    if s % STEPS == 0 and not (first[0] and s == 0):
                        pe.wait_ge(at_olo, olo0(n0, s, first))
                    M = P if i < 8 else DEC
                    n = i + 1 if i < 8 else 3
                    if i < 8:
                        out = ps[0:VD, 6 + i // 4, (i % 4) * P:(i % 4 + 1) * P]
                    else:
                        out = ps[0:VD, 5, 0:DEC]
                    for kt in range(n):
                        kr = P if (i < 8 or kt < 2) else DEC
                        vt = kt if i < 8 else 8 + kt
                        mm = three(out, vh[0:kr, hp, vt, :], vl[0:kr, hp, vt, :], pth[0:kr, s % 2, kt, 0:M],
                                   ptl[0:kr, s % 2, kt, 0:M], kt == 0, kt == n - 1)
                    mm.then_inc(at_pv, 1)

                base_n = layer * H * STEPS

                def pair(n0, i, first):
                    for s in range(PAIR):
                        scores(n0, s, (first, i))
                        for lag, fn in ((T_LAG, turn), (PV_LAG, pv)):
                            if s >= lag:
                                fn(n0, s - lag, (first, i))
                            elif not first:
                                fn(n0 - PAIR, s - lag + PAIR, (False, i - 1))

                pair(base_n, 0, True)
                with pe.Fori(1, H // 2) as i:
                    pair(i * PAIR + base_n, i, False)
                n0 = base_n + (H // 2 - 1) * PAIR
                for s in range(PAIR, PAIR + PV_LAG):
                    if s - T_LAG < PAIR:
                        turn(n0, s - T_LAG, (False, H // 2 - 1))
                    pv(n0, s - PV_LAG, (False, H // 2 - 1))

            attn_pe(0)
            fence(pe, "pe", 3)

            def ffn_pe(layer):
                name = f"ffn{layer}"
                u = USED[name]
                f0 = layer * NF

                def down(f, par, d):
                    m, b = d // NB, d % NB
                    if d == 0:
                        pe.wait_ge(w_rdy[2], f + (u[2] + 1))
                        pe.wait_ge(f_lo, f * 3 + (3 * f0 + 3))
                    if not (isinstance(f, int) and f == 0 and layer == 0 and d < 2):
                        pe.wait_ge(f_acc, f * 24 + (24 * f0 + d - 1))
                    mm = three(ps[:, 6 + d % 2, 0:TB], wh[:, 2, m * P:(m + 1) * P], wl[:, 2, m * P:(m + 1) * P],
                               hh[:, par, b * TB:(b + 1) * TB], hl[:, par, b * TB:(b + 1) * TB], True, True)
                    mm.then_inc(fd_rd, 1)

                def tile(f, par, first):
                    n, d = 0, 0
                    for slot, rd, freed in ((0, fg_rd, f_sg), (1, fu_rd, f_u)):
                        pe.wait_ge(w_rdy[slot], f + (u[slot] + 1))
                        for b in range(NB):
                            if first and slot == 0:
                                pe.wait_ge(n_done, NORM_AT[f"s{2 + 3 * layer}", "pre", b] + 1)
                            if not (first and layer == 0):
                                pe.wait_ge(freed, f * 3 + (3 * f0 + b - 2))
                            for k in range(KD):
                                xh, xl = nh[:, k, b * TB:(b + 1) * TB], nl[:, k, b * TB:(b + 1) * TB]
                                ah, al = wcols(slot, k * P, P)
                                for pas, (a, x) in enumerate(((ah, xh), (ah, xl), (al, xh))):
                                    mm = nc.tensor.matmul(ps[:, 3 * slot + b, 0:TB], a, x, start=(k == 0 and pas == 0),
                                                          stop=(k == KD - 1 and pas == 2))
                                    if k == KD - 1 and pas == 2:
                                        mm.then_inc(rd, 1)
                                    n += 1
                                    if not first and d < 24 and n == D_AT[d]:
                                        down(f - 1, 1 - par, d)
                                        d += 1

                tile(0, 0, True)
                tile(1, 1, False)
                with pe.Fori(1, NF // 2) as i:
                    for par in range(2):
                        tile(i * 2 + par, par, False)
                for d in range(24):
                    down(NF - 1, (NF - 1) % 2, d)

            def tail_pe(layer):
                s0 = 2 + 3 * layer
                lin_loop(("oa", "ob")[layer], nh, nl)
                norm_chain(f"s{s0}")
                ffn_pe(layer)
                norm_chain(f"s{s0 + 1}")
                pe.wait_ge(p_lo, layer + 1)
                lin_static(f"pe{layer}", ph, pl, K=2, heads=4)
                lin_loop(f"pg{layer}", nh, nl, waits=n_ready(f"s{s0 + 1}"))

            tail_pe(0)
            norm_chain("s4")
            fence(pe, "pe", 4)
            lin_static("kb", nh, nl)
            lin_static("wf", nh, nl, M=H)
            for j in range(2):
                pe.wait_ge(w_rdy[j], USED["vb"][j] + 1)
            for tt in range(9):
                g = GROUP0["vb"] + tt
                rows = min(P, T - tt * P)
                bank_free(g)
                for k in range(KD):
                    bh, bl = wcols(k // 4, (k % 4) * KVH * HD, KVH * HD)
                    c = slice(tt * P, tt * P + rows)
                    mm = three(ps[0:rows, bank(g), 0:KVH * HD], nh[:, k, c], nl[:, k, c], bh, bl, k == 0, k == KD - 1)
                mm.then_inc(lin_rd, 1)
            lin_loop("qb", nh, nl)
            fence(pe, "pe", 5)
            attn_pe(1)
            fence(pe, "pe", 6)
            tail_pe(1)
            for b in range(NB):
                norm(("s7", "post", b), KD)

        @block.scalar
        def _(act):
            def take(g, b, out, rows, w, func=ACT.Copy, **kw):
                act.wait_ge(lin_rd, g + 1)
                nc.scalar.activation(out, ps[0:rows, b, 0:w], func, **kw).then_inc(lin_ev, 1)

            SRC = {"q": (0, 4), "kv": (4, 2)}

            def squares(key, waits):
                k = NORM_AT[key]
                s, kind, b = key
                for sm, v in waits:
                    act.wait_ge(sm, v)
                if k >= 2:
                    act.wait_ge(n_done, k - 1)
                c = slice(b * TB, (b + 1) * TB)
                if kind == "pre":
                    src, K = res[:, :, c], KD
                elif kind == "post":
                    src, K = y[:, :, c], KD
                else:
                    k0, K = SRC[kind]
                    src = y[:, k0:k0 + K, c]
                nc.scalar.activation(sq[:, k % 2, 0:K, :], src, ACT.Square).then_inc(n_sq, 1)

            def rest(key, hi_waits=()):
                k = NORM_AT[key]
                s, kind, b = key
                width = {"q": Q_RANK, "kv": KV_RANK}.get(kind, D)
                act.wait_ge(n_mm, k + 1)
                if k >= 2:
                    act.wait_ge(n_rs, k - 1)
                nc.scalar.activation(rt[:, k % 2, :], ps[:, 7, 0:TB], ACT.Sqrt, bias=epsc[:, 0:1],
                                     scale=1.0 / width).then_inc(n_rt, 1)
                if kind != "post":
                    for sm, v in hi_waits:
                        act.wait_ge(sm, v)
                    act.wait_ge(n_ap, k + 1)
                    c = slice(b * TB, (b + 1) * TB)
                    if kind == "kv":
                        out, K = cvh[:, :, c], 2
                    elif kind == "q":
                        out, K = nh[:, 0:4, c], 4
                    else:
                        out, K = nh[:, :, c], KD
                    src = y[:, 6:8, c] if kind == "kv" else sq[:, k % 2, 0:K, :]
                    nc.scalar.activation(out, src, ACT.Copy).then_inc(n_hi, 1)

            def norms(keys, waits, hi_waits=()):
                last = None
                for key in keys:
                    squares(key, waits(key))
                    if last:
                        rest(last, hi_waits)
                    last = key
                rest(last, hi_waits)

            def chain_waits(ready):
                def waits(key):
                    s, kind, b = key
                    if kind == "post":
                        return ready[b]
                    return [(n_done, NORM_AT[s, "post", b] + 1)]
                return waits

            act.wait_ge(ones_set, 1)
            norms([("s0", "pre", b) for b in range(NB)], lambda key: [(x_in[key[2]], 16)])
            act.wait_ge(const_r, 1)
            for m in range(6):
                for b in range(NB):
                    g = GROUP0["dq"] + m * NB + b
                    take(g, bank(g), y[:, m, b * TB:(b + 1) * TB], P, TB)
            for b in range(NB):
                g = GROUP0["kr"] + b
                take(g, bank(g), y[0:2 * ROPE, 6, b * TB:(b + 1) * TB], 2 * ROPE, TB)
            norms([("s1", "q", b) for b in range(NB)] + [("s1", "kv", b) for b in range(NB)],
                  lambda key: [(lin_ev, GROUP0["kr"] + 3)])
            act.wait_ge(cache_in, 16)
            nc.scalar.activation(cvh[:, :, T:TK], cc[:], ACT.Copy).then_inc(cc_hi, 1)
            fence(act, "act", 1)
            for m in range(8):
                if m >= 2:
                    act.wait_ge(st_out[m % 2], 16 * (m // 2))
                for b in range(KB):
                    g = GROUP0["uk"] + m * KB + b
                    take(g, bank(g), stg[:, m % 2, b * TKB:(b + 1) * TKB], P, TKB)
            for g in range(2 * KT):
                rows = min(P, TK - (g % KT) * P)
                act.wait_ge(st_out[g % 2], 16 * (4 + g // 2))
                take(GROUP0["uv"] + g, bank(GROUP0["uv"] + g), stg[0:rows, g % 2, 0:512], rows, 512)
            with act.Fori(0, 4) as i:
                for h in range(4):
                    act.wait_ge(st_out[h % 2], i * 32 + 16 * (4 + KT + h // 2))
                    for b in range(NB):
                        g = GROUP0["uq"] + h * NB + b
                        take(i * 12 + g, bank(g), stg[:, h % 2, b * TB:(b + 1) * TB], P, TB)
            fence(act, "act", 2)

            def attn_act(layer):
                base_n = layer * H * STEPS
                scale = 1.0

                def exps(n0, s, first):
                    i = ORDER[s % STEPS]
                    M = P if i < 8 else DEC
                    n = (i + 1) * P if i < 8 else TK - SEQ
                    act.wait_ge(at_nm, n0 + (s + 1))
                    if not (first and s < 3):
                        act.wait_ge(at_t, n0 + (s - 2))
                    src = ps[0:M, 2 * (s % 2):2 * (s % 2) + 2, :].rearrange("p a b -> p (a b)")[:, 0:n]
                    nc.scalar.activation(pr[0:M, s % 3, 0:n], src, ACT.Exp, bias=nmx[0:M, s % 2:s % 2 + 1],
                                         accum_out=rsum[0:M, s % 2:s % 2 + 1]).then_inc(at_e, 1)

                def hi(n0, s, first):
                    i = ORDER[s % STEPS]
                    act.wait_ge(at_t, n0 + (s + 1))
                    if not (first and s < 2):
                        act.wait_ge(at_pv, n0 + (s - 1))
                    for kr, dst, src in turned(s, i, pth):
                        last = nc.scalar.activation(dst, src, ACT.Copy)
                    last.then_inc(at_hi, 1)

                def outs(n0, i, s, first):
                    st = s % STEPS
                    hp = (s % PAIR) // STEPS
                    if ORDER[st] == 8:
                        act.wait_ge(at_pv, n0 + (s + 1))
                        nc.scalar.activation(nh[64 * hp:64 * hp + 64, i, SEQ:T], ps[0:VD, 5, 0:DEC],
                                             ACT.Copy).then_inc(at_ohi, 1)
                    if st == STEPS - 1:
                        act.wait_ge(at_pv, n0 + (s + 1))
                        nc.scalar.activation(nh[64 * hp:64 * hp + 64, i, 0:SEQ],
                                             ps[0:VD, 6:8, :].rearrange("p a b -> p (a b)"),
                                             ACT.Copy).then_inc(at_ohi, 1)

                def pair(n0, i, first):
                    for s in range(PAIR):
                        exps(n0, s, first)
                        for lag, fn in ((T_LAG, "hi"), (PV_LAG, "outs")):
                            if s >= lag:
                                args = (n0, i, s - lag, first)
                            elif not first:
                                args = (n0 - PAIR, i - 1, s - lag + PAIR, False)
                            else:
                                continue
                            if fn == "hi":
                                hi(args[0], args[2], args[3])
                            else:
                                outs(*args)

                pair(base_n, 0, True)
                with act.Fori(1, H // 2) as i:
                    pair(i * PAIR + base_n, i, False)
                n0, i = base_n + (H // 2 - 1) * PAIR, H // 2 - 1
                for s in range(PAIR, PAIR + PV_LAG):
                    if s - T_LAG < PAIR:
                        hi(n0, s - T_LAG, False)
                    outs(n0, i, s - PV_LAG, False)

            attn_act(0)
            fence(act, "act", 3)

            def ffn_act(layer):
                f0 = layer * NF

                def tile(f, par, first):
                    for b in range(NB):
                        act.wait_ge(fg_rd, f * 3 + (3 * f0 + b + 1))
                        if not (first and layer == 0):
                            act.wait_ge(f_lo, f * 3 + (3 * f0 + b - 2))
                        nc.scalar.activation(sg[:, b, :], ps[:, b, 0:TB], ACT.Silu).then_inc(f_sg, 1)
                    for b in range(NB):
                        act.wait_ge(f_u, f * 3 + (3 * f0 + b + 1))
                        if not first:
                            if not (isinstance(f, int) and f + f0 < 2):
                                act.wait_ge(fd_rd, f * 24 + (24 * f0 - 24))
                        nc.scalar.activation(hh[:, par, b * TB:(b + 1) * TB], sg[:, b, :], ACT.Copy).then_inc(f_hi, 1)

                tile(0, 0, True)
                tile(1, 1, False)
                with act.Fori(1, NF // 2) as i:
                    for par in range(2):
                        tile(i * 2 + par, par, False)

            def tail_act(layer):
                s0 = 2 + 3 * layer
                name = ("oa", "ob")[layer]
                with act.Fori(0, 4) as i:
                    for s in range(2):
                        for b in range(NB):
                            g = GROUP0[name] + s * NB + b
                            take(i * 6 + g, bank(g), y[:, i * 2 + s, b * TB:(b + 1) * TB], P, TB)
                norms([(f"s{s0}", k, b) for k, b in CHAIN],
                      chain_waits([[(lin_ev, GROUP0[name] + 24)]] * NB))
                act.wait_ge(n_done, NORM_AT[f"s{s0}", "pre", 2] + 1)
                ffn_act(layer)
                norms([(f"s{s0 + 1}", k, b) for k, b in CHAIN],
                      chain_waits([[(f_acc, 24 * NF * (layer + 1))]] * NB))
                act.wait_ge(p_in, 16 * (layer + 1))
                nc.scalar.activation(ph[:], praw[:], ACT.Copy).then_inc(p_hi, 1)
                for m in range(8):
                    for b in range(NB):
                        g = GROUP0[f"pe{layer}"] + m * NB + b
                        take(g, bank(g), y[:, m, b * TB:(b + 1) * TB], P, TB)

                def gates(i, first):
                    for n in range(2 * NB):
                        g = GROUP0[f"pg{layer}"] + n
                        if not (first and n < 2):
                            act.wait_ge(g_mul, i * 6 + (24 * layer + n - 1))
                        take(i * 6 + g, bank(g), gt[:, n % 2, :], P, TB, ACT.Sigmoid)

                gates(0, True)
                with act.Fori(1, 4) as i:
                    gates(i, False)
                last = f"s{s0 + 2}"
                if layer == 0:
                    norms([(last, k, b) for k, b in CHAIN], chain_waits([[(g_mul, 24)]] * NB))
                else:
                    norms([(last, "post", b) for b in range(NB)], lambda key: [(g_mul, 48)])

            tail_act(0)
            fence(act, "act", 4)
            for m in range(2):
                act.wait_ge(st_out[m], 16 * (4 + KT + 8))
                for b in range(NB):
                    g = GROUP0["kb"] + m * NB + b
                    take(g, bank(g), stg[:, m, b * TB:(b + 1) * TB], P, TB)
            for b in range(NB):
                g = GROUP0["wf"] + b
                take(g, bank(g), fz[:, b * TB:(b + 1) * TB], H, TB, ACT.Identity,
                     bias=gains[0:H, GAIN_AT["bf"]:GAIN_AT["bf"] + 1])
            act.wait_ge(lin_ev, GROUP0["wf"] + NB)
            nc.scalar.activation(fe[:], fz[:], ACT.Abs).then_inc(fx_a, 1)
            act.wait_ge(fx_a, 1)
            nc.scalar.activation(fe[:], fe[:], ACT.Exp, scale=-1.0).then_inc(fx_a, 1)
            act.wait_ge(fx_v, 1)
            nc.scalar.activation(fl[:], fu[:], ACT.Ln).then_inc(fx_a, 1)
            for tt in range(9):
                rows = min(P, T - tt * P)
                act.wait_ge(st_out[tt % 2], 16 * (4 + KT + 8 + 1 + tt // 2))
                g = GROUP0["vb"] + tt
                take(g, bank(g), stg[0:rows, tt % 2, 0:KVH * HD], rows, KVH * HD)
            with act.Fori(0, 4) as i:
                for m in range(2):
                    act.wait_ge(st_out[m], i * 16 + 16 * (4 + KT + 8 + 1 + 5 - m))
                    for b in range(NB):
                        g = GROUP0["qb"] + m * NB + b
                        take(i * 6 + g, bank(g), stg[:, m, b * TB:(b + 1) * TB], P, TB, scale=FOX_SCALE)
            fence(act, "act", 5)
            attn_act(1)
            fence(act, "act", 6)
            tail_act(1)

        @block.vector
        def _(dve):
            V = nc.vector

            def norm(key):
                k = NORM_AT[key]
                s, kind, b = key
                c = slice(b * TB, (b + 1) * TB)
                src = {"pre": res[:, :, c], "post": y[:, :, c], "q": y[:, 0:4, c], "kv": y[:, 4:6, c]}[kind]
                K = {"q": 4, "kv": 2}.get(kind, KD)
                raw = sq[:, k % 2, 0:K, :]
                dve.wait_ge(n_rt, k + 1)
                V.reciprocal(rs[:, k % 2, :], rt[:, k % 2, :]).then_inc(n_rs, 1)
                dve.wait_ge(n_rs, k + 1)
                by = rs[:, k % 2, :].unsqueeze(1).to_broadcast((P, K, TB))
                if kind == "kv":
                    V.tensor_tensor(raw, src, by, ALU.mult).then_inc(kv_raw, 1)
                    dve.wait_ge(kv_raw, b + 1)
                    for j in range(K):
                        at_g = GAIN_AT["kv"] + j
                        last = V.tensor_scalar(y[:, 6 + j, c], sq[:, k % 2, j, :], gains[:, at_g:at_g + 1], None, ALU.mult)
                    last.then_inc(n_ap, 1)
                    raw = y[:, 6:8, c]
                else:
                    V.tensor_tensor(raw, src, by, ALU.mult).then_inc(n_ap, 1)
                if kind == "post":
                    dve.wait_ge(n_ap, k + 1)
                    for j in range(K):
                        at_g = GAIN_AT[POST_GAIN[s]] + j
                        last = V.scalar_tensor_tensor(res[:, j, c], sq[:, k % 2, j, :], gains[:, at_g:at_g + 1],
                                                      res[:, j, c], ALU.mult, ALU.add)
                    last.then_inc(n_done, 1)
                    return
                dve.wait_ge(n_hi, HI_COUNT[k])
                hi, lo = {"kv": (cvh[:, :, c], cvl[:, :, c]), "q": (nh[:, 0:4, c], nl[:, 0:4, c]),
                          "pre": (nh[:, :, c], nl[:, :, c])}[kind]
                V.tensor_tensor(lo, raw, hi.bitcast(F32), ALU.subtract).then_inc(n_done, 1)

            V.memset(epsc[:], EPS)
            V.memset(ones[:], 1.0).then_inc(ones_set, 1)
            for b in range(NB):
                norm(("s0", "pre", b))
            dve.wait_ge(const_in, 48)
            V.tensor_copy(ident_r[:], ident[:])
            V.tensor_copy(mask_r[:], y[:, 0, 0:2 * P].rearrange("p (a q) -> p a q", a=2)).then_inc(const_r, 1)
            dve.wait_ge(tab_in, 16)
            for b in range(NB):
                c = slice(b * TB, (b + 1) * TB)
                dve.wait_ge(lin_ev, GROUP0["kr"] + b + 1)
                V.tensor_tensor(y[0:ROPE, 6, c], y[0:ROPE, 6, c], krt[0:ROPE, c], ALU.mult)
                V.tensor_tensor(krf[:, c], y[ROPE:2 * ROPE, 6, c], krt[ROPE:2 * ROPE, c], ALU.mult).then_inc(kr_a, 1)
                dve.wait_ge(kr_a, b + 1)
                V.tensor_tensor(krf[:, c], krf[:, c], y[0:ROPE, 6, c], ALU.add).then_inc(kr_done, 1)
            dve.wait_ge(kr_done, NB)
            for kind in ("q", "kv"):
                for b in range(NB):
                    norm(("s1", kind, b))
            dve.wait_ge(cc_hi, 1)
            V.tensor_tensor(cvl[:, :, T:TK], cc[:], cvh[:, :, T:TK].bitcast(F32), ALU.subtract).then_inc(cc_lo, 1)
            fence(dve, "dve", 1)
            dve.wait_ge(tab_in, 32)
            with dve.Fori(0, 4) as i:
                for h in range(4):
                    for b in range(NB):
                        c = slice(b * TB, (b + 1) * TB)
                        dve.wait_ge(lin_ev, i * 12 + (GROUP0["uq"] + h * NB + b + 1))
                        V.tensor_tensor(stg[:, h % 2, c], stg[:, h % 2, c], cs[:, c], ALU.mult).then_inc(q_done, 1)
            fence(dve, "dve", 2)

            def attention(layer):
                base_n = layer * H * STEPS

                def neg_max(n0, s):
                    i = ORDER[s % STEPS]
                    M = P if i < 8 else DEC
                    n = (i + 1) * P if i < 8 else TK - SEQ
                    dve.wait_ge(at_s, n0 + (s + 1))
                    src = ps[0:M, 2 * (s % 2):2 * (s % 2) + 2, :].rearrange("p a b -> p (a b)")[:, 0:n]
                    V.tensor_reduce(nmx[0:M, s % 2:s % 2 + 1], src, AX.X, ALU.max, negate=True).then_inc(at_nm, 1)

                def normalise(n0, s):
                    i = ORDER[s % STEPS]
                    M = P if i < 8 else DEC
                    n = (i + 1) * P if i < 8 else TK - SEQ
                    dve.wait_ge(at_e, n0 + (s + 1))
                    V.reciprocal(rinv[0:M, s % 2:s % 2 + 1], rsum[0:M, s % 2:s % 2 + 1]).then_inc(at_r, 1)
                    dve.wait_ge(at_r, n0 + (s + 1))
                    V.tensor_scalar(pr[0:M, s % 3, 0:n], pr[0:M, s % 3, 0:n], rinv[0:M, s % 2:s % 2 + 1],
                                    None, ALU.mult).then_inc(at_p, 1)

                def lo(n0, s):
                    dve.wait_ge(at_hi, n0 + (s + 1))
                    i = ORDER[s % STEPS]
                    for (_, dst, src), (_, hi, _) in zip(turned(s, i, ptl), turned(s, i, pth)):
                        last = V.tensor_tensor(dst, src, hi.bitcast(F32), ALU.subtract)
                    last.then_inc(at_lo, 1)

                def outs(i, s):
                    st, hp = s % STEPS, (s % PAIR) // STEPS
                    r = slice(64 * hp, 64 * hp + 64)
                    sample = ORDER[st] == 8
                    if not sample and st != STEPS - 1:
                        return
                    dve.wait_ge(at_ohi, i * 4 + (layer * 2 * H + 2 * hp + (1 if sample else 2)))
                    if sample:
                        c, src = slice(SEQ, T), ps[0:VD, 5, 0:DEC]
                    else:
                        c, src = slice(0, SEQ), ps[0:VD, 6:8, :].rearrange("p a b -> p (a b)")
                    V.tensor_tensor(nl[r, i, c], src, nh[r, i, c].bitcast(F32), ALU.subtract).then_inc(at_olo, 1)

                def pair(n0, i, first):
                    for s in range(PAIR):
                        neg_max(n0, s)
                        for lag, fn in ((1, normalise), (T_LAG, lo), (PV_LAG, outs)):
                            if s >= lag:
                                args = (n0, i, s - lag)
                            elif not first:
                                args = (n0 - PAIR, i - 1, s - lag + PAIR)
                            else:
                                continue
                            if fn is outs:
                                outs(args[1], args[2])
                            else:
                                fn(args[0], args[2])

                pair(base_n, 0, True)
                with dve.Fori(1, H // 2) as i:
                    pair(i * PAIR + base_n, i, False)
                n0, i = base_n + (H // 2 - 1) * PAIR, H // 2 - 1
                for s in range(PAIR, PAIR + PV_LAG):
                    if s - 1 < PAIR:
                        normalise(n0, s - 1)
                    if s - T_LAG < PAIR:
                        lo(n0, s - T_LAG)
                    outs(i, s - PV_LAG)

            def ffn(layer):
                f0 = layer * NF
                events = sorted([(p, "down", d) for d, p in enumerate(D_AT)]
                                + [(72 + 24 * (b + 1), "mul", b) for b in range(NB)]
                                + [(108 + 21 * b, "lo", b) for b in range(NB)])

                def down(f, d, first):
                    m, b = d // NB, d % NB
                    c = slice(b * TB, (b + 1) * TB)
                    dve.wait_ge(fd_rd, f * 24 + (24 * f0 + d + 1))
                    if first:
                        V.tensor_copy(y[:, m, c], ps[:, 6 + d % 2, 0:TB]).then_inc(f_acc, 1)
                    else:
                        V.tensor_tensor(y[:, m, c], ps[:, 6 + d % 2, 0:TB], y[:, m, c], ALU.add).then_inc(f_acc, 1)

                def tile(f, par, first, second=False):
                    for _, what, x in events:
                        c = slice(x * TB, (x + 1) * TB)
                        if what == "down":
                            if not first:
                                down(f - 1, x, second)
                        elif what == "mul":
                            dve.wait_ge(f_sg, f * 3 + (3 * f0 + x + 1))
                            dve.wait_ge(fu_rd, f * 3 + (3 * f0 + x + 1))
                            V.tensor_tensor(sg[:, x, :], ps[:, 3 + x, 0:TB], sg[:, x, :], ALU.mult).then_inc(f_u, 1)
                        else:
                            dve.wait_ge(f_hi, f * 3 + (3 * f0 + x + 1))
                            V.tensor_tensor(hl[:, par, c], sg[:, x, :], hh[:, par, c].bitcast(F32),
                                            ALU.subtract).then_inc(f_lo, 1)

                tile(0, 0, True)
                tile(1, 1, False, True)
                with dve.Fori(1, NF // 2) as i:
                    for par in range(2):
                        tile(i * 2 + par, par, False)
                for d in range(24):
                    down(NF - 1, d, False)

            def tail(layer):
                s0 = 2 + 3 * layer
                for k, b in CHAIN:
                    norm((f"s{s0}", k, b))
                ffn(layer)
                for k, b in CHAIN:
                    norm((f"s{s0 + 1}", k, b))
                dve.wait_ge(p_hi, layer + 1)
                V.tensor_tensor(pl[:], praw[:], ph[:].bitcast(F32), ALU.subtract).then_inc(p_lo, 1)
                with dve.Fori(0, 4) as i:
                    for n in range(2 * NB):
                        c = slice((n % NB) * TB, (n % NB + 1) * TB)
                        dve.wait_ge(lin_ev, i * 6 + (GROUP0[f"pg{layer}"] + n + 1))
                        V.tensor_tensor(y[:, i * 2 + n // NB, c], gt[:, n % 2, :], y[:, i * 2 + n // NB, c],
                                        ALU.mult).then_inc(g_mul, 1)

            attention(0)
            fence(dve, "dve", 3)
            tail(0)
            for k, b in CHAIN:
                norm(("s4", k, b))
            fence(dve, "dve", 4)
            link = [0]

            def chained(ins):
                link[0] += 1
                ins.then_inc(fx_v, 1)
                dve.wait_ge(fx_v, link[0])

            dve.wait_ge(fx_a, 2)
            chained(V.tensor_scalar(fu[:], fe[:], 1.0, None, ALU.add))
            dve.wait_ge(fx_a, 3)
            chained(V.scalar_tensor_tensor(fe[:], fu[:], -1.0, fe[:], ALU.add, ALU.subtract))
            chained(V.reciprocal(fu[:], fu[:]))
            chained(V.tensor_tensor(fe[:], fe[:], fu[:], ALU.mult))
            chained(V.tensor_tensor(fl[:], fl[:], fe[:], ALU.subtract))
            chained(V.scalar_tensor_tensor(flog[:, 0:T], fz[:], 0.0, fl[:], ALU.min, ALU.subtract))
            dve.wait_ge(cache_in, 32)

            def scan(cols, initial):
                n = cols.stop - cols.start
                chained(V.tensor_tensor_scan(fcum[:, cols], ones[0:H, 0:1].to_broadcast((H, n)), flog[:, cols],
                                             initial, ALU.mult, ALU.add))

            scan(slice(T, TK), 0.0)
            scan(slice(0, SEQ), 0.0)
            scan(slice(SEQ, T), fcum[:, TK - 1:TK])
            chained(V.tensor_scalar(fcum[:], fcum[:], -1.0, None, ALU.mult))
            fence(dve, "dve", 5)
            attention(1)
            fence(dve, "dve", 6)
            tail(1)
            for b in range(NB):
                norm(("s7", "post", b))


def _weight_units(np, w):
    def cols(m, width=P):
        r, c = m.shape
        return m.reshape(r // P, P, c // width, width).transpose(2, 1, 0, 3).reshape(c // width, P, -1)

    def packed(tiles, n):
        t, p, c = tiles.shape
        return tiles.reshape(t // n, n, p, c).transpose(0, 2, 1, 3).reshape(t // n, p, n * c)

    def padded(m):
        out = np.zeros((m.shape[0], P), m.dtype)
        out[:, :m.shape[1]] = m
        return cols(out)

    def swapped(m):
        return np.concatenate([m[..., ROPE // 2:], m[..., :ROPE // 2]], -1)

    uq = w["w_uq"][0].reshape(Q_RANK, H, NOPE + ROPE)
    uq = np.concatenate([uq, swapped(uq[..., NOPE:])], -1).reshape(Q_RANK, H * P)
    kr = w["w_dkv"][0][:, KV_RANK:]

    def ffn(i):
        g, u = cols(w["w_gate"][i]), cols(w["w_up"][i])
        d = w["w_down"][i].reshape(NF, P, D)
        order = [g[0], u[0]]
        for f in range(NF - 1):
            order += [g[f + 1], d[f], u[f + 1]]
        return np.stack(order + [d[NF - 1]])

    def moving(m, per):
        r, c = m.shape
        return m.reshape(r // P // per, per, P, c).transpose(0, 2, 1, 3).reshape(-1, P, per * c)

    uv = w["w_uv"][0].reshape(KV_RANK, 2, H * VD // 2)
    parts = {
        "dq": cols(w["w_dq"][0]), "dkv": cols(w["w_dkv"][0][:, :KV_RANK]),
        "kr": padded(np.concatenate([kr, swapped(kr)], -1)),
        "uk": packed(cols(w["w_uk"][0].reshape(KV_RANK, H * NOPE)), 4),
        "uv": np.concatenate([moving(uv[:, h], 2) for h in range(2)]),
        "uq": packed(cols(uq), 2), "oa": cols(w["w_oa"][0]), "ffn0": ffn(0),
        "pe0": packed(cols(w["w_ple"][0]), 4), "pg0": cols(w["w_ple_gate"][0]),
        "kb": cols(w["w_kb"]), "wf": padded(w["w_f"]), "vb": moving(w["w_vb"], 4),
        "qb": cols(w["w_qb"][0]), "ob": cols(w["w_ob"][0]), "ffn1": ffn(1),
        "pe1": packed(cols(w["w_ple"][1]), 4), "pg1": cols(w["w_ple_gate"][1]),
    }
    for name, n, _ in LIN:
        assert parts[name].shape == (n, P, UW), (name, parts[name].shape)
    return np.concatenate([parts[name] for name, _, _ in LIN])


def _gain_table(np, w):
    def tiles(v):
        return v.reshape(-1, P).T

    def eight(v, places):
        out = np.zeros((P, 8), v.dtype)
        t = tiles(v)
        for j, k in enumerate(places):
            out[:, j] = t[:, k]
        return out

    every = range(8)
    bf = np.zeros((P, 8), w["b_f"].dtype)
    bf[:H, 0] = w["b_f"]
    cols = {"mix_pre0": eight(w["g_mix_pre"][0], every), "q": eight(w["g_q"][0], [0, 1, 2, 3] * 2),
            "mix_post0": eight(w["g_mix_post"][0], every), "ffn_pre0": eight(w["g_ffn_pre"][0], every),
            "ffn_post0": eight(w["g_ffn_post"][0], every), "ple_gate0": eight(w["g_ple_gate"][0], every),
            "ple_post0": eight(w["g_ple_post"][0], every), "shared": eight(w["g_shared"], every),
            "shared_v": eight(w["g_shared"], [0, 0, 1, 1, 2, 2, 3, 3]),
            "shared_v2": eight(w["g_shared"], [4, 4, 5, 5, 6, 6, 7, 7]),
            "mix_pre1": eight(w["g_mix_pre"][1], every), "mix_post1": eight(w["g_mix_post"][1], every),
            "ffn_pre1": eight(w["g_ffn_pre"][1], every), "ffn_post1": eight(w["g_ffn_post"][1], every),
            "ple_gate1": eight(w["g_ple_gate"][1], every), "ple_post1": eight(w["g_ple_post"][1], every),
            "kv": eight(w["g_kv"][0], range(2)), "bf": bf}
    return np.concatenate([cols[n] for n in GAINS], 1)


def _position_tables(np):
    half = ROPE // 2
    inv = np.power(np.float32(10000.0), -np.arange(half, dtype=np.float32) / half).astype(np.float32)
    pos = np.concatenate([np.arange(SEQ), PAST + np.arange(DEC)]).astype(np.float32)
    ang = (inv[:, None] * pos[None, :]).astype(np.float32)
    cos, sin = np.cos(ang).astype(np.float32), np.sin(ang).astype(np.float32)
    krt = np.concatenate([cos, cos, -sin, sin])
    scale = np.float32((NOPE + ROPE) ** -0.5)
    cs = np.concatenate([np.ones((NOPE, T), np.float32), krt]) * scale
    q, k = np.arange(P)[:, None], np.arange(P)[None, :]
    masks = np.zeros((P, 2, P), np.float32)
    masks[:, 0][k // 64 > q // 64] = NEG
    masks[:, 1][k > q] = NEG
    return krt, cs.astype(np.float32), masks.reshape(P, 2 * P), np.eye(P, dtype=np.float32)


def kernel(**w):
    import numpy as np
    import concourse.bacc as bacc
    from concourse.bass_utils import run_bass_kernel_spmd as run

    w = {k: np.asarray(v) for k, v in w.items()}
    krt, cs, masks, ident = _position_tables(np)
    c = np.ascontiguousarray
    x = np.concatenate([w["x_prompt"][0], w["x_sample"][0]])
    p = np.concatenate([w["p_prompt"][:, 0], w["p_sample"][:, 0]], 1)
    arrays = {
        "units": _weight_units(np, w), "gains": c(_gain_table(np, w)), "krt": krt, "cs": cs, "masks": masks,
        "ident": ident,
        "xT": c(x.reshape(T, KD, P).transpose(2, 1, 0)),
        "pT": c(p.reshape(2, T, 2, P).transpose(0, 3, 2, 1)),
        "cckvT": c(w["cache_ckv"][0, 0].reshape(PAST, 2, P).transpose(2, 1, 0)),
        "ckrT": c(w["cache_kr"][0, 0].T),
        "ckT": c(w["cache_k"][0].transpose(1, 2, 0)),
        "cv": c(w["cache_v"][0].reshape(PAST, KVH * HD)),
        "clfT": c(w["cache_logf"][0].T),
    }
    nc = bacc.Bacc("TRN2", target_bir_lowering=False, num_devices=1)
    io = {n: nc.dram_tensor(n, a.shape, F32, kind="ExternalInput").ap() for n, a in arrays.items()}

    def dram(name, shape, kind="Internal"):
        io[name] = nc.dram_tensor(name, shape, F32, kind=kind).ap()

    dram("yT", (P, KD, T), "ExternalOutput")
    dram("ckv_out", (P, 2, T), "ExternalOutput")
    dram("kr_out", (ROPE, T), "ExternalOutput")
    dram("kT_out", (KVH * HD, T), "ExternalOutput")
    dram("v_out", (T, KVH * HD), "ExternalOutput")
    dram("lf_out", (H, T), "ExternalOutput")
    dram("kA", (H * NOPE, TK))
    dram("vA", (TK, H * VD))
    dram("qA", (H, P, T))
    dram("qBm", (D, T))
    dram("nck_all", (H, TK))
    full = (KT - 1) * P
    io["kA_h"] = io["kA"].rearrange("(h d) t -> h d t", d=NOPE)
    io["vA_full"] = io["vA"][0:full, :].rearrange("(t p) (h d) -> h p t d", p=P, d=VD)
    io["vA_last"] = io["vA"][full:TK, :].rearrange("p (h d) -> h p d", d=VD)
    io["qB"] = io["qBm"].rearrange("(h d) t -> h d t", d=HD)
    io["qB_pair"] = io["qBm"].rearrange("(m p) t -> m p t", p=P)
    io["nck"] = io["nck_all"].rearrange("(h o) t -> h o t", o=1)
    io["kT_h"] = io["kT_out"].rearrange("(h d) t -> h d t", d=HD)
    io["v_full"] = io["v_out"][0:SEQ, :].rearrange("(t p) (h d) -> h p t d", p=P, d=HD)
    io["v_new"] = io["v_out"][SEQ:T, :].rearrange("p (h d) -> h p d", d=HD)
    cv = io["cv"].rearrange("p (h d) -> h p d", d=HD)
    n0 = P - DEC
    io["cv0"], io["cv1"], io["cv2"] = cv[:, 0:n0, :], cv[:, n0:n0 + P, :], cv[:, n0 + P:PAST, :]
    build_program(nc, io)
    r = run(nc, [arrays], core_ids=[0]).results[0]

    def rows(a):
        a = c(a.T)
        return a[None, :SEQ], a[None, SEQ:]

    y_p, y_s = rows(r["yT"].transpose(1, 0, 2).reshape(D, T))
    ckv_p, ckv_s = rows(r["ckv_out"].transpose(1, 0, 2).reshape(KV_RANK, T))
    kr_p, kr_s = rows(r["kr_out"])
    k_p, k_s = rows(r["kT_out"])
    lf_p, lf_s = rows(r["lf_out"])
    v = r["v_out"].reshape(T, KVH, HD)
    return (y_p, y_s, ckv_p[None], kr_p[None], k_p.reshape(1, SEQ, KVH, HD), v[None, :SEQ], lf_p,
            ckv_s[None], kr_s[None], k_s.reshape(1, DEC, KVH, HD), v[None, SEQ:], lf_s)
```

```python
from contextlib import ExitStack

import concourse.bass as bass
from concourse import mybir

F32 = mybir.dt.float32
F32R = mybir.dt.float32r
ACT = mybir.ActivationFunctionType
ALU = mybir.AluOpType
AX = mybir.AxisListType

P = 128
D = 1024
KD = D // P
SEQ, DEC, PAST = 1024, 32, 256
T = SEQ + DEC
TK = T + PAST
NB = 3
TB = T // NB
KB = 4
TKB = TK // KB
KT = (TK + P - 1) // P
H = 16
Q_RANK, KV_RANK, NOPE, ROPE, VD = 512, 256, 64, 32, 64
KVH, HD = 4, 64
PLE = 256
F = 2816
NF = F // P
EPS = 1e-6
NEG = -1e30
FOX_SCALE = HD ** -0.5
UW = 1024

LIN = [("dq", 4, "mix_pre0"), ("dkv", 2, "mix_pre0"), ("kr", 1, "mix_pre0"), ("uk", 2, None),
       ("uv", 2, None), ("uq", 8, "q"), ("oa", 8, None), ("ffn0", 3 * NF, "ffn_pre0"),
       ("pe0", 2, None), ("pg0", 8, "ple_gate0"),
       ("kb", 2, "shared"), ("wf", 1, "shared"), ("vb", 2, "shared_v"), ("qb", 8, "mix_pre1"),
       ("ob", 8, None), ("ffn1", 3 * NF, "ffn_pre1"), ("pe1", 2, None), ("pg1", 8, "ple_gate1")]
GAINS = ["mix_pre0", "q", "mix_post0", "ffn_pre0", "ffn_post0", "ple_gate0", "ple_post0", "shared",
         "shared_v", "shared_v2", "mix_pre1", "mix_post1", "ffn_pre1", "ffn_post1", "ple_gate1",
         "ple_post1", "kv", "bf"]
GAIN_AT = {name: 8 * i for i, name in enumerate(GAINS)}


BLOCKWISE = ("oa", "pg0", "ob", "pg1")


def slot_of(name, u):
    if name.startswith("ffn"):
        return u % 3
    return (0, 1, 0, 1, 0, 1, 2, 0)[u] if name in BLOCKWISE else u % 2


def unit_places():
    first, used, gained, uses = {}, {}, {}, {}
    at, use, gain = 0, [0, 0, 0], [0, 0, 0]
    for name, n, g in LIN:
        first[name], used[name], gained[name] = at, list(use), list(gain)
        at += n
        for u in range(n):
            s = slot_of(name, u)
            uses[name, u] = s, use[s], gain[s]
            use[s] += 1
            if g is not None and not (name.startswith("ffn") and s == 2):
                gain[s] += 1
    return first, used, gained, at, uses


UNIT0, USED, GAINED, UNITS, USES = unit_places()

GROUPS = [("dq", 12), ("dkv", 6), ("kr", 3), ("uk", 8 * KB), ("uv", 2 * KT), ("uq", 48), ("oa", 24),
          ("pe0", 24), ("pg0", 24), ("kb", 6), ("wf", 3), ("vb", 9), ("qb", 24), ("ob", 24),
          ("pe1", 24), ("pg1", 24)]
GROUP0 = {}
_at = 0
for _n, _c in GROUPS:
    GROUP0[_n] = _at
    _at += _c
LBANKS = 6

CHAIN = [("post", 0), ("post", 1), ("pre", 0), ("post", 2), ("pre", 1), ("pre", 2)]
NORMS = ([("s0", "pre", b) for b in range(NB)] + [("s1", "q", b) for b in range(NB)]
         + [("s1", "kv", b) for b in range(NB)]
         + [(s, k, b) for s in ("s2", "s3", "s4", "s5", "s6") for k, b in CHAIN]
         + [("s7", "post", b) for b in range(NB)])
NORM_AT = {n: i for i, n in enumerate(NORMS)}
POST_GAIN = {"s2": "mix_post0", "s3": "ffn_post0", "s4": "ple_post0", "s5": "mix_post1",
             "s6": "ffn_post1", "s7": "ple_post1"}

ORDER = [7, 6, 0, 1, 5, 4, 2, 8, 3]
STEPS = len(ORDER)
PAIR = 2 * STEPS
T_LAG = 3
PV_LAG, OUT_LAG = 2, 3
CHUNKS = []
for _s in range(PAIR):
    _i = ORDER[_s % STEPS]
    _n = 3 if _i == 8 else _i + 1
    CHUNKS += [(_s, _i, _k, min(4, _n - _k)) for _k in range(0, _n, 4)]
HC = len(CHUNKS) // 2
KEYS = [(_i + 1) * P for _i in range(8)] + [DEC + PAST]
S_BANK = {7: 0, 6: 2, 0: 0, 1: 1, 5: 2, 4: 0, 2: 2, 8: 3, 3: 2}
PROB_AT = {_i: sum(KEYS[:_i]) for _i in range(9)}
OUT_PARTS = sorted([(4, 5, 6, 7), (8,), (0, 1, 2, 3)], key=lambda _t: max(ORDER.index(_i) for _i in _t))
OUT_AFTER = {max(_t, key=ORDER.index): _p for _p, _t in enumerate(OUT_PARTS)}
PART_OF = {_i: _p for _p, _t in enumerate(OUT_PARTS) for _i in _t}


def score_banks(s):
    i = ORDER[s % STEPS]
    return range(S_BANK[i], S_BANK[i] + (KEYS[i] + 511) // 512)


def banks_before(s):
    return next(t for t in range(s - 1, s - STEPS - 1, -1) if set(score_banks(t)) & set(score_banks(s)))


def part_needed(tile, hp):
    if tile != min(OUT_PARTS[PART_OF[tile]], key=ORDER.index):
        return None
    return (3 * hp + PART_OF[4] + 1 if tile == 8
            else 3 * (hp - 1) + (PART_OF[8] if tile > 3 else PART_OF[0]) + 1)




def chunk(c):
    s, i, k0, n = CHUNKS[c % (2 * HC)]
    last = k0 + n == (3 if i == 8 else i + 1)
    return s + c // (2 * HC) * PAIR, i, k0, n, last


def chunks_of(s):
    at = s // PAIR * 2 * HC
    return [at + c for c, x in enumerate(CHUNKS) if x[0] == s % PAIR]


D_AT = [16 + (9 * d) // 2 for d in range(24)]


PER_UNIT = {"dq": 3, "dkv": 3, "kr": 3, "uk": 4 * KB, "uv": KT, "uq": 6, "oa": 3, "pe0": 12, "pg0": 3,
            "kb": 3, "wf": 3, "vb": 9, "qb": 3, "ob": 3, "pe1": 12, "pg1": 3}


def group_place(n):
    return (n // NB, n % NB) if n < 5 * NB else (5 + n % NB, n // NB - 5)


def group_after(name, slot, j):
    if name == "vb":
        return GROUP0[name] + 9
    return j * (2 * PER_UNIT[name]) + (GROUP0[name] + PER_UNIT[name] * (slot + 1))


HI_COUNT = [sum(n[1] != "post" for n in NORMS[:k + 1]) for k in range(len(NORMS))]


POST_COUNT = [k + 1 - HI_COUNT[k] for k in range(len(NORMS))]


def build_program(nc, io):
    with ExitStack() as ctx:
        base = (nc.sbuf_base + 31) // 32 * 32
        end = nc.sbuf_usable_end

        def at(name, shape, dt, offset):
            n = 4
            for x in shape[1:]:
                n *= x
            n = (n + 31) // 32 * 32
            assert base + offset + n <= end, (name, base + offset + n - end)
            return nc.alloc_sbuf_tensor_at(name, shape, dt, offset=base + offset), offset + n

        res, o = at("residual", [P, KD, T], F32, 0)
        n_off = o
        nh, o = at("act_hi", [P, KD, T], F32R, o)
        nl, o = at("act_lo", [P, KD, T], F32R, o)
        cvh, _ = at("latent_hi", [P, 2, TK], F32R, n_off + 4 * T * 4)
        cvl, _ = at("latent_lo", [P, 2, TK], F32R, n_off + KD * T * 4 + 4 * T * 4)
        wraw, o = at("weight_raw", [P, 3, UW], F32, o)
        attn_off = o
        wh, o = at("weight_hi", [P, 3, UW], F32R, o)
        wl, o = at("weight_lo", [P, 3, UW], F32R, o)
        y, o = at("sublayer_out", [P, KD, T], F32, o)
        scr = o
        NGC = 8 * len(GAINS)
        const_bytes = 4 * (NGC + P + P + P + 2 * P + 8)
        o = (end - base - const_bytes) // 32 * 32
        top = o
        gains, o = at("gains", [P, NGC], F32, o)
        ones, o = at("ones", [P, P], F32, o)
        ident, o = at("ident", [P, P], F32, o)
        ident_r, o = at("ident_r", [P, P], F32R, o)
        mask_r, o = at("mask_r", [P, 2, P], F32R, o)
        epsc, o = at("eps_col", [P, 8], F32, o)
        sq, o = at("squares", [P, 2, KD, TB], F32, scr)
        rt, o = at("root", [P, 2, TB], F32, o)
        rs, o = at("rstd", [P, 2, TB], F32, o)
        norm_end = o
        stg, o = at("stage", [P, 2, TK], F32, scr)
        cs, o = at("rope_table", [P, T], F32, o)
        assert o <= top
        cc, o = at("cached_latent", [P, 2, PAST], F32, scr + 4 * (2 * KD * TB + 4 * TB))
        krf, o = at("rope_key", [ROPE, T], F32, o)
        assert o <= top
        krt, _ = at("rope_table_k", [2 * ROPE, T], F32, scr - 4 * T)
        sg, o = at("ffn_act", [P, NB, TB], F32, scr)
        hh0, o = at("ffn_hi_even", [P, T], F32R, o)
        hl0, o = at("ffn_lo_even", [P, T], F32R, o)
        hh1, o = at("ffn_hi_odd", [P, T], F32R, norm_end)
        hl1, o = at("ffn_lo_odd", [P, T], F32R, o)
        assert o <= top
        hh, hl = (hh0, hh1), (hl0, hl1)
        pl, _ = at("ple_lo", [P, 2, T], F32R, scr)
        gt, _ = at("gate", [P, 2, TB], F32, norm_end)
        assert NORM_AT["s3", "pre", 2] % 2 == NORM_AT["s6", "pre", 2] % 2 == 0
        ph, o = at("ple_hi", [P, 2, T], F32R, scr + 4 * KD * TB)
        praw, o = at("ple_raw", [P, 2, T], F32, norm_end)
        assert o <= top
        yo = scr - 4 * KD * T
        fz, o = at("forget_z", [H, T], F32, yo)
        fe, o = at("forget_e", [H, T], F32, o)
        fu, o = at("forget_u", [H, T], F32, o)
        fl, o = at("forget_l", [H, T], F32, o)
        flog, o = at("forget_log", [H, TK], F32, o)
        fcum, o = at("forget_cum", [H, TK], F32, o)
        qh, o = at("q_hi", [P, 2, T], F32R, attn_off)
        ql, o = at("q_lo", [P, 2, T], F32R, o)
        kh, o = at("k_hi", [P, 2, TK], F32R, o)
        kl, o = at("k_lo", [P, 2, TK], F32R, o)
        vh, o = at("v_hi", [P, 2, KT, VD], F32R, o)
        vl, o = at("v_lo", [P, 2, KT, VD], F32R, o)
        pr, o = at("probs", [P, sum(KEYS)], F32, o)
        pth, o = at("probs_t_hi", [P, 2, 4, P], F32R, o)
        ptl, o = at("probs_t_lo", [P, 2, 4, P], F32R, o)
        nmx, o = at("neg_max", [P, STEPS], F32, o)
        rsum, o = at("row_sum", [P, STEPS], F32, o)
        rinv, o = at("row_inv", [P, STEPS], F32, o)
        assert o <= top
        rawoff = attn_off - 3 * UW * 4
        qraw, o = at("q_raw", [P, T], F32, rawoff)
        kraw, o = at("k_raw", [P, TK], F32, o)
        vraw, o = at("v_raw", [P, KT, VD], F32, o)
        assert o == attn_off

        ps = ctx.enter_context(nc.psum_tensor("ps", [P, 8, 512], F32))

        def sem(name):
            return ctx.enter_context(nc.semaphore(name))

        const_in = sem("const_in")
        ones_set = sem("ones_set")
        const_r = sem("const_r")
        x_in = [sem(f"x_in{b}") for b in range(NB)]
        w_raw = [sem(f"w_raw{s}") for s in range(3)]
        w_gain = [sem(f"w_gain{s}") for s in range(3)]
        w_hi = [sem(f"w_hi{s}") for s in range(3)]
        w_rdy = [sem(f"w_rdy{s}") for s in range(3)]
        lin_rd = sem("lin_rd")
        lin_ev = sem("lin_ev")
        n_sq, n_mm, n_rt = sem("norm_squares"), sem("norm_sum"), sem("norm_root")
        n_rs, n_ap, n_hi, n_done = sem("norm_rstd"), sem("norm_applied"), sem("norm_hi"), sem("norm_done")
        r_done = sem("residual_done")
        kv_raw = sem("kv_raw")
        tab_in, cache_in, p_in = sem("tab_in"), sem("cache_in"), sem("p_in")
        cc_hi, cc_lo = sem("cc_hi"), sem("cc_lo")
        q_raw = sem("q_raw")
        kr_a, kr_done = sem("kr_products"), sem("kr_done")
        q_done = sem("q_done")
        st_out = [sem("st_out0"), sem("st_out1")]
        ckv_out, kr_out, lf_out, nck_out, y_out = (sem("ckv_out"), sem("kr_out"), sem("lf_out"),
                                                   sem("nck_out"), sem("y_out"))
        fg_rd, fu_rd, fd_rd = sem("ffn_gate_rd"), sem("ffn_up_rd"), sem("ffn_down_rd")
        f_sg, f_u, f_hi, f_lo, f_acc = (sem("ffn_silu"), sem("ffn_mul"), sem("ffn_hi_done"),
                                        sem("ffn_lo_done"), sem("ffn_acc"))
        p_hi, p_lo, g_mul = sem("ple_hi_done"), sem("ple_lo_done"), sem("gate_mul")
        fx_a, fx_v = sem("forget_act"), sem("forget_dve")
        at_raw, at_khi, at_split = sem("at_raw"), sem("at_split_hi"), sem("at_split")
        at_kr, at_fix = sem("at_kr"), sem("at_fixed_rows")
        at_s, at_t, at_pv = sem("at_scores"), sem("at_turned"), sem("at_pv")
        at_nm, at_r, at_p, at_lo, at_olo = (sem("at_negmax"), sem("at_rinv"), sem("at_probs"),
                                            sem("at_pt_lo"), sem("at_o_lo"))
        at_e, at_hi, at_ohi = sem("at_exp"), sem("at_pt_hi"), sem("at_o_hi")
        fences = {e: sem(f"fence_{e}") for e in ("pe", "act", "dve", "pool", "sp")}

        def fence(eng, me, n):
            eng.drain().then_inc(fences[me], 1)
            for e, s in fences.items():
                if e != me:
                    eng.wait_ge(s, n)

        def bank(g):
            return g % LBANKS

        kA, vA, qA, qB, nck = io["kA"], io["vA"], io["qA"], io["qB"], io["nck"]

        def turned(c, buf):
            _, i, _, n, _ = chunk(c)
            v = ps[:, 4 + c % 2, :].rearrange("p (t q) -> p t q", q=P)
            if i < 8:
                return [(buf[:, c % 2, 0:n, :], v[:, 0:n, :])]
            return [(buf[:, c % 2, 0:2, 0:DEC], v[:, 0:2, 0:DEC]), (buf[0:DEC, c % 2, 2, 0:DEC], v[0:DEC, 2, 0:DEC])]

        def out_part(c, i, buf):
            _, tile, _, _, last = chunk(c)
            hp = c // HC
            rows = slice(64 * (hp % 2), 64 * (hp % 2) + 64)
            pair = i + (-1 if c < 0 else 0)
            part = OUT_AFTER[tile]
            cols, src = ((slice(SEQ, T), ps[0:VD, 7, 0:DEC]) if tile == 8 else
                         (slice(512, SEQ), ps[0:VD, 7, :]) if tile > 3 else (slice(0, 512), ps[0:VD, 6, :]))
            return buf[rows, pair, cols], src, 3 * hp + part + 1

        def score_tile(tile):
            M = P if tile < 8 else DEC
            return ps[0:M, 0:4, :].rearrange("p a b -> p (a b)")[:, 512 * S_BANK[tile]:512 * S_BANK[tile] + KEYS[tile]]

        def is_out(c):
            return chunk(c)[4] and chunk(c)[1] in OUT_AFTER

        block = ctx.enter_context(nc.Block())

        @block.sync
        def _(sp):
            def load_unit(name, slot, use, unit):
                if not (isinstance(use, int) and use == 0):
                    sp.wait_ge(w_rdy[slot], use)
                sp.dma_start(wraw[:, slot, :], io["units"][unit]).then_inc(w_raw[slot], 16)

            def lin_load(name, j):
                slot, use, _ = USES[name, j]
                load_unit(name, slot, use, UNIT0[name] + j)

            def lin_load_pair(name, i):
                for s in range(2):
                    load_unit(name, s, i + USED[name][s], i * 2 + (UNIT0[name] + s))

            sp.dma_start(gains[:], io["gains"]).then_inc(const_in, 16)
            sp.dma_start(ident[:], io["ident"]).then_inc(const_in, 16)
            for b in range(NB):
                sp.dma_start(res[:, :, b * TB:(b + 1) * TB], io["xT"][:, :, b * TB:(b + 1) * TB]).then_inc(x_in[b], 16)
                if b == 0:
                    lin_load("dq", 0)
                    lin_load("dq", 1)
            sp.dma_start(wraw[:, 2, 0:2 * P], io["masks"]).then_inc(const_in, 16)
            sp.dma_start(cc[:], io["cckvT"]).then_inc(cache_in, 16)
            lin_load("dq", 2)
            lin_load("dq", 3)
            for name in ("dkv", "kr"):
                for j in range(dict((n, c) for n, c, _ in LIN)[name]):
                    lin_load(name, j)
            sp.wait_ge(n_done, NB)
            sp.dma_start(krt[:], io["krt"]).then_inc(tab_in, 16)
            lin_load("uk", 0)
            lin_load("uk", 1)
            sp.wait_ge(kr_done, NB)
            sp.dma_start(io["kr_out"], krf[:]).then_inc(kr_out, 16)
            sp.wait_ge(n_ap, NORM_AT["s1", "kv", 2] + 1)
            sp.dma_start(io["ckv_out"], y[:, 6:8, :]).then_inc(ckv_out, 16)
            fence(sp, "sp", 1)
            sp.dma_start(cs[:], io["cs"]).then_inc(tab_in, 16)

            def store(slot, dst, src, waits, count=1):
                for s, v in waits:
                    sp.wait_ge(s, v)
                sp.dma_start(dst, src).then_inc(st_out[slot], 16)

            for m in range(8):
                if m < 2:
                    lin_load("uv", m)
                store(m % 2, kA[m * P:(m + 1) * P, :], stg[:, m % 2, :], [(lin_ev, GROUP0["uk"] + KB * (m + 1))])
            lin_load("uq", 0)
            lin_load("uq", 1)
            for g in range(2 * KT):
                half, kt = g // KT, g % KT
                rows = min(P, TK - kt * P)
                store(g % 2, vA[kt * P:kt * P + rows, half * 512:(half + 1) * 512], stg[0:rows, g % 2, 0:512],
                      [(lin_ev, GROUP0["uv"] + g + 1)])
            with sp.Fori(0, 3) as i:
                for s in range(2):
                    load_unit("uq", s, i + (USED["uq"][s] + 1), i * 2 + (UNIT0["uq"] + 2 + s))
                for h in range(4):
                    sp.wait_ge(q_done, i * 12 + NB * (h + 1))
                    sp.dma_start(qA[i * 4 + h], stg[:, h % 2, 0:T]).then_inc(st_out[h % 2], 16)
            for h in range(4):
                sp.wait_ge(q_done, 36 + NB * (h + 1))
                sp.dma_start(qA[12 + h], stg[:, h % 2, 0:T]).then_inc(st_out[h % 2], 16)
            for s in range(2):
                sp.wait_ge(st_out[s], 16 * (4 + KT + 8))
            sp.wait_ge(ckv_out, 16)
            sp.wait_ge(kr_out, 16)
            fence(sp, "sp", 2)

            def attn_loads(layer, h, first):
                if not first:
                    sp.wait_ge(at_split, h + layer * H)
                n = 0
                if layer == 0:
                    sp.dma_start(qraw[:], qA[h]).then_inc(at_raw, 16)
                    sp.dma_start(kraw[0:NOPE, :], io["kA_h"][h]).then_inc(at_raw, 16)
                    sp.dma_start(vraw[:, 0:KT - 1, :], io["vA_full"][h]).then_inc(at_raw, 16)
                    sp.dma_start(vraw[0:TK % P, KT - 1, :], io["vA_last"][h]).then_inc(at_raw, 16)
                else:
                    sp.dma_start(qraw[0:HD, :], qB[h]).then_inc(at_raw, 16)
                    sp.dma_start(kraw[HD:HD + 1, :], nck[h]).then_inc(at_raw, 16)

            def attn_loads_kv(kv):
                sp.dma_start(kraw[0:HD, 0:T], io["kT_h"][kv]).then_inc(at_raw, 16)
                sp.dma_start(kraw[0:HD, T:TK], io["ckT"][kv]).then_inc(at_raw, 16)
                sp.dma_start(vraw[:, 0:8, :], io["v_full"][kv]).then_inc(at_raw, 16)
                sp.dma_start(vraw[0:DEC, 8, :], io["v_new"][kv]).then_inc(at_raw, 16)
                sp.dma_start(vraw[DEC:P, 8, :], io["cv0"][kv]).then_inc(at_raw, 16)
                sp.dma_start(vraw[:, 9, :], io["cv1"][kv]).then_inc(at_raw, 16)
                sp.dma_start(vraw[0:DEC, 10, :], io["cv2"][kv]).then_inc(at_raw, 16)

            for r in range(2):
                rows = slice(NOPE + r * ROPE, NOPE + (r + 1) * ROPE)
                sp.dma_start(kraw[rows, 0:T], io["kr_out"]).then_inc(at_kr, 16)
                sp.dma_start(kraw[rows, T:TK], io["ckrT"]).then_inc(at_kr, 16)
            attn_loads(0, 0, True)
            with sp.Fori(1, H) as h:
                attn_loads(0, h, False)
            fence(sp, "sp", 3)

            def blockwise_loads(name):
                with sp.Fori(0, 2) as i:
                    lin_load_pair(name, i)
                for j in range(4, 8):
                    lin_load(name, j)

            def tail_loads(layer):
                blockwise_loads(("oa", "ob")[layer])
                name = f"ffn{layer}"
                u0 = UNIT0[name]
                for s in range(2):
                    load_unit(name, s, USED[name][s], u0 + s)
                with sp.Fori(0, NF - 1) as f:
                    for k, (s, df) in enumerate(((0, 1), (2, 0), (1, 1))):
                        load_unit(name, s, f + (USED[name][s] + df), f * 3 + (u0 + 2 + k))
                load_unit(name, 2, USED[name][2] + NF - 1, u0 + 3 * NF - 1)
                for j in range(2):
                    lin_load(f"pe{layer}", j)
                sp.wait_ge(fd_rd, 24 * NF * (layer + 1))
                sp.dma_start(praw[:], io["pT"][layer]).then_inc(p_in, 16)
                blockwise_loads(f"pg{layer}")

            tail_loads(0)

            for j in range(2):
                lin_load("kb", j)
            fence(sp, "sp", 4)
            for name, j in (("wf", 0), ("vb", 0), ("vb", 1)):
                lin_load(name, j)
            sp.dma_start(flog[:, T:TK], io["clfT"]).then_inc(cache_in, 16)
            for m in range(2):
                store(m, io["kT_out"][m * P:(m + 1) * P, :], stg[:, m, 0:T], [(lin_ev, GROUP0["kb"] + NB * (m + 1))])
            for tt in range(9):
                rows = min(P, T - tt * P)
                store(tt % 2, io["v_out"][tt * P:tt * P + rows, :], stg[0:rows, tt % 2, 0:KVH * HD],
                      [(lin_ev, GROUP0["vb"] + tt + 1)])
            sp.wait_ge(fx_v, 6)
            sp.dma_start(io["lf_out"], flog[:, 0:T]).then_inc(lf_out, 16)
            sp.wait_ge(fx_v, 10)
            sp.dma_start(io["nck_all"], fcum[:]).then_inc(nck_out, 16)
            with sp.Fori(0, 4) as i:
                lin_load_pair("qb", i)
                for m in range(2):
                    sp.wait_ge(lin_ev, i * 6 + (GROUP0["qb"] + NB * (m + 1)))
                    sp.dma_start(io["qB_pair"][i * 2 + m], stg[:, m, 0:T]).then_inc(st_out[m], 16)
            for s in range(2):
                sp.wait_ge(st_out[s], 16 * (4 + KT + 8 + 1 + (5 - s) + 4))
            sp.wait_ge(lf_out, 16)
            sp.wait_ge(nck_out, 16)
            fence(sp, "sp", 5)
            for h in range(4):
                if h:
                    sp.wait_ge(at_split, H + h)
                attn_loads_kv(0)
                attn_loads(1, h, True)
            with sp.Fori(1, KVH) as kv:
                for g in range(4):
                    sp.wait_ge(at_split, kv * 4 + (H + g))
                    attn_loads_kv(kv)
                    attn_loads(1, kv * 4 + g, True)
            fence(sp, "sp", 6)
            tail_loads(1)
            for b in range(NB):
                sp.wait_ge(r_done, POST_COUNT[NORM_AT["s7", "post", b]])
                sp.dma_start(io["yT"][:, :, b * TB:(b + 1) * TB], res[:, :, b * TB:(b + 1) * TB]).then_inc(y_out, 16)
            sp.wait_ge(y_out, 16 * NB)

        @block.gpsimd
        def _(pool):
            LAST = {}

            def split(slot, use, gain, gained=None, free=None):
                raw = wraw[:, slot, :]
                pool.wait_ge(w_raw[slot], use * 16 + 16)
                if gain is not None:
                    g = gains[:, GAIN_AT[gain]:GAIN_AT[gain] + 8].unsqueeze(2).to_broadcast((P, 8, P))
                    raw8 = raw.rearrange("p (k m) -> p k m", k=8)
                    pool.tensor_tensor(raw8, raw8, g, ALU.mult).then_inc(w_gain[slot], 1)
                    pool.wait_ge(w_gain[slot], gained + 1)
                if free is not None:
                    pool.wait_ge(*free)
                pool.tensor_tensor(wh[:, slot, :], raw, ones[:, 0:1].to_broadcast((P, UW)), ALU.mult).then_inc(w_hi[slot], 1)
                pool.wait_ge(w_hi[slot], use + 1)
                pool.tensor_tensor(wl[:, slot, :], raw, wh[:, slot, :].bitcast(F32), ALU.subtract).then_inc(w_rdy[slot], 1)

            def lin_split(name, j, gain):
                s = j % 2
                split(s, USED[name][s] + j // 2, gain, GAINED[name][s] + j // 2, LAST.get(s))
                LAST[s] = (lin_rd, group_after(name, s, j // 2))

            def blockwise_splits(name, gain):
                for j in range(8):
                    slot, use, gained = USES[name, j]
                    split(slot, use, gain, gained, LAST.get(slot))
                    done = NB * (j + 1) if j < 5 else 5 * NB + 2 * NB + (j - 5) + 1
                    LAST[slot] = (lin_rd, GROUP0[name] + done)

            def lin_split_loop(name, gain, n=4):
                for s in range(2):
                    split(s, USED[name][s], gain, GAINED[name][s], LAST.get(s))
                with pool.Fori(1, n) as i:
                    for s in range(2):
                        split(s, i + USED[name][s], gain, i + GAINED[name][s],
                              (lin_rd, (i - 1) * (2 * PER_UNIT[name]) + group_after(name, s, 0)))
                for s in range(2):
                    LAST[s] = (lin_rd, group_after(name, s, n - 1))

            def attn_split(layer, parity, h, first):
                pool.wait_ge(at_raw, h * 64 + 64 if layer == 0 else h * 144 + (16 * 4 * H - 144 * H + 144))
                if not first:
                    pool.wait_ge(at_pv, h * HC - HC)
                krows = NOPE if layer == 0 else HD + 1
                qrows = P if layer == 0 else HD
                parts = [(qh[0:qrows, parity, :], ql[0:qrows, parity, :], qraw[0:qrows, :], qrows, T),
                         (kh[0:krows, parity, :], kl[0:krows, parity, :], kraw[0:krows, :], krows, TK),
                         (vh[:, parity, 0:KT - 1, :], vl[:, parity, 0:KT - 1, :], vraw[:, 0:KT - 1, :], P, 0),
                         (vh[0:TK % P, parity, KT - 1, :], vl[0:TK % P, parity, KT - 1, :],
                          vraw[0:TK % P, KT - 1, :], TK % P, VD)]
                for hi, lo, raw, rows, n in parts:
                    one = (ones[0:rows, 0:1].to_broadcast((rows, n)) if n else
                           ones[:, 0:1].unsqueeze(2).to_broadcast((P, KT - 1, VD)))
                    last = pool.tensor_tensor(hi, raw, one, ALU.mult)
                last.then_inc(at_khi, 1)
                pool.wait_ge(at_khi, h + 1)
                for hi, lo, raw, rows, n in parts:
                    last = pool.tensor_tensor(lo, raw, hi.bitcast(F32), ALU.subtract)
                last.then_inc(at_split, 1)

            pool.wait_ge(const_in, 48)
            pool.wait_ge(ones_set, 1)
            for j in range(4):
                lin_split("dq", j, "mix_pre0")
            for j in range(2):
                lin_split("dkv", j, "mix_pre0")
            lin_split("kr", 0, "mix_pre0")
            for j in range(2):
                lin_split("uk", j, None)
            fence(pool, "pool", 1)
            for j in range(2):
                lin_split("uv", j, None)
            lin_split_loop("uq", "q")
            fence(pool, "pool", 2)

            pool.wait_ge(at_kr, 64)
            rows = slice(NOPE, P)
            for r in (slice(64, 96), slice(96, 128)):
                for b in range(2):
                    last = pool.tensor_tensor(kh[r, b, :], kraw[r, :], ones[r, 0:1].to_broadcast((ROPE, TK)), ALU.mult)
            last.then_inc(at_fix, 1)
            pool.wait_ge(at_fix, 1)
            for r in (slice(64, 96), slice(96, 128)):
                for b in range(2):
                    last = pool.tensor_tensor(kl[r, b, :], kraw[r, :], kh[r, b, :].bitcast(F32), ALU.subtract)
            last.then_inc(at_fix, 1)
            pool.wait_ge(at_fix, 2)
            for b in range(2):
                attn_split(0, b, b, True)
            with pool.Fori(1, H // 2) as i:
                for b in range(2):
                    attn_split(0, b, i * 2 + b, False)
            fence(pool, "pool", 3)

            def tail_splits(layer):
                blockwise_splits(("oa", "ob")[layer], None)
                name, gain = f"ffn{layer}", f"ffn_pre{layer}"
                u, g = USED[name], GAINED[name]
                f0 = layer * NF
                for s in range(2):
                    split(s, u[s], gain, g[s], LAST[s])

                def tile(f, down_free):
                    split(0, f + (u[0] + 1), gain, f + (g[0] + 1), (fg_rd, f * 3 + (3 * f0 + 3)))
                    split(2, f + u[2], None, None, down_free)
                    split(1, f + (u[1] + 1), gain, f + (g[1] + 1), (fu_rd, f * 3 + (3 * f0 + 3)))

                tile(0, LAST.get(2))
                with pool.Fori(1, NF - 1) as f:
                    tile(f, (fd_rd, f * 24 + 24 * f0))
                split(2, u[2] + NF - 1, None, None, (fd_rd, 24 * (f0 + NF - 1)))
                LAST[0], LAST[1] = (fg_rd, 3 * (f0 + NF)), (fu_rd, 3 * (f0 + NF))
                LAST[2] = (fd_rd, 24 * (f0 + NF))
                for j in range(2):
                    lin_split(f"pe{layer}", j, None)
                blockwise_splits(f"pg{layer}", f"ple_gate{layer}")

            tail_splits(0)
            for j in range(2):
                lin_split("kb", j, "shared")
            fence(pool, "pool", 4)
            lin_split("wf", 0, "shared")
            for j in range(2):
                lin_split("vb", j, ("shared_v", "shared_v2")[j])
            lin_split_loop("qb", "mix_pre1")
            fence(pool, "pool", 5)
            for b in range(2):
                pool.memset(qh[HD:HD + 1, b, :].bitcast(F32), 1.0)
                last = pool.memset(ql[HD:HD + 1, b, :].bitcast(F32), 0.0)
            last.then_inc(at_fix, 1)
            pool.wait_ge(at_fix, 3)
            for b in range(2):
                attn_split(1, b, H + b, True)
            with pool.Fori(1, H // 2) as i:
                for b in range(2):
                    attn_split(1, b, i * 2 + (H + b), False)
            fence(pool, "pool", 6)
            tail_splits(1)

        @block.tensor
        def _(pe):
            def three(out, ah, al, bh, bl, first, last):
                nc.tensor.matmul(out, ah, bh, start=first, stop=False)
                nc.tensor.matmul(out, ah, bl, start=False, stop=False)
                return nc.tensor.matmul(out, al, bh, start=False, stop=last)

            def wcols(slot, c0, n):
                return wh[:, slot, c0:c0 + n], wl[:, slot, c0:c0 + n]

            def bank_free(g):
                if not isinstance(g, int) or g >= LBANKS:
                    pe.wait_ge(lin_ev, g - (LBANKS - 1))

            def lin_unit(g0, b0, slot, use, xh, xl, K, heads, M, blocks, first_waits=()):
                pe.wait_ge(w_rdy[slot], use + 1)
                n = 0
                for m in range(heads):
                    for b, (c, w) in enumerate(blocks):
                        if m == 0 and first_waits:
                            for s, v in first_waits[b]:
                                pe.wait_ge(s, v)
                        bank_free(g0 + n)
                        out = ps[0:M, (b0 + n) % LBANKS, 0:w]
                        for k in range(K):
                            ah, al = wcols(slot, (m * K + k) * P, M)
                            mm = three(out, ah, al, xh[:, k, c:c + w], xl[:, k, c:c + w], k == 0, k == K - 1)
                        n += 1
                        mm.then_inc(lin_rd, 1)

            TBL = [(b * TB, TB) for b in range(NB)]

            def lin_static(name, xh, xl, K=8, heads=1, M=P, blocks=TBL, waits=()):
                n = {nm: c for nm, c, _ in LIN}[name]
                per = heads * len(blocks)
                for j in range(n):
                    g = GROUP0[name] + j * per
                    lin_unit(g, g, j % 2, USED[name][j % 2] + j // 2, xh, xl, K, heads, M, blocks,
                             waits if j == 0 else ())

            def lin_loop(name, xh, xl, K=8, heads=1, waits=()):
                per = heads * NB
                for b in waits:
                    for s, v in b:
                        pe.wait_ge(s, v)
                with pe.Fori(0, 4) as i:
                    for s in range(2):
                        g = GROUP0[name] + s * per
                        lin_unit(i * (2 * per) + g, g, s, i + USED[name][s], xh, xl, K, heads, P, TBL)

            def norm(key, K):
                k = NORM_AT[key]
                pe.wait_ge(n_sq, k + 1)
                if k:
                    pe.wait_ge(n_rt, k)
                for j in range(K):
                    mm = nc.tensor.matmul(ps[:, 7, 0:TB], ones[:], sq[:, k % 2, j, :], start=(j == 0), stop=(j == K - 1))
                mm.then_inc(n_mm, 1)

            def norm_chain(s):
                for kind, b in CHAIN:
                    norm((s, kind, b), KD)

            def blockwise(name, xh, xl, s, waits=()):
                for b in waits:
                    for sm, v in b:
                        pe.wait_ge(sm, v)
                with pe.Fori(0, 2) as i:
                    for slot in range(2):
                        g = GROUP0[name] + slot * NB
                        lin_unit(i * (2 * NB) + g, g, slot, i + USED[name][slot], xh, xl, 8, 1, P, TBL)
                g = GROUP0[name] + 4 * NB
                slot, use, _ = USES[name, 4]
                lin_unit(g, g, slot, use, xh, xl, 8, 1, P, TBL)
                for b in range(NB):
                    for u in range(5, 8):
                        g = GROUP0[name] + 5 * NB + b * NB + (u - 5)
                        slot, use, _ = USES[name, u]
                        lin_unit(g, g, slot, use, xh, xl, 8, 1, P, TBL[b:b + 1])
                        if b and u == 5:
                            norm((s, "post", b - 1), KD)

            def n_ready(s, kind="pre"):
                return [[(n_done, HI_COUNT[NORM_AT[s, kind, b]])] for b in range(NB)]

            pe.wait_ge(ones_set, 1)
            for b in range(NB):
                norm(("s0", "pre", b), KD)
            lin_static("dq", nh, nl, waits=n_ready("s0"))
            lin_static("dkv", nh, nl)
            lin_static("kr", nh, nl, M=2 * ROPE)
            for kind, K in (("q", 4), ("kv", 2)):
                for b in range(NB):
                    norm(("s1", kind, b), K)
            fence(pe, "pe", 1)
            KBL = [(b * TKB, TKB) for b in range(KB)]
            lin_static("uk", cvh, cvl, K=2, heads=4, blocks=KBL)
            for half in range(2):
                pe.wait_ge(w_rdy[half], USED["uv"][half] + 1)
                for kt in range(KT):
                    g = GROUP0["uv"] + half * KT + kt
                    rows = min(P, TK - kt * P)
                    bank_free(g)
                    for k in range(2):
                        c = slice(kt * P, kt * P + rows)
                        bh, bl = wcols(half, k * 512, 512)
                        mm = three(ps[0:rows, bank(g), :], cvh[:, k, c], cvl[:, k, c], bh, bl, k == 0, k == 1)
                    mm.then_inc(lin_rd, 1)
            lin_loop("uq", nh, nl, K=4, heads=2)
            fence(pe, "pe", 2)

            def attn_pe(layer):
                rows = P if layer == 0 else HD + 1

                base_n = layer * H * STEPS

                def scores(pair_no, s, first):
                    hp, i = s // STEPS, ORDER[s % STEPS]
                    if s % STEPS == 0:
                        pe.wait_ge(at_split, pair_no * 2 + (layer * H + hp + 1))
                    if not (first and banks_before(s) < 0):
                        pe.wait_ge(at_e, pair_no * PAIR + (base_n + banks_before(s) + 1))
                    qc = slice(i * P, i * P + (P if i < 8 else DEC))
                    M = P if i < 8 else DEC
                    k0, k1 = (0, (i + 1) * P) if i < 8 else (SEQ, TK)
                    buf = S_BANK[i]
                    masked = i < 8 or layer == 1
                    nb = 0
                    c = k0
                    while c < k1:
                        w = min(512, k1 - c)
                        out = ps[0:M, buf + nb, 0:w]
                        dg = masked and (c + w == k1 if i < 8 else c == k0)
                        mm = three(out, qh[0:rows, hp, qc], ql[0:rows, hp, qc], kh[0:rows, hp, c:c + w],
                                   kl[0:rows, hp, c:c + w], True, not dg)
                        if dg:
                            dc = w - P if i < 8 else 0
                            mm = nc.tensor.matmul(ps[0:M, buf + nb, dc:dc + M], ident_r[0:M, 0:M],
                                                  mask_r[0:M, layer, 0:M], start=False, stop=True)
                        c += w
                        nb += 1
                    mm.then_inc(at_s, 1)

                base_c = layer * H * HC

                def turn_waits(i, c, first):
                    s, _, k0, _, _ = chunk(c)
                    if k0 == 0:
                        pe.wait_ge(at_p, i * PAIR + (base_n + s + 1))
                    if not (first and c < 2):
                        pe.wait_ge(at_lo, i * (2 * HC) + (base_c + c - 1))

                def turn(i, c, first):
                    s, tile, k0, n, _ = chunk(c)
                    M = P if tile < 8 else DEC
                    if tile < 8:
                        turn_waits(i, c, first)
                    for j in range(n):
                        kt = k0 + j
                        kr = P if (tile < 8 or kt < 2) else DEC
                        mm = nc.tensor.transpose(ps[0:kr, 4 + c % 2, j * P:j * P + M],
                                                 pr[0:M, PROB_AT[tile] + kt * P:PROB_AT[tile] + kt * P + kr],
                                                 ident[0:M, 0:M])
                    mm.then_inc(at_t, 1)

                def pv(i, c, first):
                    _, tile, k0, n, last = chunk(c)
                    hp = c // HC
                    if k0 == 0:
                        need = part_needed(tile, hp)
                        if need is not None and not (first and need <= 0):
                            pe.wait_ge(at_olo, i * 6 + (3 * layer * H + need))
                    pe.wait_ge(at_lo, i * (2 * HC) + (base_c + c + 1))
                    M = P if tile < 8 else DEC
                    if tile < 8:
                        out = ps[0:VD, 6 + tile // 4, (tile % 4) * P:(tile % 4 + 1) * P]
                    else:
                        out = ps[0:VD, 7, 0:DEC]
                    for j in range(n):
                        kt = k0 + j
                        kr = P if (tile < 8 or kt < 2) else DEC
                        vt = kt if tile < 8 else 8 + kt
                        mm = three(out, vh[0:kr, hp % 2, vt, :], vl[0:kr, hp % 2, vt, :], pth[0:kr, c % 2, j, 0:M],
                                   ptl[0:kr, c % 2, j, 0:M], kt == 0, last and j == n - 1)
                    mm.then_inc(at_pv, 1)

                def pair(i, first, drain=False):
                    for s in range(T_LAG if drain else PAIR):
                        if not drain:
                            scores(i, s, first)
                        for c in chunks_of(s - T_LAG):
                            if c < 0 and first:
                                continue
                            sample = chunk(c)[1] == 8
                            if sample:
                                turn_waits(i, c, first)
                                pv(i, c - PV_LAG, first)
                            turn(i, c, first)
                            if (c >= PV_LAG or not first) and not sample:
                                pv(i, c - PV_LAG, first)
                    if drain:
                        for c in range(-PV_LAG, 0):
                            pv(i, c, False)

                pair(0, True)
                with pe.Fori(1, H // 2) as i:
                    pair(i, False)
                pair(H // 2, False, True)

            attn_pe(0)
            fence(pe, "pe", 3)

            def ffn_pe(layer):
                name = f"ffn{layer}"
                u = USED[name]
                f0 = layer * NF

                def down(f, par, d, blocks_first=False):
                    m, b = (d % KD, d // KD) if blocks_first else (d // NB, d % NB)
                    if d == 0:
                        pe.wait_ge(w_rdy[2], f + (u[2] + 1))
                        pe.wait_ge(f_lo, f * 3 + (3 * f0 + 3))
                    if not (isinstance(f, int) and f == 0 and layer == 0 and d < 2):
                        pe.wait_ge(f_acc, f * 24 + (24 * f0 + d - 1))
                    mm = three(ps[:, 6 + d % 2, 0:TB], wh[:, 2, m * P:(m + 1) * P], wl[:, 2, m * P:(m + 1) * P],
                               hh[par][:, b * TB:(b + 1) * TB], hl[par][:, b * TB:(b + 1) * TB], True, True)
                    mm.then_inc(fd_rd, 1)

                def products(f, slot, b, first=False, among=lambda n: None):
                    rd, freed = ((fg_rd, f_sg), (fu_rd, f_u))[slot]
                    if not (first and layer == 0):
                        pe.wait_ge(freed, f * 3 + (3 * f0 + b - 2))
                    for k in range(KD):
                        xh, xl = nh[:, k, b * TB:(b + 1) * TB], nl[:, k, b * TB:(b + 1) * TB]
                        ah, al = wcols(slot, k * P, P)
                        for pas, (a, x) in enumerate(((ah, xh), (ah, xl), (al, xh))):
                            mm = nc.tensor.matmul(ps[:, 3 * slot + b, 0:TB], a, x, start=(k == 0 and pas == 0),
                                                  stop=(k == KD - 1 and pas == 2))
                            if k == KD - 1 and pas == 2:
                                mm.then_inc(rd, 1)
                            among((slot * NB + b) * 3 * KD + 3 * k + pas + 1)

                def first_tile():
                    key = f"s{2 + 3 * layer}"
                    norm((key, "pre", 0), KD)
                    norm((key, "post", 2), KD)
                    norm((key, "pre", 1), KD)
                    for slot in range(2):
                        pe.wait_ge(w_rdy[slot], u[slot] + 1)
                    if layer == 0:
                        pe.wait_ge(lin_ev, GROUP0["pe0"])
                    else:
                        pe.wait_ge(lin_ev, GROUP0["pe1"])
                    for b in range(NB):
                        if b == 1:
                            norm((key, "pre", 2), KD)
                        pe.wait_ge(n_done, HI_COUNT[NORM_AT[key, "pre", b]])
                        for slot in range(2):
                            products(0, slot, b, True)

                def tile(f, par):
                    def among(n):
                        if n in D_AT:
                            down(f - 1, 1 - par, D_AT.index(n))

                    for slot in range(2):
                        pe.wait_ge(w_rdy[slot], f + (u[slot] + 1))
                        for b in range(NB):
                            products(f, slot, b, False, among)

                first_tile()
                tile(1, 1)
                with pe.Fori(1, NF // 2) as i:
                    for par in range(2):
                        tile(i * 2 + par, par)
                for d in range(24):
                    down(NF - 1, (NF - 1) % 2, d, True)

            def tail_pe(layer):
                s0 = 2 + 3 * layer
                blockwise(("oa", "ob")[layer], nh, nl, f"s{s0}")
                ffn_pe(layer)
                pe.wait_ge(f_acc, 24 * NF * (layer + 1))
                norm_chain(f"s{s0 + 1}")
                pe.wait_ge(p_lo, layer + 1)
                lin_static(f"pe{layer}", ph, pl, K=2, heads=4)
                blockwise(f"pg{layer}", nh, nl, f"s{s0 + 2}", waits=n_ready(f"s{s0 + 1}"))

            tail_pe(0)
            for kind, b in CHAIN[2:]:
                norm(("s4", kind, b), KD)
            fence(pe, "pe", 4)
            lin_static("kb", nh, nl)
            lin_static("wf", nh, nl, M=H)
            for j in range(2):
                pe.wait_ge(w_rdy[j], USED["vb"][j] + 1)
            for tt in range(9):
                g = GROUP0["vb"] + tt
                rows = min(P, T - tt * P)
                bank_free(g)
                for k in range(KD):
                    bh, bl = wcols(k // 4, (k % 4) * KVH * HD, KVH * HD)
                    c = slice(tt * P, tt * P + rows)
                    mm = three(ps[0:rows, bank(g), 0:KVH * HD], nh[:, k, c], nl[:, k, c], bh, bl, k == 0, k == KD - 1)
                mm.then_inc(lin_rd, 1)
            lin_loop("qb", nh, nl)
            fence(pe, "pe", 5)
            attn_pe(1)
            fence(pe, "pe", 6)
            tail_pe(1)
            norm(("s7", "post", 2), KD)

        @block.scalar
        def _(act):
            def take(g, b, out, rows, w, func=ACT.Copy, **kw):
                act.wait_ge(lin_rd, g + 1)
                nc.scalar.activation(out, ps[0:rows, b, 0:w], func, **kw).then_inc(lin_ev, 1)

            SRC = {"q": (0, 4), "kv": (4, 2)}

            def squares(key, waits):
                k = NORM_AT[key]
                s, kind, b = key
                for sm, v in waits:
                    act.wait_ge(sm, v)
                if k >= 2:
                    act.wait_ge(n_mm, k - 1)
                c = slice(b * TB, (b + 1) * TB)
                if kind == "pre":
                    src, K = res[:, :, c], KD
                elif kind == "post":
                    src, K = y[:, :, c], KD
                else:
                    k0, K = SRC[kind]
                    src = y[:, k0:k0 + K, c]
                nc.scalar.activation(sq[:, k % 2, 0:K, :], src, ACT.Square).then_inc(n_sq, 1)

            def rest(key, hi_waits=()):
                k = NORM_AT[key]
                s, kind, b = key
                width = {"q": Q_RANK, "kv": KV_RANK}.get(kind, D)
                act.wait_ge(n_mm, k + 1)
                if k >= 2:
                    act.wait_ge(n_rs, k - 1)
                nc.scalar.activation(rt[:, k % 2, :], ps[:, 7, 0:TB], ACT.Sqrt, bias=epsc[:, 0:1],
                                     scale=1.0 / width).then_inc(n_rt, 1)
                if kind != "post":
                    for sm, v in hi_waits:
                        act.wait_ge(sm, v)
                    act.wait_ge(n_ap, k + 1)
                    c = slice(b * TB, (b + 1) * TB)
                    out, src = {"kv": (cvh[:, :, c], y[:, 6:8, c]), "q": (nh[:, 0:4, c], y[:, 0:4, c]),
                                "pre": (nh[:, :, c], y[:, :, c])}[kind]
                    nc.scalar.activation(out, src, ACT.Copy).then_inc(n_hi, 1)

            def norms(keys, waits, hi_waits=()):
                last = None
                for key in keys:
                    squares(key, waits(key))
                    if last:
                        rest(last, hi_waits)
                    last = key
                rest(last, hi_waits)

            def norms_among(keys, last_groups, waits):
                last_groups(0)
                squares(keys[0], waits(keys[0]))
                last_groups(1)
                rest(keys[0])
                squares(keys[1], waits(keys[1]))
                last_groups(2)
                for before, key in zip(keys[1:], keys[2:]):
                    squares(key, waits(key))
                    rest(before)
                rest(keys[-1])

            def chain_waits(ready):
                def waits(key):
                    s, kind, b = key
                    if kind == "post":
                        return ready[b]
                    return [(r_done, POST_COUNT[NORM_AT[s, "post", b]])]
                return waits

            act.wait_ge(ones_set, 1)
            norms([("s0", "pre", b) for b in range(NB)], lambda key: [(x_in[key[2]], 16)])
            act.wait_ge(const_r, 1)
            for m in range(6):
                for b in range(NB):
                    g = GROUP0["dq"] + m * NB + b
                    take(g, bank(g), y[:, m, b * TB:(b + 1) * TB], P, TB)
            for b in range(NB):
                g = GROUP0["kr"] + b
                take(g, bank(g), y[0:2 * ROPE, 6, b * TB:(b + 1) * TB], 2 * ROPE, TB)
            norms([("s1", "q", b) for b in range(NB)] + [("s1", "kv", b) for b in range(NB)],
                  lambda key: [(lin_ev, GROUP0["kr"] + 3)])
            act.wait_ge(cache_in, 16)
            nc.scalar.activation(cvh[:, :, T:TK], cc[:], ACT.Copy).then_inc(cc_hi, 1)
            fence(act, "act", 1)
            for m in range(8):
                if m >= 2:
                    act.wait_ge(st_out[m % 2], 16 * (m // 2))
                for b in range(KB):
                    g = GROUP0["uk"] + m * KB + b
                    take(g, bank(g), stg[:, m % 2, b * TKB:(b + 1) * TKB], P, TKB)
            for g in range(2 * KT):
                rows = min(P, TK - (g % KT) * P)
                act.wait_ge(st_out[g % 2], 16 * (4 + g // 2))
                take(GROUP0["uv"] + g, bank(GROUP0["uv"] + g), stg[0:rows, g % 2, 0:512], rows, 512)
            with act.Fori(0, 4) as i:
                for h in range(4):
                    act.wait_ge(st_out[h % 2], i * 32 + 16 * (4 + KT + h // 2))
                    for b in range(NB):
                        g = GROUP0["uq"] + h * NB + b
                        take(i * 12 + g, bank(g), stg[:, h % 2, b * TB:(b + 1) * TB], P, TB)
            fence(act, "act", 2)

            def attn_act(layer):
                base_n, base_c = layer * H * STEPS, layer * H * HC

                def exps(i, s, first):
                    tile = ORDER[s % STEPS]
                    M = P if tile < 8 else DEC
                    k = s % STEPS
                    act.wait_ge(at_nm, i * PAIR + (base_n + s + 1))
                    if not (first and s < STEPS):
                        act.wait_ge(at_t, i * (2 * HC) + (base_c + chunks_of(s - STEPS)[-1] + 1))
                    nc.scalar.activation(pr[0:M, PROB_AT[tile]:PROB_AT[tile] + KEYS[tile]], score_tile(tile), ACT.Exp,
                                         bias=nmx[0:M, k:k + 1], accum_out=rsum[0:M, k:k + 1]).then_inc(at_e, 1)

                def hi(i, c, first):
                    act.wait_ge(at_t, i * (2 * HC) + (base_c + c + 1))
                    if not (first and c < 2):
                        act.wait_ge(at_pv, i * (2 * HC) + (base_c + c - 1))
                    for dst, src in turned(c, pth):
                        last = nc.scalar.activation(dst, src, ACT.Copy)
                    last.then_inc(at_hi, 1)

                def outs(i, c):
                    if is_out(c):
                        dst, src, _ = out_part(c, i, nh)
                        act.wait_ge(at_pv, i * (2 * HC) + (base_c + c + 1))
                        nc.scalar.activation(dst, src, ACT.Copy).then_inc(at_ohi, 1)

                def pair(i, first, drain=False):
                    for s in range(T_LAG if drain else PAIR):
                        todo = [] if drain else [s]
                        for c in chunks_of(s - T_LAG):
                            if c >= 0 or not first:
                                hi(i, c, first)
                            if c >= OUT_LAG or not first:
                                outs(i, c - OUT_LAG)
                            while todo:
                                exps(i, todo.pop(), first)
                    if drain:
                        for c in range(-OUT_LAG, 0):
                            outs(i, c)

                pair(0, True)
                with act.Fori(1, H // 2) as i:
                    pair(i, False)
                pair(H // 2, False, True)

            attn_act(0)
            fence(act, "act", 3)

            def ffn_act(layer):
                f0 = layer * NF

                def tile(f, par, first):
                    for b in range(NB):
                        act.wait_ge(fg_rd, f * 3 + (3 * f0 + b + 1))
                        if not (first and layer == 0):
                            act.wait_ge(f_lo, f * 3 + (3 * f0 + b - 2))
                        nc.scalar.activation(sg[:, b, :], ps[:, b, 0:TB], ACT.Silu).then_inc(f_sg, 1)
                    for b in range(NB):
                        act.wait_ge(f_u, f * 3 + (3 * f0 + b + 1))
                        if not first:
                            if not (isinstance(f, int) and f + f0 < 2):
                                act.wait_ge(fd_rd, f * 24 + (24 * f0 - 24))
                        nc.scalar.activation(hh[par][:, b * TB:(b + 1) * TB], sg[:, b, :], ACT.Copy).then_inc(f_hi, 1)

                tile(0, 0, True)
                tile(1, 1, False)
                with act.Fori(1, NF // 2) as i:
                    for par in range(2):
                        tile(i * 2 + par, par, False)

            def tail_act(layer):
                s0 = 2 + 3 * layer
                name = ("oa", "ob")[layer]
                with act.Fori(0, 2) as i:
                    for s in range(2):
                        for b in range(NB):
                            g = GROUP0[name] + s * NB + b
                            take(i * 6 + g, bank(g), y[:, i * 2 + s, b * TB:(b + 1) * TB], P, TB)

                def last_groups(b):
                    for n in range(12 if b == 0 else 15 + 3 * b, 18 + 3 * b):
                        m, tb = group_place(n)
                        take(GROUP0[name] + n, bank(GROUP0[name] + n), y[:, m, tb * TB:(tb + 1) * TB], P, TB)

                norms_among([(f"s{s0}", k, b) for k, b in CHAIN], last_groups,
                            chain_waits([[(lin_ev, GROUP0[name] + 18 + 3 * b)] for b in range(NB)]))
                act.wait_ge(n_done, HI_COUNT[NORM_AT[f"s{s0}", "pre", 2]])
                ffn_act(layer)
                norms([(f"s{s0 + 1}", k, b) for k, b in CHAIN],
                      chain_waits([[(f_acc, 24 * (NF * (layer + 1) - 1) + KD * (b + 1))] for b in range(NB)]))
                act.wait_ge(p_in, 16 * (layer + 1))
                act.wait_ge(n_done, HI_COUNT[NORM_AT[f"s{s0 + 1}", "pre", 1]])
                nc.scalar.activation(ph[:], praw[:], ACT.Copy).then_inc(p_hi, 1)
                for m in range(8):
                    for b in range(NB):
                        g = GROUP0[f"pe{layer}"] + m * NB + b
                        take(g, bank(g), y[:, m, b * TB:(b + 1) * TB], P, TB)

                def gates(i, first, groups=range(2 * NB)):
                    for n in groups:
                        g = GROUP0[f"pg{layer}"] + n
                        if not (first and n < 2):
                            act.wait_ge(g_mul, i * 6 + (24 * layer + n - 1))
                        take(i * 6 + g, bank(g), gt[:, n % 2, :], P, TB, ACT.Sigmoid)

                gates(0, True)
                with act.Fori(1, 2) as i:
                    gates(i, False)
                chain = CHAIN if layer == 0 else [("post", b) for b in range(NB)]
                norms_among([(f"s{s0 + 2}", k, b) for k, b in chain],
                            lambda b: gates(0, False, range(12 if b == 0 else 15 + 3 * b, 18 + 3 * b)),
                            chain_waits([[(g_mul, 24 * layer + 18 + 3 * b)] for b in range(NB)]))

            tail_act(0)
            fence(act, "act", 4)
            for m in range(2):
                act.wait_ge(st_out[m], 16 * (4 + KT + 8))
                for b in range(NB):
                    g = GROUP0["kb"] + m * NB + b
                    take(g, bank(g), stg[:, m, b * TB:(b + 1) * TB], P, TB)
            for b in range(NB):
                g = GROUP0["wf"] + b
                take(g, bank(g), fz[:, b * TB:(b + 1) * TB], H, TB, ACT.Identity,
                     bias=gains[0:H, GAIN_AT["bf"]:GAIN_AT["bf"] + 1])
            act.wait_ge(lin_ev, GROUP0["wf"] + NB)
            nc.scalar.activation(fe[:], fz[:], ACT.Abs).then_inc(fx_a, 1)
            act.wait_ge(fx_a, 1)
            nc.scalar.activation(fe[:], fe[:], ACT.Exp, scale=-1.0).then_inc(fx_a, 1)
            act.wait_ge(fx_v, 1)
            nc.scalar.activation(fl[:], fu[:], ACT.Ln).then_inc(fx_a, 1)
            for tt in range(9):
                rows = min(P, T - tt * P)
                act.wait_ge(st_out[tt % 2], 16 * (4 + KT + 8 + 1 + tt // 2))
                g = GROUP0["vb"] + tt
                take(g, bank(g), stg[0:rows, tt % 2, 0:KVH * HD], rows, KVH * HD)
            with act.Fori(0, 4) as i:
                for m in range(2):
                    act.wait_ge(st_out[m], i * 16 + 16 * (4 + KT + 8 + 1 + 5 - m))
                    for b in range(NB):
                        g = GROUP0["qb"] + m * NB + b
                        take(i * 6 + g, bank(g), stg[:, m, b * TB:(b + 1) * TB], P, TB, scale=FOX_SCALE)
            fence(act, "act", 5)
            attn_act(1)
            fence(act, "act", 6)
            tail_act(1)

        @block.vector
        def _(dve):
            V = nc.vector

            def apply(key):
                k = NORM_AT[key]
                s, kind, b = key
                c = slice(b * TB, (b + 1) * TB)
                src = {"pre": res[:, :, c], "post": y[:, :, c], "q": y[:, 0:4, c], "kv": y[:, 4:6, c]}[kind]
                raw = y[:, :, c] if kind == "pre" else src
                K = {"q": 4, "kv": 2}.get(kind, KD)
                dve.wait_ge(n_rt, k + 1)
                V.reciprocal(rs[:, k % 2, :], rt[:, k % 2, :]).then_inc(n_rs, 1)
                dve.wait_ge(n_rs, k + 1)
                by = rs[:, k % 2, :].unsqueeze(1).to_broadcast((P, K, TB))
                if kind == "kv":
                    V.tensor_tensor(raw, src, by, ALU.mult).then_inc(kv_raw, 1)
                    dve.wait_ge(kv_raw, b + 1)
                    for j in range(K):
                        at_g = GAIN_AT["kv"] + j
                        last = V.tensor_scalar(y[:, 6 + j, c], y[:, 4 + j, c], gains[:, at_g:at_g + 1], None, ALU.mult)
                    last.then_inc(n_ap, 1)
                else:
                    V.tensor_tensor(raw, src, by, ALU.mult).then_inc(n_ap, 1)
                if kind == "post":
                    dve.wait_ge(n_ap, k + 1)
                    for j in range(K):
                        at_g = GAIN_AT[POST_GAIN[s]] + j
                        last = V.scalar_tensor_tensor(res[:, j, c], y[:, j, c], gains[:, at_g:at_g + 1],
                                                      res[:, j, c], ALU.mult, ALU.add)
                    last.then_inc(r_done, 1)

            def low(key):
                k = NORM_AT[key]
                _, kind, b = key
                c = slice(b * TB, (b + 1) * TB)
                if kind == "post":
                    return
                dve.wait_ge(n_hi, HI_COUNT[k])
                hi, lo = {"kv": (cvh[:, :, c], cvl[:, :, c]), "q": (nh[:, 0:4, c], nl[:, 0:4, c]),
                          "pre": (nh[:, :, c], nl[:, :, c])}[kind]
                raw = {"kv": y[:, 6:8, c], "q": y[:, 0:4, c], "pre": y[:, :, c]}[kind]
                V.tensor_tensor(lo, raw, hi.bitcast(F32), ALU.subtract).then_inc(n_done, 1)

            def norms(keys):
                for before, key in zip([None] + keys, keys + [None]):
                    if key:
                        apply(key)
                    if before:
                        low(before)

            V.memset(epsc[:], EPS)
            V.memset(ones[:], 1.0).then_inc(ones_set, 1)
            norms([("s0", "pre", b) for b in range(NB)])
            dve.wait_ge(const_in, 48)
            V.tensor_copy(ident_r[:], ident[:])
            V.tensor_copy(mask_r[:], wraw[:, 2, 0:2 * P].rearrange("p (a q) -> p a q", a=2)).then_inc(const_r, 1)
            dve.wait_ge(tab_in, 16)
            for b in range(NB):
                c = slice(b * TB, (b + 1) * TB)
                dve.wait_ge(lin_ev, GROUP0["kr"] + b + 1)
                V.tensor_tensor(y[0:ROPE, 6, c], y[0:ROPE, 6, c], krt[0:ROPE, c], ALU.mult)
                V.tensor_tensor(krf[:, c], y[ROPE:2 * ROPE, 6, c], krt[ROPE:2 * ROPE, c], ALU.mult).then_inc(kr_a, 1)
                dve.wait_ge(kr_a, b + 1)
                V.tensor_tensor(krf[:, c], krf[:, c], y[0:ROPE, 6, c], ALU.add).then_inc(kr_done, 1)
            dve.wait_ge(kr_done, NB)
            norms([("s1", kind, b) for kind in ("q", "kv") for b in range(NB)])
            dve.wait_ge(cc_hi, 1)
            V.tensor_tensor(cvl[:, :, T:TK], cc[:], cvh[:, :, T:TK].bitcast(F32), ALU.subtract).then_inc(cc_lo, 1)
            fence(dve, "dve", 1)
            dve.wait_ge(tab_in, 32)
            with dve.Fori(0, 4) as i:
                for h in range(4):
                    for b in range(NB):
                        c = slice(b * TB, (b + 1) * TB)
                        dve.wait_ge(lin_ev, i * 12 + (GROUP0["uq"] + h * NB + b + 1))
                        V.tensor_tensor(stg[:, h % 2, c], stg[:, h % 2, c], cs[:, c], ALU.mult).then_inc(q_done, 1)
            fence(dve, "dve", 2)

            def attention(layer):
                base_n, base_c = layer * H * STEPS, layer * H * HC

                def neg_max(i, s):
                    k, tile = s % STEPS, ORDER[s % STEPS]
                    M = P if tile < 8 else DEC
                    dve.wait_ge(at_s, i * PAIR + (base_n + s + 1))
                    V.tensor_reduce(nmx[0:M, k:k + 1], score_tile(tile), AX.X, ALU.max, negate=True).then_inc(at_nm, 1)

                def normalise(i, s):
                    k, tile = s % STEPS, ORDER[s % STEPS]
                    M = P if tile < 8 else DEC
                    p = pr[0:M, PROB_AT[tile]:PROB_AT[tile] + KEYS[tile]]
                    dve.wait_ge(at_e, i * PAIR + (base_n + s + 1))
                    V.reciprocal(rinv[0:M, k:k + 1], rsum[0:M, k:k + 1]).then_inc(at_r, 1)
                    dve.wait_ge(at_r, i * PAIR + (base_n + s + 1))
                    V.tensor_scalar(p, p, rinv[0:M, k:k + 1], None, ALU.mult).then_inc(at_p, 1)

                def lo(i, c):
                    dve.wait_ge(at_hi, i * (2 * HC) + (base_c + c + 1))
                    for (dst, src), (hi, _) in zip(turned(c, ptl), turned(c, pth)):
                        last = V.tensor_tensor(dst, src, hi.bitcast(F32), ALU.subtract)
                    last.then_inc(at_lo, 1)

                def outs(i, c):
                    if is_out(c):
                        dst, src, n = out_part(c, i, nl)
                        dve.wait_ge(at_ohi, i * 6 + (3 * layer * H + n))
                        V.tensor_tensor(dst, src, out_part(c, i, nh)[0].bitcast(F32), ALU.subtract).then_inc(at_olo, 1)

                def pair(i, first, drain=False):
                    for s in range(T_LAG if drain else PAIR):
                        if not drain:
                            neg_max(i, s)
                        todo = [s - 1] if (s >= 1 or not first) and not (drain and s > 0) else []
                        while todo:
                            normalise(i, todo.pop())
                        for c in chunks_of(s - T_LAG):
                            if c >= 0 or not first:
                                lo(i, c)
                            if c >= OUT_LAG or not first:
                                outs(i, c - OUT_LAG)
                    if drain:
                        for c in range(-OUT_LAG, 0):
                            outs(i, c)

                pair(0, True)
                with dve.Fori(1, H // 2) as i:
                    pair(i, False)
                pair(H // 2, False, True)

            def ffn(layer):
                f0 = layer * NF
                events = sorted([(p, "down", d) for d, p in enumerate(D_AT)]
                                + [(72 + 24 * (b + 1), "mul", b) for b in range(NB)]
                                + [(108 + 21 * b, "lo", b) for b in range(NB)])

                def down(f, d, first, blocks_first=False):
                    m, b = (d % KD, d // KD) if blocks_first else (d // NB, d % NB)
                    c = slice(b * TB, (b + 1) * TB)
                    dve.wait_ge(fd_rd, f * 24 + (24 * f0 + d + 1))
                    if first:
                        V.tensor_copy(y[:, m, c], ps[:, 6 + d % 2, 0:TB]).then_inc(f_acc, 1)
                    else:
                        V.tensor_tensor(y[:, m, c], ps[:, 6 + d % 2, 0:TB], y[:, m, c], ALU.add).then_inc(f_acc, 1)

                def tile(f, par, first, second=False):
                    for _, what, x in events:
                        c = slice(x * TB, (x + 1) * TB)
                        if what == "down":
                            if not first:
                                down(f - 1, x, second)
                        elif what == "mul":
                            dve.wait_ge(f_sg, f * 3 + (3 * f0 + x + 1))
                            dve.wait_ge(fu_rd, f * 3 + (3 * f0 + x + 1))
                            V.tensor_tensor(sg[:, x, :], ps[:, 3 + x, 0:TB], sg[:, x, :], ALU.mult).then_inc(f_u, 1)
                        else:
                            dve.wait_ge(f_hi, f * 3 + (3 * f0 + x + 1))
                            V.tensor_tensor(hl[par][:, c], sg[:, x, :], hh[par][:, c].bitcast(F32),
                                            ALU.subtract).then_inc(f_lo, 1)

                tile(0, 0, True)
                tile(1, 1, False, True)
                with dve.Fori(1, NF // 2) as i:
                    for par in range(2):
                        tile(i * 2 + par, par, False)
                for d in range(24):
                    down(NF - 1, d, False, True)

            def tail(layer):
                s0 = 2 + 3 * layer
                norms([(f"s{s0}", k, b) for k, b in CHAIN])
                ffn(layer)
                norms([(f"s{s0 + 1}", k, b) for k, b in CHAIN])
                dve.wait_ge(n_done, HI_COUNT[NORM_AT[f"s{s0 + 1}", "pre", 2]])
                dve.wait_ge(p_hi, layer + 1)
                V.tensor_tensor(pl[:], praw[:], ph[:].bitcast(F32), ALU.subtract).then_inc(p_lo, 1)
                def gated(i, n):
                    m, b = group_place(n)
                    c = slice(b * TB, (b + 1) * TB)
                    dve.wait_ge(lin_ev, i * 6 + (GROUP0[f"pg{layer}"] + n + 1))
                    V.tensor_tensor(y[:, i * 2 + m, c], gt[:, n % 2, :], y[:, i * 2 + m, c], ALU.mult).then_inc(g_mul, 1)

                with dve.Fori(0, 2) as i:
                    for n in range(2 * NB):
                        gated(i, n)
                for n in range(4 * NB, 24):
                    gated(0, n)
                    if n == 6 * NB + 2:
                        norms([(f"s{s0 + 2}", "post", 0)])

            attention(0)
            fence(dve, "dve", 3)
            tail(0)
            norms([("s4", k, b) for k, b in CHAIN[1:]])
            fence(dve, "dve", 4)
            link = [0]

            def chained(ins):
                link[0] += 1
                ins.then_inc(fx_v, 1)
                dve.wait_ge(fx_v, link[0])

            dve.wait_ge(fx_a, 2)
            chained(V.tensor_scalar(fu[:], fe[:], 1.0, None, ALU.add))
            dve.wait_ge(fx_a, 3)
            chained(V.scalar_tensor_tensor(fe[:], fu[:], -1.0, fe[:], ALU.add, ALU.subtract))
            chained(V.reciprocal(fu[:], fu[:]))
            chained(V.tensor_tensor(fe[:], fe[:], fu[:], ALU.mult))
            chained(V.tensor_tensor(fl[:], fl[:], fe[:], ALU.subtract))
            chained(V.scalar_tensor_tensor(flog[:, 0:T], fz[:], 0.0, fl[:], ALU.min, ALU.subtract))
            dve.wait_ge(cache_in, 32)

            def scan(cols, initial):
                n = cols.stop - cols.start
                chained(V.tensor_tensor_scan(fcum[:, cols], ones[0:H, 0:1].to_broadcast((H, n)), flog[:, cols],
                                             initial, ALU.mult, ALU.add))

            scan(slice(T, TK), 0.0)
            scan(slice(0, SEQ), 0.0)
            scan(slice(SEQ, T), fcum[:, TK - 1:TK])
            chained(V.tensor_scalar(fcum[:], fcum[:], -1.0, None, ALU.mult))
            fence(dve, "dve", 5)
            attention(1)
            fence(dve, "dve", 6)
            tail(1)
            norms([("s7", "post", b) for b in range(1, NB)])


def _weight_units(np, w):
    def cols(m, width=P):
        r, c = m.shape
        return m.reshape(r // P, P, c // width, width).transpose(2, 1, 0, 3).reshape(c // width, P, -1)

    def packed(tiles, n):
        t, p, c = tiles.shape
        return tiles.reshape(t // n, n, p, c).transpose(0, 2, 1, 3).reshape(t // n, p, n * c)

    def padded(m):
        out = np.zeros((m.shape[0], P), m.dtype)
        out[:, :m.shape[1]] = m
        return cols(out)

    def swapped(m):
        return np.concatenate([m[..., ROPE // 2:], m[..., :ROPE // 2]], -1)

    uq = w["w_uq"][0].reshape(Q_RANK, H, NOPE + ROPE)
    uq = np.concatenate([uq, swapped(uq[..., NOPE:])], -1).reshape(Q_RANK, H * P)
    kr = w["w_dkv"][0][:, KV_RANK:]

    def ffn(i):
        g, u = cols(w["w_gate"][i]), cols(w["w_up"][i])
        d = w["w_down"][i].reshape(NF, P, D)
        order = [g[0], u[0]]
        for f in range(NF - 1):
            order += [g[f + 1], d[f], u[f + 1]]
        return np.stack(order + [d[NF - 1]])

    def moving(m, per):
        r, c = m.shape
        return m.reshape(r // P // per, per, P, c).transpose(0, 2, 1, 3).reshape(-1, P, per * c)

    uv = w["w_uv"][0].reshape(KV_RANK, 2, H * VD // 2)
    parts = {
        "dq": cols(w["w_dq"][0]), "dkv": cols(w["w_dkv"][0][:, :KV_RANK]),
        "kr": padded(np.concatenate([kr, swapped(kr)], -1)),
        "uk": packed(cols(w["w_uk"][0].reshape(KV_RANK, H * NOPE)), 4),
        "uv": np.concatenate([moving(uv[:, h], 2) for h in range(2)]),
        "uq": packed(cols(uq), 2), "oa": cols(w["w_oa"][0]), "ffn0": ffn(0),
        "pe0": packed(cols(w["w_ple"][0]), 4), "pg0": cols(w["w_ple_gate"][0]),
        "kb": cols(w["w_kb"]), "wf": padded(w["w_f"]), "vb": moving(w["w_vb"], 4),
        "qb": cols(w["w_qb"][0]), "ob": cols(w["w_ob"][0]), "ffn1": ffn(1),
        "pe1": packed(cols(w["w_ple"][1]), 4), "pg1": cols(w["w_ple_gate"][1]),
    }
    for name, n, _ in LIN:
        assert parts[name].shape == (n, P, UW), (name, parts[name].shape)
    return np.concatenate([parts[name] for name, _, _ in LIN])


def _gain_table(np, w):
    def tiles(v):
        return v.reshape(-1, P).T

    def eight(v, places):
        out = np.zeros((P, 8), v.dtype)
        t = tiles(v)
        for j, k in enumerate(places):
            out[:, j] = t[:, k]
        return out

    every = range(8)
    bf = np.zeros((P, 8), w["b_f"].dtype)
    bf[:H, 0] = w["b_f"]
    cols = {"mix_pre0": eight(w["g_mix_pre"][0], every), "q": eight(w["g_q"][0], [0, 1, 2, 3] * 2),
            "mix_post0": eight(w["g_mix_post"][0], every), "ffn_pre0": eight(w["g_ffn_pre"][0], every),
            "ffn_post0": eight(w["g_ffn_post"][0], every), "ple_gate0": eight(w["g_ple_gate"][0], every),
            "ple_post0": eight(w["g_ple_post"][0], every), "shared": eight(w["g_shared"], every),
            "shared_v": eight(w["g_shared"], [0, 0, 1, 1, 2, 2, 3, 3]),
            "shared_v2": eight(w["g_shared"], [4, 4, 5, 5, 6, 6, 7, 7]),
            "mix_pre1": eight(w["g_mix_pre"][1], every), "mix_post1": eight(w["g_mix_post"][1], every),
            "ffn_pre1": eight(w["g_ffn_pre"][1], every), "ffn_post1": eight(w["g_ffn_post"][1], every),
            "ple_gate1": eight(w["g_ple_gate"][1], every), "ple_post1": eight(w["g_ple_post"][1], every),
            "kv": eight(w["g_kv"][0], range(2)), "bf": bf}
    return np.concatenate([cols[n] for n in GAINS], 1)


def _position_tables(np):
    half = ROPE // 2
    inv = np.power(np.float32(10000.0), -np.arange(half, dtype=np.float32) / half).astype(np.float32)
    pos = np.concatenate([np.arange(SEQ), PAST + np.arange(DEC)]).astype(np.float32)
    ang = (inv[:, None] * pos[None, :]).astype(np.float32)
    cos, sin = np.cos(ang).astype(np.float32), np.sin(ang).astype(np.float32)
    krt = np.concatenate([cos, cos, -sin, sin])
    scale = np.float32((NOPE + ROPE) ** -0.5)
    cs = np.concatenate([np.ones((NOPE, T), np.float32), krt]) * scale
    q, k = np.arange(P)[:, None], np.arange(P)[None, :]
    masks = np.zeros((P, 2, P), np.float32)
    masks[:, 0][k // 64 > q // 64] = NEG
    masks[:, 1][k > q] = NEG
    return krt, cs.astype(np.float32), masks.reshape(P, 2 * P), np.eye(P, dtype=np.float32)


def kernel(**w):
    import numpy as np
    import concourse.bacc as bacc
    from concourse.bass_utils import run_bass_kernel_spmd as run

    w = {k: np.asarray(v) for k, v in w.items()}
    krt, cs, masks, ident = _position_tables(np)
    c = np.ascontiguousarray
    x = np.concatenate([w["x_prompt"][0], w["x_sample"][0]])
    p = np.concatenate([w["p_prompt"][:, 0], w["p_sample"][:, 0]], 1)
    arrays = {
        "units": _weight_units(np, w), "gains": c(_gain_table(np, w)), "krt": krt, "cs": cs, "masks": masks,
        "ident": ident,
        "xT": c(x.reshape(T, KD, P).transpose(2, 1, 0)),
        "pT": c(p.reshape(2, T, 2, P).transpose(0, 3, 2, 1)),
        "cckvT": c(w["cache_ckv"][0, 0].reshape(PAST, 2, P).transpose(2, 1, 0)),
        "ckrT": c(w["cache_kr"][0, 0].T),
        "ckT": c(w["cache_k"][0].transpose(1, 2, 0)),
        "cv": c(w["cache_v"][0].reshape(PAST, KVH * HD)),
        "clfT": c(w["cache_logf"][0].T),
    }
    nc = bacc.Bacc("TRN2", target_bir_lowering=False, num_devices=1)
    io = {n: nc.dram_tensor(n, a.shape, F32, kind="ExternalInput").ap() for n, a in arrays.items()}

    def dram(name, shape, kind="Internal"):
        io[name] = nc.dram_tensor(name, shape, F32, kind=kind).ap()

    dram("yT", (P, KD, T), "ExternalOutput")
    dram("ckv_out", (P, 2, T), "ExternalOutput")
    dram("kr_out", (ROPE, T), "ExternalOutput")
    dram("kT_out", (KVH * HD, T), "ExternalOutput")
    dram("v_out", (T, KVH * HD), "ExternalOutput")
    dram("lf_out", (H, T), "ExternalOutput")
    dram("kA", (H * NOPE, TK))
    dram("vA", (TK, H * VD))
    dram("qA", (H, P, T))
    dram("qBm", (D, T))
    dram("nck_all", (H, TK))
    full = (KT - 1) * P
    io["kA_h"] = io["kA"].rearrange("(h d) t -> h d t", d=NOPE)
    io["vA_full"] = io["vA"][0:full, :].rearrange("(t p) (h d) -> h p t d", p=P, d=VD)
    io["vA_last"] = io["vA"][full:TK, :].rearrange("p (h d) -> h p d", d=VD)
    io["qB"] = io["qBm"].rearrange("(h d) t -> h d t", d=HD)
    io["qB_pair"] = io["qBm"].rearrange("(m p) t -> m p t", p=P)
    io["nck"] = io["nck_all"].rearrange("(h o) t -> h o t", o=1)
    io["kT_h"] = io["kT_out"].rearrange("(h d) t -> h d t", d=HD)
    io["v_full"] = io["v_out"][0:SEQ, :].rearrange("(t p) (h d) -> h p t d", p=P, d=HD)
    io["v_new"] = io["v_out"][SEQ:T, :].rearrange("p (h d) -> h p d", d=HD)
    cv = io["cv"].rearrange("p (h d) -> h p d", d=HD)
    n0 = P - DEC
    io["cv0"], io["cv1"], io["cv2"] = cv[:, 0:n0, :], cv[:, n0:n0 + P, :], cv[:, n0 + P:PAST, :]
    build_program(nc, io)
    r = run(nc, [arrays], core_ids=[0]).results[0]

    def rows(a):
        a = c(a.T)
        return a[None, :SEQ], a[None, SEQ:]

    y_p, y_s = rows(r["yT"].transpose(1, 0, 2).reshape(D, T))
    ckv_p, ckv_s = rows(r["ckv_out"].transpose(1, 0, 2).reshape(KV_RANK, T))
    kr_p, kr_s = rows(r["kr_out"])
    k_p, k_s = rows(r["kT_out"])
    lf_p, lf_s = rows(r["lf_out"])
    v = r["v_out"].reshape(T, KVH, HD)
    return (y_p, y_s, ckv_p[None], kr_p[None], k_p.reshape(1, SEQ, KVH, HD), v[None, :SEQ], lf_p,
            ckv_s[None], kr_s[None], k_s.reshape(1, DEC, KVH, HD), v[None, SEQ:], lf_s)
```

```python
from contextlib import ExitStack

import concourse.bass as bass
from concourse import mybir

F32 = mybir.dt.float32
F32R = mybir.dt.float32r
ACT = mybir.ActivationFunctionType
ALU = mybir.AluOpType
AX = mybir.AxisListType

P = 128
D = 1024
KD = D // P
SEQ, DEC, PAST = 1024, 32, 256
T = SEQ + DEC
TK = T + PAST
NB = 3
TB = T // NB
KB = 4
TKB = TK // KB
KT = (TK + P - 1) // P
H = 16
Q_RANK, KV_RANK, NOPE, ROPE, VD = 512, 256, 64, 32, 64
KVH, HD = 4, 64
PLE = 256
F = 2816
NF = F // P
EPS = 1e-6
NEG = -1e30
FOX_SCALE = HD ** -0.5
UW = 1024

LIN = [("dq", 4, "mix_pre0"), ("dkv", 2, "mix_pre0"), ("kr", 1, "mix_pre0"), ("uk", 2, None),
       ("uv", 2, None), ("uq", 8, "q"), ("oa", 8, None), ("ffn0", 3 * NF, "ffn_pre0"),
       ("pe0", 2, None), ("pg0", 8, "ple_gate0"),
       ("kb", 2, "shared"), ("wf", 1, "shared"), ("vb", 2, "shared_v"), ("qb", 8, "mix_pre1"),
       ("ob", 8, None), ("ffn1", 3 * NF, "ffn_pre1"), ("pe1", 2, None), ("pg1", 8, "ple_gate1")]
GAINS = ["mix_pre0", "q", "mix_post0", "ffn_pre0", "ffn_post0", "ple_gate0", "ple_post0", "shared",
         "shared_v", "shared_v2", "mix_pre1", "mix_post1", "ffn_pre1", "ffn_post1", "ple_gate1",
         "ple_post1", "kv", "bf"]
GAIN_AT = {name: 8 * i for i, name in enumerate(GAINS)}


BLOCKWISE = ("oa", "pg0", "ob", "pg1")


def slot_of(name, u):
    if name.startswith("ffn"):
        return u % 3
    return (0, 1, 0, 1, 0, 1, 2, 0)[u] if name in BLOCKWISE else u % 2


def unit_places():
    first, used, gained, uses = {}, {}, {}, {}
    at, use, gain = 0, [0, 0, 0], [0, 0, 0]
    for name, n, g in LIN:
        first[name], used[name], gained[name] = at, list(use), list(gain)
        at += n
        for u in range(n):
            s = slot_of(name, u)
            uses[name, u] = s, use[s], gain[s]
            use[s] += 1
            if g is not None and not (name.startswith("ffn") and s == 2):
                gain[s] += 1
    return first, used, gained, at, uses


UNIT0, USED, GAINED, UNITS, USES = unit_places()

GROUPS = [("dq", 12), ("dkv", 6), ("kr", 3), ("uk", 8 * KB), ("uv", 2 * KT), ("uq", 48), ("oa", 24),
          ("pe0", 24), ("pg0", 24), ("kb", 6), ("wf", 3), ("vb", 9), ("qb", 24), ("ob", 24),
          ("pe1", 24), ("pg1", 24)]
GROUP0 = {}
_at = 0
for _n, _c in GROUPS:
    GROUP0[_n] = _at
    _at += _c
LBANKS = 6

CHAIN = [("post", 0), ("post", 1), ("pre", 0), ("post", 2), ("pre", 1), ("pre", 2)]
NORMS = ([("s0", "pre", b) for b in range(NB)] + [("s1", "q", b) for b in range(NB)]
         + [("s1", "kv", b) for b in range(NB)]
         + [(s, k, b) for s in ("s2", "s3", "s4", "s5", "s6") for k, b in CHAIN]
         + [("s7", "post", b) for b in range(NB)])
NORM_AT = {n: i for i, n in enumerate(NORMS)}
POST_GAIN = {"s2": "mix_post0", "s3": "ffn_post0", "s4": "ple_post0", "s5": "mix_post1",
             "s6": "ffn_post1", "s7": "ple_post1"}

ORDER = [7, 6, 0, 1, 5, 4, 2, 8, 3]
STEPS = len(ORDER)
PAIR = 2 * STEPS
T_LAG = 4
TURN_SLOTS = 4
PV_LAG, OUT_LAG = 2, 2
CHUNKS = []
for _s in range(PAIR):
    _i = ORDER[_s % STEPS]
    _n = 3 if _i == 8 else _i + 1
    CHUNKS += [(_s, _i, _k, min(4, _n - _k)) for _k in range(0, _n, 4)]
HC = len(CHUNKS) // 2
KEYS = [(_i + 1) * P for _i in range(8)] + [DEC + PAST]
S_BANK = {7: 0, 6: 2, 0: 0, 1: 1, 5: 2, 4: 0, 2: 2, 8: 3, 3: 2}
PROB_AT = {_i: sum(KEYS[:_i]) for _i in range(9)}
OUT_PARTS = sorted([(4, 5, 6, 7), (8,), (0, 1, 2, 3)], key=lambda _t: max(ORDER.index(_i) for _i in _t))
OUT_AFTER = {max(_t, key=ORDER.index): _p for _p, _t in enumerate(OUT_PARTS)}
PART_OF = {_i: _p for _p, _t in enumerate(OUT_PARTS) for _i in _t}


def score_banks(s):
    i = ORDER[s % STEPS]
    return range(S_BANK[i], S_BANK[i] + (KEYS[i] + 511) // 512)


def banks_before(s):
    return next(t for t in range(s - 1, s - STEPS - 1, -1) if set(score_banks(t)) & set(score_banks(s)))


def part_needed(tile, hp):
    if tile != min(OUT_PARTS[PART_OF[tile]], key=ORDER.index):
        return None
    return (3 * hp + PART_OF[4] + 1 if tile == 8
            else 3 * (hp - 1) + (PART_OF[8] if tile > 3 else PART_OF[0]) + 1)




def chunk(c):
    s, i, k0, n = CHUNKS[c % (2 * HC)]
    last = k0 + n == (3 if i == 8 else i + 1)
    return s + c // (2 * HC) * PAIR, i, k0, n, last


def chunks_of(s):
    at = s // PAIR * 2 * HC
    return [at + c for c, x in enumerate(CHUNKS) if x[0] == s % PAIR]


def turn_slot(c):
    p = c % (2 * HC)
    whole = 2 * HC // TURN_SLOTS * TURN_SLOTS
    return p % TURN_SLOTS if p < whole else p - 2 * HC + TURN_SLOTS


def slot_before(c):
    return next(b for b in range(c - 1, c - 2 * HC - 1, -1) if turn_slot(b) == turn_slot(c))


D_AT = [16 + (9 * d) // 2 for d in range(24)]


PER_UNIT = {"dq": 3, "dkv": 3, "kr": 3, "uk": 4 * KB, "uv": KT, "uq": 6, "oa": 3, "pe0": 12, "pg0": 3,
            "kb": 3, "wf": 3, "vb": 9, "qb": 3, "ob": 3, "pe1": 12, "pg1": 3}


def group_place(n):
    return (n // NB, n % NB) if n < 5 * NB else (5 + n % NB, n // NB - 5)


def group_after(name, slot, j):
    if name == "vb":
        return GROUP0[name] + 9
    return j * (2 * PER_UNIT[name]) + (GROUP0[name] + PER_UNIT[name] * (slot + 1))


HI_COUNT = [sum(n[1] != "post" for n in NORMS[:k + 1]) for k in range(len(NORMS))]


POOL_LOW = [s in ("s2", "s3", "s4", "s5", "s6") and kind == "pre" and b < 2 for s, kind, b in NORMS]
POOL_COUNT = [sum(POOL_LOW[:k + 1]) for k in range(len(NORMS))]
DVE_COUNT = [HI_COUNT[k] - POOL_COUNT[k] for k in range(len(NORMS))]
POST_COUNT = [k + 1 - HI_COUNT[k] for k in range(len(NORMS))]


def halves(K):
    return [(0, K // 2), (K // 2, K)]


def build_program(nc, io):
    with ExitStack() as ctx:
        base = (nc.sbuf_base + 31) // 32 * 32
        end = nc.sbuf_usable_end

        def at(name, shape, dt, offset):
            n = 4
            for x in shape[1:]:
                n *= x
            n = (n + 31) // 32 * 32
            assert base + offset + n <= end, (name, base + offset + n - end)
            return nc.alloc_sbuf_tensor_at(name, shape, dt, offset=base + offset), offset + n

        res, o = at("residual", [P, KD, T], F32, 0)
        n_off = o
        nh, o = at("act_hi", [P, KD, T], F32R, o)
        nl, o = at("act_lo", [P, KD, T], F32R, o)
        cvh, _ = at("latent_hi", [P, 2, TK], F32R, n_off + 4 * T * 4)
        cvl, _ = at("latent_lo", [P, 2, TK], F32R, n_off + KD * T * 4 + 4 * T * 4)
        wraw, o = at("weight_raw", [P, 3, UW], F32, o)
        attn_off = o
        wh, o = at("weight_hi", [P, 3, UW], F32R, o)
        wl, o = at("weight_lo", [P, 3, UW], F32R, o)
        y, o = at("sublayer_out", [P, KD, T], F32, o)
        scr = o
        NGC = 8 * len(GAINS)
        const_bytes = 4 * (NGC + P + P + P + 2 * P + 8)
        o = (end - base - const_bytes) // 32 * 32
        top = o
        gains, o = at("gains", [P, NGC], F32, o)
        ones, o = at("ones", [P, P], F32, o)
        ident, o = at("ident", [P, P], F32, o)
        ident_r, o = at("ident_r", [P, P], F32R, o)
        mask_r, o = at("mask_r", [P, 2, P], F32R, o)
        epsc, o = at("eps_col", [P, 8], F32, o)
        sq, o = at("squares", [P, 2, KD, TB], F32, scr)
        rt, o = at("root", [P, 2, TB], F32, o)
        rs, o = at("rstd", [P, 2, TB], F32, o)
        norm_end = o
        stg, o = at("stage", [P, 2, TK], F32, scr)
        cs, o = at("rope_table", [P, T], F32, o)
        assert o <= top
        cc, o = at("cached_latent", [P, 2, PAST], F32, scr + 4 * (2 * KD * TB + 4 * TB))
        krf, o = at("rope_key", [ROPE, T], F32, o)
        assert o <= top
        krt, _ = at("rope_table_k", [2 * ROPE, T], F32, scr - 4 * T)
        sg, o = at("ffn_act", [P, NB, TB], F32, scr)
        hh0, o = at("ffn_hi_even", [P, T], F32R, o)
        hl0, o = at("ffn_lo_even", [P, T], F32R, o)
        hh1, o = at("ffn_hi_odd", [P, T], F32R, norm_end)
        hl1, o = at("ffn_lo_odd", [P, T], F32R, o)
        assert o <= top
        hh, hl = (hh0, hh1), (hl0, hl1)
        pl, _ = at("ple_lo", [P, 2, T], F32R, scr)
        gt, _ = at("gate", [P, 2, TB], F32, norm_end)
        assert NORM_AT["s3", "pre", 2] % 2 == NORM_AT["s6", "pre", 2] % 2 == 0
        ph, o = at("ple_hi", [P, 2, T], F32R, scr + 4 * KD * TB)
        praw, o = at("ple_raw", [P, 2, T], F32, norm_end)
        assert o <= top
        yo = scr - 4 * KD * T
        fz, o = at("forget_z", [H, T], F32, yo)
        fe, o = at("forget_e", [H, T], F32, o)
        fu, o = at("forget_u", [H, T], F32, o)
        fl, o = at("forget_l", [H, T], F32, o)
        flog, o = at("forget_log", [H, TK], F32, o)
        fcum, o = at("forget_cum", [H, TK], F32, o)
        qh, o = at("q_hi", [P, 2, T], F32R, attn_off)
        ql, o = at("q_lo", [P, 2, T], F32R, o)
        kh, o = at("k_hi", [P, 2, TK], F32R, o)
        kl, o = at("k_lo", [P, 2, TK], F32R, o)
        vh, o = at("v_hi", [P, 2, KT, VD], F32R, o)
        vl, o = at("v_lo", [P, 2, KT, VD], F32R, o)
        pr, o = at("probs", [P, sum(KEYS)], F32, o)
        pth, o = at("probs_t_hi", [P, TURN_SLOTS, 4, P], F32R, o)
        ptl, o = at("probs_t_lo", [P, TURN_SLOTS, 4, P], F32R, o)
        nmx, o = at("neg_max", [P, STEPS], F32, o)
        rsum, o = at("row_sum", [P, STEPS], F32, o)
        rinv, o = at("row_inv", [P, STEPS], F32, o)
        assert o <= top
        rawoff = attn_off - 3 * UW * 4
        qraw, o = at("q_raw", [P, T], F32, rawoff)
        kraw, o = at("k_raw", [P, TK], F32, o)
        vraw, o = at("v_raw", [P, KT, VD], F32, o)
        assert o == attn_off

        ps = ctx.enter_context(nc.psum_tensor("ps", [P, 8, 512], F32))

        def sem(name):
            return ctx.enter_context(nc.semaphore(name))

        const_in = sem("const_in")
        ones_set = sem("ones_set")
        const_r = sem("const_r")
        x_in = [sem(f"x_in{b}") for b in range(NB)]
        w_raw = [sem(f"w_raw{s}") for s in range(3)]
        w_gain = [sem(f"w_gain{s}") for s in range(3)]
        w_hi = [sem(f"w_hi{s}") for s in range(3)]
        w_rdy = [sem(f"w_rdy{s}") for s in range(3)]
        lin_rd = sem("lin_rd")
        lin_ev = sem("lin_ev")
        n_sq, n_mm, n_rt = sem("norm_squares"), sem("norm_sum"), sem("norm_root")
        n_rs, n_ap, n_hi, n_done = sem("norm_rstd"), sem("norm_applied"), sem("norm_hi"), sem("norm_done")
        n_done_pool = sem("norm_done_pool")
        r_done = sem("residual_done")
        kv_raw = sem("kv_raw")
        tab_in, cache_in, p_in = sem("tab_in"), sem("cache_in"), sem("p_in")
        cc_hi, cc_lo = sem("cc_hi"), sem("cc_lo")
        kr_a, kr_done = sem("kr_products"), sem("kr_done")
        q_done = sem("q_done")
        st_out = [sem("st_out0"), sem("st_out1")]
        ckv_out, kr_out, lf_out, nck_out, y_out = (sem("ckv_out"), sem("kr_out"), sem("lf_out"),
                                                   sem("nck_out"), sem("y_out"))
        fg_rd, fu_rd, fd_rd = sem("ffn_gate_rd"), sem("ffn_up_rd"), sem("ffn_down_rd")
        f_sg, f_u, f_hi, f_lo, f_acc = (sem("ffn_silu"), sem("ffn_mul"), sem("ffn_hi_done"),
                                        sem("ffn_lo_done"), sem("ffn_acc"))
        p_hi, p_lo, g_mul = sem("ple_hi_done"), sem("ple_lo_done"), sem("gate_mul")
        fx_a, fx_v = sem("forget_act"), sem("forget_dve")
        at_raw, at_khi, at_split = sem("at_raw"), sem("at_split_hi"), sem("at_split")
        at_vraw, at_vhi, at_vsplit = sem("at_values_raw"), sem("at_values_hi"), sem("at_values_split")
        at_kr = sem("at_kr")
        fix_hi, fix_lo, first_hi, first_split = (sem("fixed_rows_hi"), sem("fixed_rows_lo"), sem("first_head_hi"),
                                                 sem("first_head_split"))
        at_s, at_t, at_pv = sem("at_scores"), sem("at_turned"), sem("at_pv")
        at_nm, at_r, at_p, at_lo, at_olo = (sem("at_negmax"), sem("at_rinv"), sem("at_probs"),
                                            sem("at_pt_lo"), sem("at_o_lo"))
        at_e, at_hi, at_ohi = sem("at_exp"), sem("at_pt_hi"), sem("at_o_hi")
        fences = {e: sem(f"fence_{e}") for e in ("pe", "act", "dve", "pool", "sp")}

        def fence(eng, me, n):
            eng.drain().then_inc(fences[me], 1)
            for e, s in fences.items():
                if e != me:
                    eng.wait_ge(s, n)

        def rows_ready(key):
            k = NORM_AT[key]
            return (n_done_pool, POOL_COUNT[k]) if POOL_LOW[k] else (n_done, DVE_COUNT[k])

        def sum_bank(key):
            return 5 if key[0] in ("s3", "s6") else 7

        def bank(g):
            return g % LBANKS

        kA, vA, qA, qB, nck = io["kA"], io["vA"], io["qA"], io["qB"], io["nck"]

        def turned(c, buf):
            _, i, _, n, _ = chunk(c)
            v = ps[:, 4 + c % 2, :].rearrange("p (t q) -> p t q", q=P)
            if i < 8:
                return [(buf[:, turn_slot(c), 0:n, :], v[:, 0:n, :])]
            return [(buf[:, turn_slot(c), 0:2, 0:DEC], v[:, 0:2, 0:DEC]),
                    (buf[0:DEC, turn_slot(c), 2, 0:DEC], v[0:DEC, 2, 0:DEC])]

        def out_part(c, i, buf):
            _, tile, _, _, last = chunk(c)
            hp = c // HC
            rows = slice(64 * (hp % 2), 64 * (hp % 2) + 64)
            pair = i + (-1 if c < 0 else 0)
            part = OUT_AFTER[tile]
            cols, src = ((slice(SEQ, T), ps[0:VD, 7, 0:DEC]) if tile == 8 else
                         (slice(512, SEQ), ps[0:VD, 7, :]) if tile > 3 else (slice(0, 512), ps[0:VD, 6, :]))
            return buf[rows, pair, cols], src, 3 * hp + part + 1

        def score_tile(tile):
            M = P if tile < 8 else DEC
            return ps[0:M, 0:4, :].rearrange("p a b -> p (a b)")[:, 512 * S_BANK[tile]:512 * S_BANK[tile] + KEYS[tile]]

        def is_out(c):
            return chunk(c)[4] and chunk(c)[1] in OUT_AFTER

        def head_parts(layer, parity):
            krows = NOPE if layer == 0 else HD + 1
            qrows = P if layer == 0 else HD
            rows = [(qh[0:qrows, parity, :], ql[0:qrows, parity, :], qraw[0:qrows, :], qrows, T),
                    (kh[0:krows, parity, :], kl[0:krows, parity, :], kraw[0:krows, :], krows, TK)]
            values = [(vh[:, parity, 0:KT - 1, :], vl[:, parity, 0:KT - 1, :], vraw[:, 0:KT - 1, :], P, 0),
                      (vh[0:TK % P, parity, KT - 1, :], vl[0:TK % P, parity, KT - 1, :],
                       vraw[0:TK % P, KT - 1, :], TK % P, VD)]
            return rows, values

        block = ctx.enter_context(nc.Block())

        @block.sync
        def _(sp):
            def load_unit(name, slot, use, unit):
                if not (isinstance(use, int) and use == 0):
                    sp.wait_ge(w_rdy[slot], use)
                sp.dma_start(wraw[:, slot, :], io["units"][unit]).then_inc(w_raw[slot], 16)

            def lin_load(name, j):
                slot, use, _ = USES[name, j]
                load_unit(name, slot, use, UNIT0[name] + j)

            def lin_load_pair(name, i):
                for s in range(2):
                    load_unit(name, s, i + USED[name][s], i * 2 + (UNIT0[name] + s))

            sp.dma_start(gains[:], io["gains"]).then_inc(const_in, 16)
            sp.dma_start(ident[:], io["ident"]).then_inc(const_in, 16)
            for b in range(NB):
                sp.dma_start(res[:, :, b * TB:(b + 1) * TB], io["xT"][:, :, b * TB:(b + 1) * TB]).then_inc(x_in[b], 16)
                if b == 0:
                    lin_load("dq", 0)
                    lin_load("dq", 1)
            sp.dma_start(wraw[:, 2, 0:2 * P], io["masks"]).then_inc(const_in, 16)
            sp.dma_start(cc[:], io["cckvT"]).then_inc(cache_in, 16)
            lin_load("dq", 2)
            lin_load("dq", 3)
            for name in ("dkv", "kr"):
                for j in range(dict((n, c) for n, c, _ in LIN)[name]):
                    lin_load(name, j)
            sp.wait_ge(n_done, NB)
            sp.dma_start(krt[:], io["krt"]).then_inc(tab_in, 16)
            lin_load("uk", 0)
            lin_load("uk", 1)
            sp.wait_ge(kr_done, NB)
            sp.dma_start(io["kr_out"], krf[:]).then_inc(kr_out, 16)
            sp.wait_ge(n_ap, 2 * NORM_AT["s1", "kv", 2] + 2)
            sp.dma_start(io["ckv_out"], y[:, 6:8, :]).then_inc(ckv_out, 16)
            fence(sp, "sp", 1)
            sp.dma_start(cs[:], io["cs"]).then_inc(tab_in, 16)

            def store(slot, dst, src, waits, count=1):
                for s, v in waits:
                    sp.wait_ge(s, v)
                sp.dma_start(dst, src).then_inc(st_out[slot], 16)

            for m in range(8):
                if m < 2:
                    lin_load("uv", m)
                store(m % 2, kA[m * P:(m + 1) * P, :], stg[:, m % 2, :], [(lin_ev, GROUP0["uk"] + KB * (m + 1))])
            lin_load("uq", 0)
            lin_load("uq", 1)
            for g in range(2 * KT):
                half, kt = g // KT, g % KT
                rows = min(P, TK - kt * P)
                store(g % 2, vA[kt * P:kt * P + rows, half * 512:(half + 1) * 512], stg[0:rows, g % 2, 0:512],
                      [(lin_ev, GROUP0["uv"] + g + 1)])
            with sp.Fori(0, 3) as i:
                for s in range(2):
                    load_unit("uq", s, i + (USED["uq"][s] + 1), i * 2 + (UNIT0["uq"] + 2 + s))
                for h in range(4):
                    sp.wait_ge(q_done, i * 12 + NB * (h + 1))
                    sp.dma_start(qA[i * 4 + h], stg[:, h % 2, 0:T]).then_inc(st_out[h % 2], 16)
            def attn_loads(layer, h, kv, after=None):
                if after is not None:
                    sp.wait_ge(at_split, after)
                if layer == 0:
                    sp.dma_start(qraw[:], qA[h]).then_inc(at_raw, 16)
                    sp.dma_start(kraw[0:NOPE, :], io["kA_h"][h]).then_inc(at_raw, 16)
                else:
                    sp.dma_start(kraw[0:HD, 0:T], io["kT_h"][kv]).then_inc(at_raw, 16)
                    sp.dma_start(kraw[0:HD, T:TK], io["ckT"][kv]).then_inc(at_raw, 16)
                    sp.dma_start(qraw[0:HD, :], qB[h]).then_inc(at_raw, 16)
                    sp.dma_start(kraw[HD:HD + 1, :], nck[h]).then_inc(at_raw, 16)
                if after is not None:
                    sp.wait_ge(at_vsplit, after)
                if layer == 0:
                    sp.dma_start(vraw[:, 0:KT - 1, :], io["vA_full"][h]).then_inc(at_vraw, 16)
                    sp.dma_start(vraw[0:TK % P, KT - 1, :], io["vA_last"][h]).then_inc(at_vraw, 16)
                else:
                    sp.dma_start(vraw[:, 0:8, :], io["v_full"][kv]).then_inc(at_vraw, 16)
                    sp.dma_start(vraw[0:DEC, 8, :], io["v_new"][kv]).then_inc(at_vraw, 16)
                    sp.dma_start(vraw[DEC:P, 8, :], io["cv0"][kv]).then_inc(at_vraw, 16)
                    sp.dma_start(vraw[:, 9, :], io["cv1"][kv]).then_inc(at_vraw, 16)
                    sp.dma_start(vraw[0:DEC, 10, :], io["cv2"][kv]).then_inc(at_vraw, 16)

            def first_units(name, splits):
                sp.wait_ge(at_vsplit, splits)
                for j in range(2):
                    lin_load(name, j)

            for s in range(2):
                sp.wait_ge(w_rdy[s], USED["oa"][s])
            sp.wait_ge(const_r, 1)
            sp.wait_ge(st_out[0], 16 * (4 + KT + 1))
            sp.wait_ge(st_out[1], 16 * (4 + KT))
            sp.wait_ge(kr_out, 16)
            for r in range(2):
                rows = slice(NOPE + r * ROPE, NOPE + (r + 1) * ROPE)
                sp.dma_start(kraw[rows, 0:T], io["kr_out"]).then_inc(at_kr, 16)
                sp.dma_start(kraw[rows, T:TK], io["ckrT"]).then_inc(at_kr, 16)
            attn_loads(0, 0, None)
            for h in range(4):
                sp.wait_ge(q_done, 36 + NB * (h + 1))
                sp.dma_start(qA[12 + h], stg[:, h % 2, 0:T]).then_inc(st_out[h % 2], 16)
            for s in range(2):
                sp.wait_ge(st_out[s], 16 * (4 + KT + 8))
            sp.wait_ge(ckv_out, 16)
            fence(sp, "sp", 2)
            sp.wait_ge(first_split, 1)
            attn_loads(0, 1, None)
            with sp.Fori(2, H) as h:
                attn_loads(0, h, None, h - 1)
            first_units("oa", H - 1)
            fence(sp, "sp", 3)

            def blockwise_loads(name, begun=False):
                if begun:
                    for j in range(2, 4):
                        lin_load(name, j)
                else:
                    with sp.Fori(0, 2) as i:
                        lin_load_pair(name, i)
                for j in range(4, 8):
                    lin_load(name, j)

            def tail_loads(layer):
                blockwise_loads(("oa", "ob")[layer], True)
                name = f"ffn{layer}"
                u0 = UNIT0[name]
                for s in range(2):
                    load_unit(name, s, USED[name][s], u0 + s)
                with sp.Fori(0, NF - 1) as f:
                    for k, (s, df) in enumerate(((0, 1), (2, 0), (1, 1))):
                        load_unit(name, s, f + (USED[name][s] + df), f * 3 + (u0 + 2 + k))
                load_unit(name, 2, USED[name][2] + NF - 1, u0 + 3 * NF - 1)
                for j in range(2):
                    lin_load(f"pe{layer}", j)
                sp.wait_ge(fd_rd, 24 * NF * (layer + 1))
                sp.dma_start(praw[:], io["pT"][layer]).then_inc(p_in, 16)
                blockwise_loads(f"pg{layer}")

            tail_loads(0)

            for j in range(2):
                lin_load("kb", j)
            fence(sp, "sp", 4)
            for name, j in (("wf", 0), ("vb", 0), ("vb", 1)):
                lin_load(name, j)
            sp.dma_start(flog[:, T:TK], io["clfT"]).then_inc(cache_in, 16)
            for m in range(2):
                store(m, io["kT_out"][m * P:(m + 1) * P, :], stg[:, m, 0:T], [(lin_ev, GROUP0["kb"] + NB * (m + 1))])
            lin_load("qb", 0)
            for tt in range(9):
                rows = min(P, T - tt * P)
                store(tt % 2, io["v_out"][tt * P:tt * P + rows, :], stg[0:rows, tt % 2, 0:KVH * HD],
                      [(lin_ev, GROUP0["vb"] + tt + 1)])
                if tt == 4:
                    lin_load("qb", 1)
            sp.wait_ge(fx_v, 6)
            sp.dma_start(io["lf_out"], flog[:, 0:T]).then_inc(lf_out, 16)
            sp.wait_ge(fx_v, 10)
            sp.dma_start(io["nck_all"], fcum[:]).then_inc(nck_out, 16)
            with sp.Fori(0, 3) as i:
                for s in range(2):
                    load_unit("qb", s, i + (USED["qb"][s] + 1), i * 2 + (UNIT0["qb"] + 2 + s))
                for m in range(2):
                    sp.wait_ge(lin_ev, i * 6 + (GROUP0["qb"] + NB * (m + 1)))
                    sp.dma_start(io["qB_pair"][i * 2 + m], stg[:, m, 0:T]).then_inc(st_out[m], 16)
            for s in range(2):
                sp.wait_ge(w_rdy[s], USED["ob"][s])
            sp.wait_ge(st_out[0], 16 * (4 + KT + 8 + 1 + 5 + 1))
            sp.wait_ge(st_out[1], 16 * (4 + KT + 8 + 1 + 4))
            sp.wait_ge(nck_out, 16)
            attn_loads(1, 0, 0)
            for m in range(2):
                sp.wait_ge(lin_ev, 18 + (GROUP0["qb"] + NB * (m + 1)))
                sp.dma_start(io["qB_pair"][6 + m], stg[:, m, 0:T]).then_inc(st_out[m], 16)
            for s in range(2):
                sp.wait_ge(st_out[s], 16 * (4 + KT + 8 + 1 + (5 - s) + 4))
            sp.wait_ge(lf_out, 16)
            fence(sp, "sp", 5)
            sp.wait_ge(first_split, 2)
            attn_loads(1, 1, 0)
            for h in range(2, 4):
                attn_loads(1, h, 0, H - 1 + h - 1)
            with sp.Fori(1, KVH) as kv:
                for g in range(4):
                    attn_loads(1, kv * 4 + g, kv, kv * 4 + (H - 1 + g - 1))
            first_units("ob", 2 * H - 2)
            fence(sp, "sp", 6)
            tail_loads(1)
            for b in range(NB):
                sp.wait_ge(r_done, 2 * POST_COUNT[NORM_AT["s7", "post", b]])
                sp.dma_start(io["yT"][:, :, b * TB:(b + 1) * TB], res[:, :, b * TB:(b + 1) * TB]).then_inc(y_out, 16)
            sp.wait_ge(y_out, 16 * NB)

        @block.gpsimd
        def _(pool):
            LAST = {}

            def split(slot, use, gain, gained=None, free=None):
                raw = wraw[:, slot, :]
                pool.wait_ge(w_raw[slot], use * 16 + 16)
                if gain is not None:
                    g = gains[:, GAIN_AT[gain]:GAIN_AT[gain] + 8].unsqueeze(2).to_broadcast((P, 8, P))
                    raw8 = raw.rearrange("p (k m) -> p k m", k=8)
                    pool.tensor_tensor(raw8, raw8, g, ALU.mult).then_inc(w_gain[slot], 1)
                    pool.wait_ge(w_gain[slot], gained + 1)
                if free is not None:
                    pool.wait_ge(*free)
                pool.tensor_tensor(wh[:, slot, :], raw, ones[:, 0:1].to_broadcast((P, UW)), ALU.mult).then_inc(w_hi[slot], 1)
                pool.wait_ge(w_hi[slot], use + 1)
                pool.tensor_tensor(wl[:, slot, :], raw, wh[:, slot, :].bitcast(F32), ALU.subtract).then_inc(w_rdy[slot], 1)

            def lin_split(name, j, gain):
                s = j % 2
                split(s, USED[name][s] + j // 2, gain, GAINED[name][s] + j // 2, LAST.get(s))
                LAST[s] = (lin_rd, group_after(name, s, j // 2))

            def blockwise_splits(name, gain):
                for j in range(8):
                    slot, use, gained = USES[name, j]
                    split(slot, use, gain, gained, LAST.get(slot))
                    done = NB * (j + 1) if j < 5 else 5 * NB + 2 * NB + (j - 5) + 1
                    LAST[slot] = (lin_rd, GROUP0[name] + done)

            def lin_split_loop(name, gain, n=4):
                for s in range(2):
                    split(s, USED[name][s], gain, GAINED[name][s], LAST.get(s))
                with pool.Fori(1, n) as i:
                    for s in range(2):
                        split(s, i + USED[name][s], gain, i + GAINED[name][s],
                              (lin_rd, (i - 1) * (2 * PER_UNIT[name]) + group_after(name, s, 0)))
                for s in range(2):
                    LAST[s] = (lin_rd, group_after(name, s, n - 1))

            def low(s, b):
                k = NORM_AT[s, "pre", b]
                c = slice(b * TB, (b + 1) * TB)
                pool.wait_ge(n_hi, 2 * HI_COUNT[k])
                pool.tensor_tensor(nl[:, :, c], y[:, :, c], nh[:, :, c].bitcast(F32), ALU.subtract).then_inc(n_done_pool, 1)

            def attn_split(layer, parity, h, first):
                rows, values = head_parts(layer, parity)
                for parts, raw_in, landed, used, per_head, half, done in (
                        (rows, at_raw, (32, 64), at_s, STEPS, at_khi, at_split),
                        (values, at_vraw, (32, 80), at_pv, HC, at_vhi, at_vsplit)):
                    n = landed[layer]
                    pool.wait_ge(raw_in, h * n + n + layer * H * (landed[0] - landed[1]))
                    if not first:
                        pool.wait_ge(used, h * per_head - per_head)
                    for hi, lo, raw, m, w in parts:
                        one = (ones[0:m, 0:1].to_broadcast((m, w)) if w else
                               ones[:, 0:1].unsqueeze(2).to_broadcast((P, KT - 1, VD)))
                        last = pool.tensor_tensor(hi, raw, one, ALU.mult)
                    last.then_inc(half, 1)
                    pool.wait_ge(half, h - layer)
                    for hi, lo, raw, m, w in parts:
                        last = pool.tensor_tensor(lo, raw, hi.bitcast(F32), ALU.subtract)
                    last.then_inc(done, 1)

            pool.wait_ge(const_in, 48)
            pool.wait_ge(ones_set, 1)
            for j in range(4):
                lin_split("dq", j, "mix_pre0")
            for j in range(2):
                lin_split("dkv", j, "mix_pre0")
            lin_split("kr", 0, "mix_pre0")
            for j in range(2):
                lin_split("uk", j, None)
            fence(pool, "pool", 1)
            for j in range(2):
                lin_split("uv", j, None)
            lin_split_loop("uq", "q")
            fence(pool, "pool", 2)

            attn_split(0, 1, 1, True)
            with pool.Fori(1, H // 2) as i:
                for b in range(2):
                    attn_split(0, b, i * 2 + b, False)
            fence(pool, "pool", 3)

            def tail_splits(layer):
                blockwise_splits(("oa", "ob")[layer], None)
                name, gain = f"ffn{layer}", f"ffn_pre{layer}"
                u, g = USED[name], GAINED[name]
                f0 = layer * NF
                for s in range(2):
                    split(s, u[s], gain, g[s], LAST[s])
                    low(f"s{2 + 3 * layer}", s)

                def tile(f, down_free):
                    split(0, f + (u[0] + 1), gain, f + (g[0] + 1), (fg_rd, f * 3 + (3 * f0 + 3)))
                    split(2, f + u[2], None, None, down_free)
                    split(1, f + (u[1] + 1), gain, f + (g[1] + 1), (fu_rd, f * 3 + (3 * f0 + 3)))

                tile(0, LAST.get(2))
                with pool.Fori(1, NF - 1) as f:
                    tile(f, (fd_rd, f * 24 + 24 * f0))
                split(2, u[2] + NF - 1, None, None, (fd_rd, 24 * (f0 + NF - 1)))
                LAST[0], LAST[1] = (fg_rd, 3 * (f0 + NF)), (fu_rd, 3 * (f0 + NF))
                LAST[2] = (fd_rd, 24 * (f0 + NF))
                for j in range(2):
                    lin_split(f"pe{layer}", j, None)
                    low(f"s{3 + 3 * layer}", j)
                blockwise_splits(f"pg{layer}", f"ple_gate{layer}")

            tail_splits(0)
            for j in range(2):
                lin_split("kb", j, "shared")
                low("s4", j)
            fence(pool, "pool", 4)
            lin_split("wf", 0, "shared")
            for j in range(2):
                lin_split("vb", j, ("shared_v", "shared_v2")[j])
            lin_split_loop("qb", "mix_pre1")
            fence(pool, "pool", 5)
            attn_split(1, 1, H + 1, True)
            with pool.Fori(1, H // 2) as i:
                for b in range(2):
                    attn_split(1, b, i * 2 + (H + b), False)
            fence(pool, "pool", 6)
            tail_splits(1)

        @block.tensor
        def _(pe):
            def three(out, ah, al, bh, bl, first, last):
                nc.tensor.matmul(out, ah, bh, start=first, stop=False)
                nc.tensor.matmul(out, ah, bl, start=False, stop=False)
                return nc.tensor.matmul(out, al, bh, start=False, stop=last)

            def wcols(slot, c0, n):
                return wh[:, slot, c0:c0 + n], wl[:, slot, c0:c0 + n]

            def bank_free(g):
                if not isinstance(g, int) or g >= LBANKS:
                    pe.wait_ge(lin_ev, g - (LBANKS - 1))

            def lin_unit(g0, b0, slot, use, xh, xl, K, heads, M, blocks, first_waits=()):
                pe.wait_ge(w_rdy[slot], use + 1)
                n = 0
                for m in range(heads):
                    for b, (c, w) in enumerate(blocks):
                        if m == 0 and first_waits:
                            for s, v in first_waits[b]:
                                pe.wait_ge(s, v)
                        bank_free(g0 + n)
                        out = ps[0:M, (b0 + n) % LBANKS, 0:w]
                        for k in range(K):
                            ah, al = wcols(slot, (m * K + k) * P, M)
                            mm = three(out, ah, al, xh[:, k, c:c + w], xl[:, k, c:c + w], k == 0, k == K - 1)
                        n += 1
                        mm.then_inc(lin_rd, 1)

            TBL = [(b * TB, TB) for b in range(NB)]

            def lin_static(name, xh, xl, K=8, heads=1, M=P, blocks=TBL, waits=()):
                n = {nm: c for nm, c, _ in LIN}[name]
                per = heads * len(blocks)
                for j in range(n):
                    g = GROUP0[name] + j * per
                    lin_unit(g, g, j % 2, USED[name][j % 2] + j // 2, xh, xl, K, heads, M, blocks,
                             waits if j == 0 else ())

            def lin_loop(name, xh, xl, K=8, heads=1, waits=()):
                per = heads * NB
                for b in waits:
                    for s, v in b:
                        pe.wait_ge(s, v)
                with pe.Fori(0, 4) as i:
                    for s in range(2):
                        g = GROUP0[name] + s * per
                        lin_unit(i * (2 * per) + g, g, s, i + USED[name][s], xh, xl, K, heads, P, TBL)

            def norm(key, K):
                k = NORM_AT[key]
                if k:
                    pe.wait_ge(n_rt, k)
                for j in range(K):
                    if j % (K // 2) == 0:
                        pe.wait_ge(n_sq, 2 * k + 1 + j // (K // 2))
                    mm = nc.tensor.matmul(ps[:, sum_bank(key), 0:TB], ones[:], sq[:, k % 2, j, :], start=(j == 0),
                                          stop=(j == K - 1))
                mm.then_inc(n_mm, 1)

            def blockwise(name, xh, xl, s, waits=()):
                for b in waits:
                    for sm, v in b:
                        pe.wait_ge(sm, v)
                with pe.Fori(0, 2) as i:
                    for slot in range(2):
                        g = GROUP0[name] + slot * NB
                        lin_unit(i * (2 * NB) + g, g, slot, i + USED[name][slot], xh, xl, 8, 1, P, TBL)
                g = GROUP0[name] + 4 * NB
                slot, use, _ = USES[name, 4]
                lin_unit(g, g, slot, use, xh, xl, 8, 1, P, TBL)
                for b in range(NB):
                    for u in range(5, 8):
                        g = GROUP0[name] + 5 * NB + b * NB + (u - 5)
                        slot, use, _ = USES[name, u]
                        lin_unit(g, g, slot, use, xh, xl, 8, 1, P, TBL[b:b + 1])
                        if b and u == 5:
                            norm((s, "post", b - 1), KD)

            def n_ready(s, kind="pre"):
                return [[rows_ready((s, kind, b))] for b in range(NB)]

            pe.wait_ge(ones_set, 1)
            for b in range(NB):
                norm(("s0", "pre", b), KD)
            lin_static("dq", nh, nl, waits=n_ready("s0"))
            lin_static("dkv", nh, nl)
            lin_static("kr", nh, nl, M=2 * ROPE)
            for kind, K in (("q", 4), ("kv", 2)):
                for b in range(NB):
                    norm(("s1", kind, b), K)
            fence(pe, "pe", 1)
            KBL = [(b * TKB, TKB) for b in range(KB)]
            lin_static("uk", cvh, cvl, K=2, heads=4, blocks=KBL)
            for half in range(2):
                pe.wait_ge(w_rdy[half], USED["uv"][half] + 1)
                for kt in range(KT):
                    g = GROUP0["uv"] + half * KT + kt
                    rows = min(P, TK - kt * P)
                    bank_free(g)
                    for k in range(2):
                        c = slice(kt * P, kt * P + rows)
                        bh, bl = wcols(half, k * 512, 512)
                        mm = three(ps[0:rows, bank(g), :], cvh[:, k, c], cvl[:, k, c], bh, bl, k == 0, k == 1)
                    mm.then_inc(lin_rd, 1)
            lin_loop("uq", nh, nl, K=4, heads=2)
            fence(pe, "pe", 2)

            def attn_pe(layer):
                rows = P if layer == 0 else HD + 1

                base_n = layer * H * STEPS

                def scores(pair_no, s, first):
                    hp, i = s // STEPS, ORDER[s % STEPS]
                    if first and s == 0:
                        pe.wait_ge(first_split, layer + 1)
                        pe.wait_ge(fix_lo, layer + 1)
                    elif s % STEPS == 0:
                        pe.wait_ge(at_split, pair_no * 2 + (layer * (H - 1) + hp))
                    if not (first and banks_before(s) < 0):
                        pe.wait_ge(at_e, pair_no * PAIR + (base_n + banks_before(s) + 1))
                    qc = slice(i * P, i * P + (P if i < 8 else DEC))
                    M = P if i < 8 else DEC
                    k0, k1 = (0, (i + 1) * P) if i < 8 else (SEQ, TK)
                    buf = S_BANK[i]
                    masked = i < 8 or layer == 1
                    nb = 0
                    c = k0
                    while c < k1:
                        w = min(512, k1 - c)
                        out = ps[0:M, buf + nb, 0:w]
                        dg = masked and (c + w == k1 if i < 8 else c == k0)
                        mm = three(out, qh[0:rows, hp, qc], ql[0:rows, hp, qc], kh[0:rows, hp, c:c + w],
                                   kl[0:rows, hp, c:c + w], True, not dg)
                        if dg:
                            dc = w - P if i < 8 else 0
                            mm = nc.tensor.matmul(ps[0:M, buf + nb, dc:dc + M], ident_r[0:M, 0:M],
                                                  mask_r[0:M, layer, 0:M], start=False, stop=True)
                        c += w
                        nb += 1
                    mm.then_inc(at_s, 1)

                base_c = layer * H * HC

                def turn_waits(i, c, first):
                    s, _, k0, _, _ = chunk(c)
                    if k0 == 0:
                        pe.wait_ge(at_p, i * PAIR + (base_n + s + 1))
                    if not (first and c < 2):
                        pe.wait_ge(at_lo, i * (2 * HC) + (base_c + c - 1))

                def turn(i, c, first):
                    s, tile, k0, n, _ = chunk(c)
                    M = P if tile < 8 else DEC
                    if tile < 8:
                        turn_waits(i, c, first)
                    for j in range(n):
                        kt = k0 + j
                        kr = P if (tile < 8 or kt < 2) else DEC
                        mm = nc.tensor.transpose(ps[0:kr, 4 + c % 2, j * P:j * P + M],
                                                 pr[0:M, PROB_AT[tile] + kt * P:PROB_AT[tile] + kt * P + kr],
                                                 ident[0:M, 0:M])
                    mm.then_inc(at_t, 1)

                def pv(i, c, first):
                    _, tile, k0, n, last = chunk(c)
                    hp = c // HC
                    if k0 == 0:
                        need = part_needed(tile, hp)
                        if need is not None and not (first and need <= 0):
                            pe.wait_ge(at_olo, i * 6 + (3 * layer * H + need))
                    if c % HC == 0 and not (first and c == 0):
                        pe.wait_ge(at_vsplit, i * 2 + (layer * (H - 1) + hp))
                    pe.wait_ge(at_lo, i * (2 * HC) + (base_c + c + 1))
                    M = P if tile < 8 else DEC
                    if tile < 8:
                        out = ps[0:VD, 6 + tile // 4, (tile % 4) * P:(tile % 4 + 1) * P]
                    else:
                        out = ps[0:VD, 7, 0:DEC]
                    for j in range(n):
                        kt = k0 + j
                        kr = P if (tile < 8 or kt < 2) else DEC
                        vt = kt if tile < 8 else 8 + kt
                        mm = three(out, vh[0:kr, hp % 2, vt, :], vl[0:kr, hp % 2, vt, :], pth[0:kr, turn_slot(c), j, 0:M],
                                   ptl[0:kr, turn_slot(c), j, 0:M], kt == 0, last and j == n - 1)
                    mm.then_inc(at_pv, 1)

                def pair(i, first, drain=False):
                    for s in range(T_LAG if drain else PAIR):
                        if not drain:
                            scores(i, s, first)
                        for c in chunks_of(s - T_LAG):
                            if c < 0 and first:
                                continue
                            sample = chunk(c)[1] == 8
                            if sample:
                                turn_waits(i, c, first)
                                pv(i, c - PV_LAG, first)
                            turn(i, c, first)
                            if (c >= PV_LAG or not first) and not sample:
                                pv(i, c - PV_LAG, first)
                    if drain:
                        for c in range(-PV_LAG, 0):
                            pv(i, c, False)

                pair(0, True)
                with pe.Fori(1, H // 2) as i:
                    pair(i, False)
                pair(H // 2, False, True)

            attn_pe(0)
            fence(pe, "pe", 3)

            def ffn_pe(layer):
                name = f"ffn{layer}"
                u = USED[name]
                f0 = layer * NF

                def down(f, par, d, blocks_first=False):
                    m, b = (d % KD, d // KD) if blocks_first else (d // NB, d % NB)
                    if d == 0:
                        pe.wait_ge(w_rdy[2], f + (u[2] + 1))
                        pe.wait_ge(f_lo, f * 3 + (3 * f0 + 3))
                    if not (isinstance(f, int) and f == 0 and layer == 0 and d < 2):
                        pe.wait_ge(f_acc, f * 24 + (24 * f0 + d - 1))
                    mm = three(ps[:, 6 + d % 2, 0:TB], wh[:, 2, m * P:(m + 1) * P], wl[:, 2, m * P:(m + 1) * P],
                               hh[par][:, b * TB:(b + 1) * TB], hl[par][:, b * TB:(b + 1) * TB], True, True)
                    mm.then_inc(fd_rd, 1)

                def products(f, slot, b, first=False, among=lambda n: None):
                    rd, freed = ((fg_rd, f_sg), (fu_rd, f_u))[slot]
                    if not (first and layer == 0):
                        pe.wait_ge(freed, f * 3 + (3 * f0 + b - 2))
                    for k in range(KD):
                        xh, xl = nh[:, k, b * TB:(b + 1) * TB], nl[:, k, b * TB:(b + 1) * TB]
                        ah, al = wcols(slot, k * P, P)
                        for pas, (a, x) in enumerate(((ah, xh), (ah, xl), (al, xh))):
                            mm = nc.tensor.matmul(ps[:, 3 * slot + b, 0:TB], a, x, start=(k == 0 and pas == 0),
                                                  stop=(k == KD - 1 and pas == 2))
                            if k == KD - 1 and pas == 2:
                                mm.then_inc(rd, 1)
                            among((slot * NB + b) * 3 * KD + 3 * k + pas + 1)

                def first_tile():
                    key = f"s{2 + 3 * layer}"
                    norm((key, "pre", 0), KD)
                    norm((key, "post", 2), KD)
                    norm((key, "pre", 1), KD)
                    norm((key, "pre", 2), KD)
                    for slot in range(2):
                        pe.wait_ge(w_rdy[slot], u[slot] + 1)
                    pe.wait_ge(lin_ev, GROUP0[f"pe{layer}"])
                    for b in range(NB):
                        pe.wait_ge(*rows_ready((key, "pre", b)))
                        for slot in range(2):
                            products(0, slot, b, True)

                def tile(f, par):
                    def among(n):
                        if n in D_AT:
                            down(f - 1, 1 - par, D_AT.index(n))

                    for slot in range(2):
                        pe.wait_ge(w_rdy[slot], f + (u[slot] + 1))
                        for b in range(NB):
                            products(f, slot, b, False, among)

                first_tile()
                tile(1, 1)
                with pe.Fori(1, NF // 2) as i:
                    for par in range(2):
                        tile(i * 2 + par, par)
                for d in range(24):
                    down(NF - 1, (NF - 1) % 2, d, True)
                    if d == 15:
                        pe.wait_ge(f_u, 3 * (f0 + NF))
                        norm((f"s{3 + 3 * layer}", "post", 0), KD)

            def tail_pe(layer):
                s0 = 2 + 3 * layer
                blockwise(("oa", "ob")[layer], nh, nl, f"s{s0}")
                ffn_pe(layer)
                pe.wait_ge(f_acc, 24 * NF * (layer + 1))
                for kind, b in CHAIN[1:]:
                    norm((f"s{s0 + 1}", kind, b), KD)
                pe.wait_ge(*rows_ready((f"s{s0 + 1}", "pre", 1)))
                pe.wait_ge(p_lo, layer + 1)
                lin_static(f"pe{layer}", ph, pl, K=2, heads=4)
                blockwise(f"pg{layer}", nh, nl, f"s{s0 + 2}", waits=n_ready(f"s{s0 + 1}"))

            tail_pe(0)
            for kind, b in CHAIN[2:]:
                norm(("s4", kind, b), KD)
            fence(pe, "pe", 4)
            lin_static("kb", nh, nl)
            lin_static("wf", nh, nl, M=H)
            for j in range(2):
                pe.wait_ge(w_rdy[j], USED["vb"][j] + 1)
            for tt in range(9):
                g = GROUP0["vb"] + tt
                rows = min(P, T - tt * P)
                bank_free(g)
                for k in range(KD):
                    bh, bl = wcols(k // 4, (k % 4) * KVH * HD, KVH * HD)
                    c = slice(tt * P, tt * P + rows)
                    mm = three(ps[0:rows, bank(g), 0:KVH * HD], nh[:, k, c], nl[:, k, c], bh, bl, k == 0, k == KD - 1)
                mm.then_inc(lin_rd, 1)
            lin_loop("qb", nh, nl)
            fence(pe, "pe", 5)
            attn_pe(1)
            fence(pe, "pe", 6)
            tail_pe(1)
            norm(("s7", "post", 2), KD)

        @block.scalar
        def _(act):
            def take(g, b, out, rows, w, func=ACT.Copy, **kw):
                act.wait_ge(lin_rd, g + 1)
                nc.scalar.activation(out, ps[0:rows, b, 0:w], func, **kw).then_inc(lin_ev, 1)

            SRC = {"q": (0, 4), "kv": (4, 2)}

            def squares(key, waits):
                k = NORM_AT[key]
                s, kind, b = key
                if k >= 2:
                    act.wait_ge(n_mm, k - 1)
                c = slice(b * TB, (b + 1) * TB)
                k0, K = SRC.get(kind, (0, KD))
                src = res if kind == "pre" else y
                for (j0, j1), half_waits in zip(halves(K), waits):
                    for sm, v in half_waits:
                        act.wait_ge(sm, v)
                    nc.scalar.activation(sq[:, k % 2, j0:j1, :], src[:, k0 + j0:k0 + j1, c], ACT.Square).then_inc(n_sq, 1)

            def root(key):
                k = NORM_AT[key]
                width = {"q": Q_RANK, "kv": KV_RANK}.get(key[1], D)
                act.wait_ge(n_mm, k + 1)
                if k >= 2:
                    act.wait_ge(n_rs, k - 1)
                nc.scalar.activation(rt[:, k % 2, :], ps[:, sum_bank(key), 0:TB], ACT.Sqrt, bias=epsc[:, 0:1],
                                     scale=1.0 / width).then_inc(n_rt, 1)

            def high(key):
                k = NORM_AT[key]
                _, kind, b = key
                if kind != "post":
                    c = slice(b * TB, (b + 1) * TB)
                    out, src, K = {"kv": (cvh, y[:, 6:8], 2), "q": (nh, y, 4), "pre": (nh, y, KD)}[kind]
                    for h, (j0, j1) in enumerate(halves(K)):
                        act.wait_ge(n_ap, 2 * k + 1 + h)
                        nc.scalar.activation(out[:, j0:j1, c], src[:, j0:j1, c], ACT.Copy).then_inc(n_hi, 1)

            def link(before, key, behind, waits):
                late = behind and key[0] != "s0" and (key[1], behind[1]) == ("pre", "pre")
                if behind and not late:
                    squares(behind, waits(behind))
                if before and not behind:
                    high(before)
                root(key)
                if late:
                    squares(behind, waits(behind))
                if before and behind:
                    high(before)

            def norms(keys, waits):
                squares(keys[0], waits(keys[0]))
                for before, key, behind in zip([None] + keys, keys, keys[1:] + [None]):
                    link(before, key, behind, waits)
                high(keys[-1])

            def norms_among(keys, last_groups, waits):
                last_groups(0)
                squares(keys[0], waits(keys[0]))
                last_groups(1)
                root(keys[0])
                squares(keys[1], waits(keys[1]))
                last_groups(2)
                for before, key, behind in zip(keys, keys[1:], keys[2:] + [None]):
                    link(before, key, behind, waits)
                high(keys[-1])

            def chain_waits(ready):
                def waits(key):
                    s, kind, b = key
                    if kind == "post":
                        return [ready[b], []]
                    n = POST_COUNT[NORM_AT[s, "post", b]]
                    return [[(r_done, 2 * n - 1)], [(r_done, 2 * n)]]
                return waits

            act.wait_ge(ones_set, 1)
            norms([("s0", "pre", b) for b in range(NB)], lambda key: [[(x_in[key[2]], 16)], []])
            act.wait_ge(const_r, 1)
            for m in range(6):
                for b in range(NB):
                    g = GROUP0["dq"] + m * NB + b
                    take(g, bank(g), y[:, m, b * TB:(b + 1) * TB], P, TB)
            for b in range(NB):
                g = GROUP0["kr"] + b
                take(g, bank(g), y[0:2 * ROPE, 6, b * TB:(b + 1) * TB], 2 * ROPE, TB)
            norms([("s1", "q", b) for b in range(NB)] + [("s1", "kv", b) for b in range(NB)],
                  lambda key: [[(lin_ev, GROUP0["kr"] + 3)], []])
            act.wait_ge(cache_in, 16)
            nc.scalar.activation(cvh[:, :, T:TK], cc[:], ACT.Copy).then_inc(cc_hi, 1)
            fence(act, "act", 1)
            for m in range(8):
                if m >= 2:
                    act.wait_ge(st_out[m % 2], 16 * (m // 2))
                for b in range(KB):
                    g = GROUP0["uk"] + m * KB + b
                    take(g, bank(g), stg[:, m % 2, b * TKB:(b + 1) * TKB], P, TKB)
            for g in range(2 * KT):
                rows = min(P, TK - (g % KT) * P)
                act.wait_ge(st_out[g % 2], 16 * (4 + g // 2))
                take(GROUP0["uv"] + g, bank(GROUP0["uv"] + g), stg[0:rows, g % 2, 0:512], rows, 512)
            with act.Fori(0, 4) as i:
                for h in range(4):
                    act.wait_ge(st_out[h % 2], i * 32 + 16 * (4 + KT + h // 2))
                    for b in range(NB):
                        g = GROUP0["uq"] + h * NB + b
                        take(i * 12 + g, bank(g), stg[:, h % 2, b * TB:(b + 1) * TB], P, TB)
            fence(act, "act", 2)

            def attn_act(layer):
                base_n, base_c = layer * H * STEPS, layer * H * HC

                def exps(i, s, first):
                    tile = ORDER[s % STEPS]
                    M = P if tile < 8 else DEC
                    k = s % STEPS
                    act.wait_ge(at_nm, i * PAIR + (base_n + s + 1))
                    if not (first and s < STEPS):
                        act.wait_ge(at_t, i * (2 * HC) + (base_c + chunks_of(s - STEPS)[-1] + 1))
                    nc.scalar.activation(pr[0:M, PROB_AT[tile]:PROB_AT[tile] + KEYS[tile]], score_tile(tile), ACT.Exp,
                                         bias=nmx[0:M, k:k + 1], accum_out=rsum[0:M, k:k + 1]).then_inc(at_e, 1)

                def hi(i, c, first):
                    act.wait_ge(at_t, i * (2 * HC) + (base_c + c + 1))
                    if not (first and slot_before(c) < 0):
                        act.wait_ge(at_pv, i * (2 * HC) + (base_c + slot_before(c) + 1))
                    for dst, src in turned(c, pth):
                        last = nc.scalar.activation(dst, src, ACT.Copy)
                    last.then_inc(at_hi, 1)

                def outs(i, c):
                    if is_out(c):
                        dst, src, _ = out_part(c, i, nh)
                        act.wait_ge(at_pv, i * (2 * HC) + (base_c + c + 1))
                        nc.scalar.activation(dst, src, ACT.Copy).then_inc(at_ohi, 1)

                def pair(i, first, drain=False):
                    for s in range(T_LAG if drain else PAIR):
                        todo = [] if drain else [s]
                        for c in chunks_of(s - T_LAG):
                            if c >= 0 or not first:
                                hi(i, c, first)
                            if c >= OUT_LAG or not first:
                                outs(i, c - OUT_LAG)
                            while todo:
                                exps(i, todo.pop(), first)
                    if drain:
                        for c in range(-OUT_LAG, 0):
                            outs(i, c)

                pair(0, True)
                with act.Fori(1, H // 2) as i:
                    pair(i, False)
                pair(H // 2, False, True)

            def first_head_hi(layer):
                act.wait_ge(at_raw, 32 if layer == 0 else 32 * H + 64)
                act.wait_ge(at_vraw, 32 if layer == 0 else 32 * H + 80)
                for hi, _, raw, _, _ in sum(head_parts(layer, 0), []):
                    last = nc.scalar.activation(hi, raw, ACT.Copy)
                last.then_inc(first_hi, 1)

            act.wait_ge(at_kr, 64)
            for b in range(2):
                last = nc.scalar.activation(kh[NOPE:P, b, :], kraw[NOPE:P, :], ACT.Copy)
            last.then_inc(fix_hi, 1)
            first_head_hi(0)
            attn_act(0)
            fence(act, "act", 3)

            def ffn_act(layer):
                f0 = layer * NF

                def tile(f, par, first):
                    for b in range(NB):
                        act.wait_ge(fg_rd, f * 3 + (3 * f0 + b + 1))
                        if not (first and layer == 0):
                            act.wait_ge(f_lo, f * 3 + (3 * f0 + b - 2))
                        nc.scalar.activation(sg[:, b, :], ps[:, b, 0:TB], ACT.Silu).then_inc(f_sg, 1)
                    for b in range(NB):
                        act.wait_ge(f_u, f * 3 + (3 * f0 + b + 1))
                        if not first:
                            if not (isinstance(f, int) and f + f0 < 2):
                                act.wait_ge(fd_rd, f * 24 + (24 * f0 - 24))
                        nc.scalar.activation(hh[par][:, b * TB:(b + 1) * TB], sg[:, b, :], ACT.Copy).then_inc(f_hi, 1)

                tile(0, 0, True)
                tile(1, 1, False)
                with act.Fori(1, NF // 2) as i:
                    for par in range(2):
                        tile(i * 2 + par, par, False)

            def tail_act(layer):
                s0 = 2 + 3 * layer
                name = ("oa", "ob")[layer]
                with act.Fori(0, 2) as i:
                    for s in range(2):
                        for b in range(NB):
                            g = GROUP0[name] + s * NB + b
                            take(i * 6 + g, bank(g), y[:, i * 2 + s, b * TB:(b + 1) * TB], P, TB)

                def last_groups(b):
                    for n in range(12 if b == 0 else 15 + 3 * b, 18 + 3 * b):
                        m, tb = group_place(n)
                        take(GROUP0[name] + n, bank(GROUP0[name] + n), y[:, m, tb * TB:(tb + 1) * TB], P, TB)

                norms_among([(f"s{s0}", k, b) for k, b in CHAIN], last_groups,
                            chain_waits([[(lin_ev, GROUP0[name] + 18 + 3 * b)] for b in range(NB)]))
                act.wait_ge(*rows_ready((f"s{s0}", "pre", 2)))
                ffn_act(layer)
                norms([(f"s{s0 + 1}", k, b) for k, b in CHAIN],
                      chain_waits([[(f_acc, 24 * (NF * (layer + 1) - 1) + KD * (b + 1))] for b in range(NB)]))
                act.wait_ge(p_in, 16 * (layer + 1))
                act.wait_ge(n_mm, NORM_AT[f"s{s0 + 1}", "pre", 1] + 1)
                nc.scalar.activation(ph[:], praw[:], ACT.Copy).then_inc(p_hi, 1)
                for m in range(8):
                    for b in range(NB):
                        g = GROUP0[f"pe{layer}"] + m * NB + b
                        take(g, bank(g), y[:, m, b * TB:(b + 1) * TB], P, TB)

                def gates(i, first, groups=range(2 * NB)):
                    for n in groups:
                        g = GROUP0[f"pg{layer}"] + n
                        if not (first and n < 2):
                            act.wait_ge(g_mul, i * 6 + (24 * layer + n - 1))
                        take(i * 6 + g, bank(g), gt[:, n % 2, :], P, TB, ACT.Sigmoid)

                gates(0, True)
                with act.Fori(1, 2) as i:
                    gates(i, False)
                chain = CHAIN if layer == 0 else [("post", b) for b in range(NB)]
                norms_among([(f"s{s0 + 2}", k, b) for k, b in chain],
                            lambda b: gates(0, False, range(12 if b == 0 else 15 + 3 * b, 18 + 3 * b)),
                            chain_waits([[(g_mul, 24 * layer + 18 + 3 * b)] for b in range(NB)]))

            tail_act(0)
            fence(act, "act", 4)
            for m in range(2):
                act.wait_ge(st_out[m], 16 * (4 + KT + 8))
                for b in range(NB):
                    g = GROUP0["kb"] + m * NB + b
                    take(g, bank(g), stg[:, m, b * TB:(b + 1) * TB], P, TB)
            for b in range(NB):
                g = GROUP0["wf"] + b
                take(g, bank(g), fz[:, b * TB:(b + 1) * TB], H, TB, ACT.Identity,
                     bias=gains[0:H, GAIN_AT["bf"]:GAIN_AT["bf"] + 1])
            act.wait_ge(lin_ev, GROUP0["wf"] + NB)
            nc.scalar.activation(fe[:], fz[:], ACT.Abs).then_inc(fx_a, 1)
            act.wait_ge(fx_a, 1)
            nc.scalar.activation(fe[:], fe[:], ACT.Exp, scale=-1.0).then_inc(fx_a, 1)
            act.wait_ge(fx_v, 1)
            nc.scalar.activation(fl[:], fu[:], ACT.Ln).then_inc(fx_a, 1)
            for tt in range(9):
                rows = min(P, T - tt * P)
                act.wait_ge(st_out[tt % 2], 16 * (4 + KT + 8 + 1 + tt // 2))
                g = GROUP0["vb"] + tt
                take(g, bank(g), stg[0:rows, tt % 2, 0:KVH * HD], rows, KVH * HD)
            with act.Fori(0, 4) as i:
                for m in range(2):
                    act.wait_ge(st_out[m], i * 16 + 16 * (4 + KT + 8 + 1 + 5 - m))
                    for b in range(NB):
                        g = GROUP0["qb"] + m * NB + b
                        take(i * 6 + g, bank(g), stg[:, m, b * TB:(b + 1) * TB], P, TB, scale=FOX_SCALE)
            fence(act, "act", 5)
            first_head_hi(1)
            attn_act(1)
            fence(act, "act", 6)
            tail_act(1)

        @block.vector
        def _(dve):
            V = nc.vector

            def apply(key):
                k = NORM_AT[key]
                s, kind, b = key
                c = slice(b * TB, (b + 1) * TB)
                src = {"pre": res[:, :, c], "post": y[:, :, c], "q": y[:, 0:4, c], "kv": y[:, 4:6, c]}[kind]
                raw = y[:, :, c] if kind == "pre" else src
                K = {"q": 4, "kv": 2}.get(kind, KD)
                dve.wait_ge(n_rt, k + 1)
                V.reciprocal(rs[:, k % 2, :], rt[:, k % 2, :]).then_inc(n_rs, 1)
                dve.wait_ge(n_rs, k + 1)
                if kind == "kv":
                    V.tensor_tensor(raw, src, rs[:, k % 2, :].unsqueeze(1).to_broadcast((P, K, TB)),
                                    ALU.mult).then_inc(kv_raw, 1)
                    dve.wait_ge(kv_raw, b + 1)
                    for j in range(K):
                        at_g = GAIN_AT["kv"] + j
                        V.tensor_scalar(y[:, 6 + j, c], y[:, 4 + j, c], gains[:, at_g:at_g + 1], None,
                                        ALU.mult).then_inc(n_ap, 1)
                    return
                by = rs[:, k % 2, :].unsqueeze(1).to_broadcast((P, K // 2, TB))
                for j0, j1 in halves(K):
                    V.tensor_tensor(raw[:, j0:j1, :], src[:, j0:j1, :], by, ALU.mult).then_inc(n_ap, 1)
                if kind == "post":
                    for h, (j0, j1) in enumerate(halves(K)):
                        dve.wait_ge(n_ap, 2 * k + 1 + h)
                        for j in range(j0, j1):
                            at_g = GAIN_AT[POST_GAIN[s]] + j
                            last = V.scalar_tensor_tensor(res[:, j, c], y[:, j, c], gains[:, at_g:at_g + 1],
                                                          res[:, j, c], ALU.mult, ALU.add)
                        last.then_inc(r_done, 1)

            def low(key):
                k = NORM_AT[key]
                _, kind, b = key
                c = slice(b * TB, (b + 1) * TB)
                if kind == "post" or POOL_LOW[k]:
                    return
                hi, lo, raw, K = {"kv": (cvh, cvl, y[:, 6:8], 2), "q": (nh, nl, y, 4), "pre": (nh, nl, y, KD)}[kind]
                for h, (j0, j1) in enumerate(halves(K)):
                    dve.wait_ge(n_hi, 2 * HI_COUNT[k] - 1 + h)
                    last = V.tensor_tensor(lo[:, j0:j1, c], raw[:, j0:j1, c], hi[:, j0:j1, c].bitcast(F32), ALU.subtract)
                last.then_inc(n_done, 1)

            def norms(keys):
                for before, key in zip([None] + keys, keys + [None]):
                    if key:
                        apply(key)
                    if before:
                        low(before)

            V.memset(epsc[:], EPS)
            V.memset(ones[:], 1.0).then_inc(ones_set, 1)
            norms([("s0", "pre", b) for b in range(NB)])
            dve.wait_ge(const_in, 48)
            V.tensor_copy(ident_r[:], ident[:])
            V.tensor_copy(mask_r[:], wraw[:, 2, 0:2 * P].rearrange("p (a q) -> p a q", a=2)).then_inc(const_r, 1)
            dve.wait_ge(tab_in, 16)
            for b in range(NB):
                c = slice(b * TB, (b + 1) * TB)
                dve.wait_ge(lin_ev, GROUP0["kr"] + b + 1)
                V.tensor_tensor(y[0:ROPE, 6, c], y[0:ROPE, 6, c], krt[0:ROPE, c], ALU.mult)
                V.tensor_tensor(krf[:, c], y[ROPE:2 * ROPE, 6, c], krt[ROPE:2 * ROPE, c], ALU.mult).then_inc(kr_a, 1)
                dve.wait_ge(kr_a, b + 1)
                V.tensor_tensor(krf[:, c], krf[:, c], y[0:ROPE, 6, c], ALU.add).then_inc(kr_done, 1)
            dve.wait_ge(kr_done, NB)
            norms([("s1", kind, b) for kind in ("q", "kv") for b in range(NB)])
            dve.wait_ge(cc_hi, 1)
            V.tensor_tensor(cvl[:, :, T:TK], cc[:], cvh[:, :, T:TK].bitcast(F32), ALU.subtract).then_inc(cc_lo, 1)
            fence(dve, "dve", 1)
            dve.wait_ge(tab_in, 32)
            with dve.Fori(0, 4) as i:
                for h in range(4):
                    for b in range(NB):
                        c = slice(b * TB, (b + 1) * TB)
                        dve.wait_ge(lin_ev, i * 12 + (GROUP0["uq"] + h * NB + b + 1))
                        V.tensor_tensor(stg[:, h % 2, c], stg[:, h % 2, c], cs[:, c], ALU.mult).then_inc(q_done, 1)
            fence(dve, "dve", 2)

            def attention(layer):
                base_n, base_c = layer * H * STEPS, layer * H * HC

                def neg_max(i, s):
                    k, tile = s % STEPS, ORDER[s % STEPS]
                    M = P if tile < 8 else DEC
                    dve.wait_ge(at_s, i * PAIR + (base_n + s + 1))
                    V.tensor_reduce(nmx[0:M, k:k + 1], score_tile(tile), AX.X, ALU.max, negate=True).then_inc(at_nm, 1)

                def normalise(i, s):
                    k, tile = s % STEPS, ORDER[s % STEPS]
                    M = P if tile < 8 else DEC
                    p = pr[0:M, PROB_AT[tile]:PROB_AT[tile] + KEYS[tile]]
                    dve.wait_ge(at_e, i * PAIR + (base_n + s + 1))
                    V.reciprocal(rinv[0:M, k:k + 1], rsum[0:M, k:k + 1]).then_inc(at_r, 1)
                    dve.wait_ge(at_r, i * PAIR + (base_n + s + 1))
                    V.tensor_scalar(p, p, rinv[0:M, k:k + 1], None, ALU.mult).then_inc(at_p, 1)

                def lo(i, c):
                    dve.wait_ge(at_hi, i * (2 * HC) + (base_c + c + 1))
                    for (dst, src), (hi, _) in zip(turned(c, ptl), turned(c, pth)):
                        last = V.tensor_tensor(dst, src, hi.bitcast(F32), ALU.subtract)
                    last.then_inc(at_lo, 1)

                def outs(i, c):
                    if is_out(c):
                        dst, src, n = out_part(c, i, nl)
                        dve.wait_ge(at_ohi, i * 6 + (3 * layer * H + n))
                        V.tensor_tensor(dst, src, out_part(c, i, nh)[0].bitcast(F32), ALU.subtract).then_inc(at_olo, 1)

                def pair(i, first, drain=False):
                    for s in range(T_LAG if drain else PAIR):
                        if not drain:
                            neg_max(i, s)
                        todo = [s - 1] if (s >= 1 or not first) and not (drain and s > 0) else []
                        while todo:
                            normalise(i, todo.pop())
                        for c in chunks_of(s - T_LAG):
                            if c >= 0 or not first:
                                lo(i, c)
                            if c >= OUT_LAG or not first:
                                outs(i, c - OUT_LAG)
                    if drain:
                        for c in range(-OUT_LAG, 0):
                            outs(i, c)

                pair(0, True)
                with dve.Fori(1, H // 2) as i:
                    pair(i, False)
                pair(H // 2, False, True)

            def ffn(layer):
                f0 = layer * NF
                events = sorted([(p, "down", d) for d, p in enumerate(D_AT)]
                                + [(72 + 24 * (b + 1), "mul", b) for b in range(NB)]
                                + [(108 + 21 * b, "lo", b) for b in range(NB)])

                def down(f, d, first, blocks_first=False):
                    m, b = (d % KD, d // KD) if blocks_first else (d // NB, d % NB)
                    c = slice(b * TB, (b + 1) * TB)
                    dve.wait_ge(fd_rd, f * 24 + (24 * f0 + d + 1))
                    if first:
                        V.tensor_copy(y[:, m, c], ps[:, 6 + d % 2, 0:TB]).then_inc(f_acc, 1)
                    else:
                        V.tensor_tensor(y[:, m, c], ps[:, 6 + d % 2, 0:TB], y[:, m, c], ALU.add).then_inc(f_acc, 1)

                def tile(f, par, first, second=False):
                    for _, what, x in events:
                        c = slice(x * TB, (x + 1) * TB)
                        if what == "down":
                            if not first:
                                down(f - 1, x, second)
                        elif what == "mul":
                            dve.wait_ge(f_sg, f * 3 + (3 * f0 + x + 1))
                            dve.wait_ge(fu_rd, f * 3 + (3 * f0 + x + 1))
                            V.tensor_tensor(sg[:, x, :], ps[:, 3 + x, 0:TB], sg[:, x, :], ALU.mult).then_inc(f_u, 1)
                        else:
                            dve.wait_ge(f_hi, f * 3 + (3 * f0 + x + 1))
                            V.tensor_tensor(hl[par][:, c], sg[:, x, :], hh[par][:, c].bitcast(F32),
                                            ALU.subtract).then_inc(f_lo, 1)

                tile(0, 0, True)
                tile(1, 1, False, True)
                with dve.Fori(1, NF // 2) as i:
                    for par in range(2):
                        tile(i * 2 + par, par, False)
                for d in range(24):
                    down(NF - 1, d, False, True)

            def tail(layer):
                s0 = 2 + 3 * layer
                norms([(f"s{s0}", k, b) for k, b in CHAIN])
                ffn(layer)
                norms([(f"s{s0 + 1}", k, b) for k, b in CHAIN])
                dve.wait_ge(*rows_ready((f"s{s0 + 1}", "pre", 2)))
                dve.wait_ge(p_hi, layer + 1)
                V.tensor_tensor(pl[:], praw[:], ph[:].bitcast(F32), ALU.subtract).then_inc(p_lo, 1)
                def gated(i, n):
                    m, b = group_place(n)
                    c = slice(b * TB, (b + 1) * TB)
                    dve.wait_ge(lin_ev, i * 6 + (GROUP0[f"pg{layer}"] + n + 1))
                    V.tensor_tensor(y[:, i * 2 + m, c], gt[:, n % 2, :], y[:, i * 2 + m, c], ALU.mult).then_inc(g_mul, 1)

                with dve.Fori(0, 2) as i:
                    for n in range(2 * NB):
                        gated(i, n)
                for n in range(4 * NB, 24):
                    gated(0, n)
                    if n == 6 * NB + 2:
                        norms([(f"s{s0 + 2}", "post", 0)])

            def first_head_lo(layer):
                dve.wait_ge(first_hi, layer + 1)
                for hi, lo, raw, _, _ in sum(head_parts(layer, 0), []):
                    last = V.tensor_tensor(lo, raw, hi.bitcast(F32), ALU.subtract)
                last.then_inc(first_split, 1)

            dve.wait_ge(fix_hi, 1)
            for b in range(2):
                last = V.tensor_tensor(kl[NOPE:P, b, :], kraw[NOPE:P, :], kh[NOPE:P, b, :].bitcast(F32), ALU.subtract)
            last.then_inc(fix_lo, 1)
            first_head_lo(0)
            attention(0)
            fence(dve, "dve", 3)
            tail(0)
            norms([("s4", k, b) for k, b in CHAIN[1:]])
            fence(dve, "dve", 4)
            link = [0]

            def chained(ins):
                link[0] += 1
                ins.then_inc(fx_v, 1)
                dve.wait_ge(fx_v, link[0])

            dve.wait_ge(fx_a, 2)
            chained(V.tensor_scalar(fu[:], fe[:], 1.0, None, ALU.add))
            dve.wait_ge(fx_a, 3)
            chained(V.scalar_tensor_tensor(fe[:], fu[:], -1.0, fe[:], ALU.add, ALU.subtract))
            chained(V.reciprocal(fu[:], fu[:]))
            chained(V.tensor_tensor(fe[:], fe[:], fu[:], ALU.mult))
            chained(V.tensor_tensor(fl[:], fl[:], fe[:], ALU.subtract))
            chained(V.scalar_tensor_tensor(flog[:, 0:T], fz[:], 0.0, fl[:], ALU.min, ALU.subtract))
            dve.wait_ge(cache_in, 32)

            def scan(cols, initial):
                n = cols.stop - cols.start
                chained(V.tensor_tensor_scan(fcum[:, cols], ones[0:H, 0:1].to_broadcast((H, n)), flog[:, cols],
                                             initial, ALU.mult, ALU.add))

            scan(slice(T, TK), 0.0)
            scan(slice(0, SEQ), 0.0)
            scan(slice(SEQ, T), fcum[:, TK - 1:TK])
            chained(V.tensor_scalar(fcum[:], fcum[:], -1.0, None, ALU.mult))
            fence(dve, "dve", 5)
            for b in range(2):
                V.memset(qh[HD:HD + 1, b, :].bitcast(F32), 1.0)
                last = V.memset(ql[HD:HD + 1, b, :].bitcast(F32), 0.0)
            last.then_inc(fix_lo, 1)
            first_head_lo(1)
            attention(1)
            fence(dve, "dve", 6)
            tail(1)
            norms([("s7", "post", b) for b in range(1, NB)])


def _weight_units(np, w):
    def cols(m, width=P):
        r, c = m.shape
        return m.reshape(r // P, P, c // width, width).transpose(2, 1, 0, 3).reshape(c // width, P, -1)

    def packed(tiles, n):
        t, p, c = tiles.shape
        return tiles.reshape(t // n, n, p, c).transpose(0, 2, 1, 3).reshape(t // n, p, n * c)

    def padded(m):
        out = np.zeros((m.shape[0], P), m.dtype)
        out[:, :m.shape[1]] = m
        return cols(out)

    def swapped(m):
        return np.concatenate([m[..., ROPE // 2:], m[..., :ROPE // 2]], -1)

    uq = w["w_uq"][0].reshape(Q_RANK, H, NOPE + ROPE)
    uq = np.concatenate([uq, swapped(uq[..., NOPE:])], -1).reshape(Q_RANK, H * P)
    kr = w["w_dkv"][0][:, KV_RANK:]

    def ffn(i):
        g, u = cols(w["w_gate"][i]), cols(w["w_up"][i])
        d = w["w_down"][i].reshape(NF, P, D)
        order = [g[0], u[0]]
        for f in range(NF - 1):
            order += [g[f + 1], d[f], u[f + 1]]
        return np.stack(order + [d[NF - 1]])

    def moving(m, per):
        r, c = m.shape
        return m.reshape(r // P // per, per, P, c).transpose(0, 2, 1, 3).reshape(-1, P, per * c)

    uv = w["w_uv"][0].reshape(KV_RANK, 2, H * VD // 2)
    parts = {
        "dq": cols(w["w_dq"][0]), "dkv": cols(w["w_dkv"][0][:, :KV_RANK]),
        "kr": padded(np.concatenate([kr, swapped(kr)], -1)),
        "uk": packed(cols(w["w_uk"][0].reshape(KV_RANK, H * NOPE)), 4),
        "uv": np.concatenate([moving(uv[:, h], 2) for h in range(2)]),
        "uq": packed(cols(uq), 2), "oa": cols(w["w_oa"][0]), "ffn0": ffn(0),
        "pe0": packed(cols(w["w_ple"][0]), 4), "pg0": cols(w["w_ple_gate"][0]),
        "kb": cols(w["w_kb"]), "wf": padded(w["w_f"]), "vb": moving(w["w_vb"], 4),
        "qb": cols(w["w_qb"][0]), "ob": cols(w["w_ob"][0]), "ffn1": ffn(1),
        "pe1": packed(cols(w["w_ple"][1]), 4), "pg1": cols(w["w_ple_gate"][1]),
    }
    for name, n, _ in LIN:
        assert parts[name].shape == (n, P, UW), (name, parts[name].shape)
    return np.concatenate([parts[name] for name, _, _ in LIN])


def _gain_table(np, w):
    def tiles(v):
        return v.reshape(-1, P).T

    def eight(v, places):
        out = np.zeros((P, 8), v.dtype)
        t = tiles(v)
        for j, k in enumerate(places):
            out[:, j] = t[:, k]
        return out

    every = range(8)
    bf = np.zeros((P, 8), w["b_f"].dtype)
    bf[:H, 0] = w["b_f"]
    cols = {"mix_pre0": eight(w["g_mix_pre"][0], every), "q": eight(w["g_q"][0], [0, 1, 2, 3] * 2),
            "mix_post0": eight(w["g_mix_post"][0], every), "ffn_pre0": eight(w["g_ffn_pre"][0], every),
            "ffn_post0": eight(w["g_ffn_post"][0], every), "ple_gate0": eight(w["g_ple_gate"][0], every),
            "ple_post0": eight(w["g_ple_post"][0], every), "shared": eight(w["g_shared"], every),
            "shared_v": eight(w["g_shared"], [0, 0, 1, 1, 2, 2, 3, 3]),
            "shared_v2": eight(w["g_shared"], [4, 4, 5, 5, 6, 6, 7, 7]),
            "mix_pre1": eight(w["g_mix_pre"][1], every), "mix_post1": eight(w["g_mix_post"][1], every),
            "ffn_pre1": eight(w["g_ffn_pre"][1], every), "ffn_post1": eight(w["g_ffn_post"][1], every),
            "ple_gate1": eight(w["g_ple_gate"][1], every), "ple_post1": eight(w["g_ple_post"][1], every),
            "kv": eight(w["g_kv"][0], range(2)), "bf": bf}
    return np.concatenate([cols[n] for n in GAINS], 1)


def _position_tables(np):
    half = ROPE // 2
    inv = np.power(np.float32(10000.0), -np.arange(half, dtype=np.float32) / half).astype(np.float32)
    pos = np.concatenate([np.arange(SEQ), PAST + np.arange(DEC)]).astype(np.float32)
    ang = (inv[:, None] * pos[None, :]).astype(np.float32)
    cos, sin = np.cos(ang).astype(np.float32), np.sin(ang).astype(np.float32)
    krt = np.concatenate([cos, cos, -sin, sin])
    scale = np.float32((NOPE + ROPE) ** -0.5)
    cs = np.concatenate([np.ones((NOPE, T), np.float32), krt]) * scale
    q, k = np.arange(P)[:, None], np.arange(P)[None, :]
    masks = np.zeros((P, 2, P), np.float32)
    masks[:, 0][k // 64 > q // 64] = NEG
    masks[:, 1][k > q] = NEG
    return krt, cs.astype(np.float32), masks.reshape(P, 2 * P), np.eye(P, dtype=np.float32)


def kernel(**w):
    import numpy as np
    import concourse.bacc as bacc
    from concourse.bass_utils import run_bass_kernel_spmd as run

    w = {k: np.asarray(v) for k, v in w.items()}
    krt, cs, masks, ident = _position_tables(np)
    c = np.ascontiguousarray
    x = np.concatenate([w["x_prompt"][0], w["x_sample"][0]])
    p = np.concatenate([w["p_prompt"][:, 0], w["p_sample"][:, 0]], 1)
    arrays = {
        "units": _weight_units(np, w), "gains": c(_gain_table(np, w)), "krt": krt, "cs": cs, "masks": masks,
        "ident": ident,
        "xT": c(x.reshape(T, KD, P).transpose(2, 1, 0)),
        "pT": c(p.reshape(2, T, 2, P).transpose(0, 3, 2, 1)),
        "cckvT": c(w["cache_ckv"][0, 0].reshape(PAST, 2, P).transpose(2, 1, 0)),
        "ckrT": c(w["cache_kr"][0, 0].T),
        "ckT": c(w["cache_k"][0].transpose(1, 2, 0)),
        "cv": c(w["cache_v"][0].reshape(PAST, KVH * HD)),
        "clfT": c(w["cache_logf"][0].T),
    }
    nc = bacc.Bacc("TRN2", target_bir_lowering=False, num_devices=1)
    io = {n: nc.dram_tensor(n, a.shape, F32, kind="ExternalInput").ap() for n, a in arrays.items()}

    def dram(name, shape, kind="Internal"):
        io[name] = nc.dram_tensor(name, shape, F32, kind=kind).ap()

    dram("yT", (P, KD, T), "ExternalOutput")
    dram("ckv_out", (P, 2, T), "ExternalOutput")
    dram("kr_out", (ROPE, T), "ExternalOutput")
    dram("kT_out", (KVH * HD, T), "ExternalOutput")
    dram("v_out", (T, KVH * HD), "ExternalOutput")
    dram("lf_out", (H, T), "ExternalOutput")
    dram("kA", (H * NOPE, TK))
    dram("vA", (TK, H * VD))
    dram("qA", (H, P, T))
    dram("qBm", (D, T))
    dram("nck_all", (H, TK))
    full = (KT - 1) * P
    io["kA_h"] = io["kA"].rearrange("(h d) t -> h d t", d=NOPE)
    io["vA_full"] = io["vA"][0:full, :].rearrange("(t p) (h d) -> h p t d", p=P, d=VD)
    io["vA_last"] = io["vA"][full:TK, :].rearrange("p (h d) -> h p d", d=VD)
    io["qB"] = io["qBm"].rearrange("(h d) t -> h d t", d=HD)
    io["qB_pair"] = io["qBm"].rearrange("(m p) t -> m p t", p=P)
    io["nck"] = io["nck_all"].rearrange("(h o) t -> h o t", o=1)
    io["kT_h"] = io["kT_out"].rearrange("(h d) t -> h d t", d=HD)
    io["v_full"] = io["v_out"][0:SEQ, :].rearrange("(t p) (h d) -> h p t d", p=P, d=HD)
    io["v_new"] = io["v_out"][SEQ:T, :].rearrange("p (h d) -> h p d", d=HD)
    cv = io["cv"].rearrange("p (h d) -> h p d", d=HD)
    n0 = P - DEC
    io["cv0"], io["cv1"], io["cv2"] = cv[:, 0:n0, :], cv[:, n0:n0 + P, :], cv[:, n0 + P:PAST, :]
    build_program(nc, io)
    r = run(nc, [arrays], core_ids=[0]).results[0]

    def rows(a):
        a = c(a.T)
        return a[None, :SEQ], a[None, SEQ:]

    y_p, y_s = rows(r["yT"].transpose(1, 0, 2).reshape(D, T))
    ckv_p, ckv_s = rows(r["ckv_out"].transpose(1, 0, 2).reshape(KV_RANK, T))
    kr_p, kr_s = rows(r["kr_out"])
    k_p, k_s = rows(r["kT_out"])
    lf_p, lf_s = rows(r["lf_out"])
    v = r["v_out"].reshape(T, KVH, HD)
    return (y_p, y_s, ckv_p[None], kr_p[None], k_p.reshape(1, SEQ, KVH, HD), v[None, :SEQ], lf_p,
            ckv_s[None], kr_s[None], k_s.reshape(1, DEC, KVH, HD), v[None, SEQ:], lf_s)
```
